# Optimizing a Trainium2 kernel written in Bass

```python
import math
import numpy as np
import jax
import jax.numpy as jnp
from jax import lax
import jax, jax.numpy as jnp

D_MODEL = 1024
BATCH = 1
SEQ = 256
DEPTH = 2

GRID_W = 64
CTX_LEN = 256
HEAD_DIM = 64
D_CONV = 512
CONV_K = 31
NA_HEADS = 8
NA_MAX_ROWS = 8
NA_COLS = 16
WA_HEADS = 8
WA_KV_HEADS = 2
WA_WINDOW = 128
WA_BLOCK = 128
ROPE_BASE = 10000.0
EPS = 1e-6
D_NA = NA_HEADS * HEAD_DIM
D_WA = WA_HEADS * HEAD_DIM
D_WA_KV = WA_KV_HEADS * HEAD_DIM
SPLIT_SIZES = (2 * D_CONV, D_CONV, D_NA, D_NA, D_NA, D_NA, D_WA, D_WA_KV, D_WA_KV, D_WA, 3 * D_MODEL)
D_IN = sum(SPLIT_SIZES)
SPLIT_POINTS = tuple(int(v) for v in np.cumsum(SPLIT_SIZES)[:-1])
SPLIT_STARTS = (0,) + SPLIT_POINTS


def rms_norm(x, g):
    xf = x.astype(jnp.float32)
    y = xf * lax.rsqrt(jnp.mean(xf * xf, axis=-1, keepdims=True) + EPS)
    return (y * g.astype(jnp.float32)).astype(x.dtype)

def layer_norm(x, g, b):
    xf = x.astype(jnp.float32)
    mu = jnp.mean(xf, axis=-1, keepdims=True)
    var = jnp.mean(jnp.square(xf - mu), axis=-1, keepdims=True)
    y = (xf - mu) * lax.rsqrt(var + EPS)
    return (y * g.astype(jnp.float32) + b.astype(jnp.float32)).astype(x.dtype)

def depthwise_conv(x, w, b):
    y = lax.conv_general_dilated(
        x, w[:, None, :].astype(x.dtype), window_strides=(1,),
        padding=[(CONV_K // 2, CONV_K // 2)],
        dimension_numbers=('NWC', 'WIO', 'NWC'),
        feature_group_count=x.shape[-1])
    return y + b

def conv_branch(u_glu, u_gate, conv_w, conv_b, ln_g, ln_b, w_proj):
    a = u_glu[..., :D_CONV] * jax.nn.sigmoid(u_glu[..., D_CONV:])
    a = depthwise_conv(a, conv_w, conv_b)
    a = jax.nn.silu(layer_norm(a, ln_g, ln_b))
    return (a * jax.nn.silu(u_gate)) @ w_proj

def split_heads(t, n):
    return t.reshape(t.shape[0], t.shape[1], n, HEAD_DIM)

def rotate(x, pos):
    half = x.shape[-1] // 2
    inv = ROPE_BASE ** (-jnp.arange(half, dtype=jnp.float32) / half)
    ang = pos.astype(jnp.float32)[:, None] * inv[None, :]
    cos = jnp.cos(ang)[None, :, None, :]
    sin = jnp.sin(ang)[None, :, None, :]
    x1 = x[..., :half].astype(jnp.float32)
    x2 = x[..., half:].astype(jnp.float32)
    return jnp.concatenate([x1 * cos - x2 * sin, x1 * sin + x2 * cos], axis=-1).astype(x.dtype)

def axial_rope(t, row_pos, col_pos):
    half = HEAD_DIM // 2
    return jnp.concatenate([rotate(t[..., :half], row_pos), rotate(t[..., half:], col_pos)], axis=-1)

def sink_softmax(s, sink):
    m = jnp.maximum(jnp.max(s, axis=-1, keepdims=True), sink)
    e = jnp.exp(s - m)
    return e / (jnp.sum(e, axis=-1, keepdims=True) + jnp.exp(sink - m))

def context_attention(q, k, v, sink):
    s = jnp.einsum('bqkgd,bnkd->bkgqn', q, k).astype(jnp.float32) * HEAD_DIM ** -0.5
    if sink is None:
        p = jax.nn.softmax(s, axis=-1)
    else:
        p = sink_softmax(s, sink.astype(jnp.float32)[None, :, :, None, None])
    o = jnp.einsum('bkgqn,bnkd->bqkgd', p.astype(v.dtype), v)
    return o.reshape(o.shape[0], o.shape[1], -1)

def neighbourhood_attention(q, k, v, k_ctx, v_ctx, rpb):
    B, S = q.shape[0], q.shape[1]
    rows = S // GRID_W
    kr = min(NA_MAX_ROWS, rows)
    scale = HEAD_DIM ** -0.5
    grid = (B, rows, GRID_W, NA_HEADS, HEAD_DIM)
    qg, kg, vg = q.reshape(grid), k.reshape(grid), v.reshape(grid)
    col_start = np.clip(np.arange(GRID_W) - NA_COLS // 2, 0, GRID_W - NA_COLS)
    col_idx = col_start[:, None] + np.arange(NA_COLS)[None, :]
    col_off = col_idx - np.arange(GRID_W)[:, None] + (NA_COLS - 1)
    rpb_cols = rpb[:, :, col_off]

    def row_fn(i):
        rs = jnp.clip(i - kr // 2, 0, rows - kr)
        q_i = lax.dynamic_index_in_dim(qg, i, axis=1, keepdims=False)
        k_w = lax.dynamic_slice_in_dim(kg, rs, kr, axis=1)[:, :, col_idx]
        v_w = lax.dynamic_slice_in_dim(vg, rs, kr, axis=1)[:, :, col_idx]
        row_off = rs + jnp.arange(kr) - i + (NA_MAX_ROWS - 1)
        bias = jnp.transpose(rpb_cols[:, row_off], (0, 2, 1, 3)).astype(jnp.float32)
        s_w = jnp.einsum('bjhd,brjchd->bhjrc', q_i, k_w).astype(jnp.float32) * scale + bias[None]
        s_c = jnp.einsum('bjhd,bnhd->bhjn', q_i, k_ctx).astype(jnp.float32) * scale
        s = jnp.concatenate([s_w.reshape(B, NA_HEADS, GRID_W, kr * NA_COLS), s_c], axis=-1)
        p = jax.nn.softmax(s, axis=-1).astype(v.dtype)
        p_w = p[..., :kr * NA_COLS].reshape(B, NA_HEADS, GRID_W, kr, NA_COLS)
        o = (jnp.einsum('bhjrc,brjchd->bjhd', p_w, v_w)
             + jnp.einsum('bhjn,bnhd->bjhd', p[..., kr * NA_COLS:], v_ctx))
        return o

    out = lax.map(row_fn, jnp.arange(rows))
    return jnp.moveaxis(out, 0, 1).reshape(B, S, NA_HEADS * HEAD_DIM)

def window_attention(q, k, v, k_ctx, v_ctx, sink):
    B, S = q.shape[0], q.shape[1]
    G = WA_HEADS // WA_KV_HEADS
    nb = S // WA_BLOCK
    span = WA_BLOCK + 2 * WA_WINDOW
    scale = HEAD_DIM ** -0.5
    qb = q.reshape(B, nb, WA_BLOCK, WA_KV_HEADS, G, HEAD_DIM)
    pad = ((0, 0), (WA_WINDOW, WA_WINDOW), (0, 0), (0, 0))
    kp = jnp.pad(k, pad)
    vp = jnp.pad(v, pad)
    rel = (jnp.arange(span) - WA_WINDOW)[None, :] - jnp.arange(WA_BLOCK)[:, None]
    in_window = jnp.abs(rel) <= WA_WINDOW
    sink_b = sink.astype(jnp.float32).reshape(1, WA_KV_HEADS, G, 1, 1)

    def block_fn(n):
        start = n * WA_BLOCK
        q_n = lax.dynamic_index_in_dim(qb, n, axis=1, keepdims=False)
        k_n = lax.dynamic_slice_in_dim(kp, start, span, axis=1)
        v_n = lax.dynamic_slice_in_dim(vp, start, span, axis=1)
        kpos = start - WA_WINDOW + jnp.arange(span)
        valid = in_window & ((kpos >= 0) & (kpos < S))[None, :]
        s_w = jnp.einsum('bqkgd,bskd->bkgqs', q_n, k_n).astype(jnp.float32) * scale
        s_w = jnp.where(valid, s_w, -jnp.inf)
        s_c = jnp.einsum('bqkgd,bnkd->bkgqn', q_n, k_ctx).astype(jnp.float32) * scale
        p = sink_softmax(jnp.concatenate([s_w, s_c], axis=-1), sink_b).astype(v.dtype)
        o = (jnp.einsum('bkgqs,bskd->bqkgd', p[..., :span], v_n)
             + jnp.einsum('bkgqn,bnkd->bqkgd', p[..., span:], v_ctx))
        return o

    out = lax.map(block_fn, jnp.arange(nb))
    return jnp.moveaxis(out, 0, 1).reshape(B, S, WA_HEADS * HEAD_DIM)

def merge_branches(a_glu, a_gate, o_na, n_gate, o_wa, w_gate, merge,
                   conv_w, conv_b, cln_g, cln_b, w_proj_a, w_proj_b, w_proj_c, w_o):
    y_a = conv_branch(a_glu, a_gate, conv_w, conv_b, cln_g, cln_b, w_proj_a)
    y_b = (o_na * jax.nn.silu(n_gate)) @ w_proj_b
    y_c = (o_wa * jax.nn.silu(w_gate)) @ w_proj_c
    g_a, g_b, g_c = jnp.split(merge, 3, axis=-1)
    y = jax.nn.sigmoid(g_a) * y_a + jax.nn.sigmoid(g_b) * y_b + jax.nn.sigmoid(g_c) * y_c
    return y @ w_o

def context_kv(hc, w_in_l):
    st = SPLIT_STARTS
    nk, nv = jnp.split(hc @ w_in_l[:, st[3]:st[5]], 2, axis=-1)
    wk, wv = jnp.split(hc @ w_in_l[:, st[7]:st[9]], 2, axis=-1)
    return nk, nv, wk, wv

def first_inputs(seed: int = 0) -> dict:
    key = jax.random.key(seed)
    ks = jax.random.split(key, 24)
    L = DEPTH

    def nrm(k, shape, s):
        return jax.random.normal(k, shape, jnp.float32) * s

    return {
        'x': nrm(ks[0], (BATCH, SEQ, D_MODEL), 1.0),
        'c': nrm(ks[1], (BATCH, D_MODEL), 1.0),
        'ctx': nrm(ks[2], (BATCH, CTX_LEN, D_MODEL), 1.0),
        'c_ctx': nrm(ks[3], (D_MODEL,), 1.0),
        'norm_g': 1.0 + nrm(ks[4], (L, D_MODEL), 0.02),
        'w_ada': nrm(ks[5], (L, D_MODEL, 3 * D_MODEL), 0.5 * D_MODEL ** -0.5),
        'b_ada': nrm(ks[6], (L, 3 * D_MODEL), 0.02),
        'w_in': nrm(ks[7], (L, D_MODEL, D_IN), D_MODEL ** -0.5),
        'conv_w': nrm(ks[8], (L, CONV_K, D_CONV), CONV_K ** -0.5),
        'conv_b': nrm(ks[9], (L, D_CONV), 0.02),
        'cln_g': 1.0 + nrm(ks[10], (L, D_CONV), 0.02),
        'cln_b': nrm(ks[11], (L, D_CONV), 0.02),
        'w_proj_a': nrm(ks[12], (L, D_CONV, D_MODEL), D_CONV ** -0.5),
        'na_q_norm': 1.0 + nrm(ks[13], (L, HEAD_DIM), 0.02),
        'na_k_norm': 1.0 + nrm(ks[14], (L, HEAD_DIM), 0.02),
        'na_rpb': nrm(ks[15], (L, NA_HEADS, 2 * NA_MAX_ROWS - 1, 2 * NA_COLS - 1), 0.1),
        'w_proj_b': nrm(ks[16], (L, D_NA, D_MODEL), D_NA ** -0.5),
        'wa_q_norm': 1.0 + nrm(ks[17], (L, HEAD_DIM), 0.02),
        'wa_k_norm': 1.0 + nrm(ks[18], (L, HEAD_DIM), 0.02),
        'wa_sink': nrm(ks[19], (L, WA_HEADS), 1.0),
        'w_proj_c': nrm(ks[20], (L, D_WA, D_MODEL), D_WA ** -0.5),
        'w_o': nrm(ks[21], (L, D_MODEL, D_MODEL), D_MODEL ** -0.5),
    }

def first_block(x, c, ctx, c_ctx, norm_g, w_ada, b_ada, w_in, conv_w, conv_b, cln_g, cln_b,
              w_proj_a, na_q_norm, na_k_norm, na_rpb, w_proj_b, wa_q_norm, wa_k_norm,
              wa_sink, w_proj_c, w_o):
    B, S, _ = x.shape
    N = ctx.shape[1]
    G = WA_HEADS // WA_KV_HEADS
    t = jnp.arange(S)
    row_pos = t // GRID_W
    col_pos = t % GRID_W
    for l in range(DEPTH):
        update_ctx = l < DEPTH - 1
        mod = jax.nn.silu(c) @ w_ada[l] + b_ada[l]
        mod_c = jax.nn.silu(c_ctx) @ w_ada[l] + b_ada[l]
        shift, scale, gate = jnp.split(mod[:, None, :], 3, axis=-1)
        shift_c, scale_c, gate_c = jnp.split(mod_c[None, None, :], 3, axis=-1)
        h = rms_norm(x, norm_g[l]) * (1.0 + scale) + shift
        hc = rms_norm(ctx, norm_g[l]) * (1.0 + scale_c) + shift_c

        (a_glu, a_gate, nq, nk, nv, n_gate, wq, wk, wv, w_gate, merge) = jnp.split(
            h @ w_in[l], SPLIT_POINTS, axis=-1)
        if update_ctx:
            cp = jnp.split(hc @ w_in[l], SPLIT_POINTS, axis=-1)
            nck, ncv, wck, wcv = cp[3], cp[4], cp[7], cp[8]
        else:
            nck, ncv, wck, wcv = context_kv(hc, w_in[l])

        nk_c = rms_norm(split_heads(nck, NA_HEADS), na_k_norm[l])
        nv_c = split_heads(ncv, NA_HEADS)
        wk_c = rms_norm(split_heads(wck, WA_KV_HEADS), wa_k_norm[l])
        wv_c = split_heads(wcv, WA_KV_HEADS)

        o_na = neighbourhood_attention(
            rms_norm(split_heads(nq, NA_HEADS), na_q_norm[l]),
            rms_norm(split_heads(nk, NA_HEADS), na_k_norm[l]),
            split_heads(nv, NA_HEADS), nk_c, nv_c, na_rpb[l])
        o_wa = window_attention(
            axial_rope(rms_norm(split_heads(wq, WA_HEADS), wa_q_norm[l]), row_pos, col_pos),
            axial_rope(rms_norm(split_heads(wk, WA_KV_HEADS), wa_k_norm[l]), row_pos, col_pos),
            split_heads(wv, WA_KV_HEADS), wk_c, wv_c, wa_sink[l])
        y = merge_branches(a_glu, a_gate, o_na, n_gate, o_wa, w_gate, merge,
                           conv_w[l], conv_b[l], cln_g[l], cln_b[l],
                           w_proj_a[l], w_proj_b[l], w_proj_c[l], w_o[l])
        x_new = x + gate * y

        if update_ctx:
            (ac_glu, ac_gate, ncq, _, _, nc_gate, wcq, _, _, wc_gate, merge_c) = cp
            q_na_c = rms_norm(split_heads(ncq, NA_HEADS), na_q_norm[l])[:, :, :, None, :]
            oc_na = context_attention(q_na_c, nk_c, nv_c, None)
            q_wa_c = rms_norm(split_heads(wcq, WA_HEADS), wa_q_norm[l]).reshape(
                B, N, WA_KV_HEADS, G, HEAD_DIM)
            oc_wa = context_attention(q_wa_c, wk_c, wv_c, wa_sink[l].reshape(WA_KV_HEADS, G))
            yc = merge_branches(ac_glu, ac_gate, oc_na, nc_gate, oc_wa, wc_gate, merge_c,
                                conv_w[l], conv_b[l], cln_g[l], cln_b[l],
                                w_proj_a[l], w_proj_b[l], w_proj_c[l], w_o[l])
            ctx = ctx + gate_c * yc
        x = x_new
    return x


NSA_HEADS = 8
NSA_GROUPS = 2
CMP_BLOCK = 32
CMP_STRIDE = 16
CMP_HIDDEN = 256
SEL_BLOCK = 64
SEL_TOPK = 8
NSA_WINDOW = 512
SWA_HEADS = 8
SWA_GROUPS = 2
SWA_WINDOW = 128
FOX_HEADS = 8
FOX_GATE_BIAS = 3.0
Q_BLOCK = 128
REL_BUCKETS = 32
REL_MAX_DIST = 128
D_FF = 2816
N_BRANCH = 3
LN_EPS = 1e-5
DN_ALPHA = (2 * DEPTH) ** 0.25
DN_BETA = (8 * DEPTH) ** -0.25

W_A = NSA_HEADS * HEAD_DIM
KV_A = NSA_GROUPS * HEAD_DIM
W_B = SWA_HEADS * HEAD_DIM
KV_B = SWA_GROUPS * HEAD_DIM
W_C = FOX_HEADS * HEAD_DIM
D_IN_2 = W_A + 6 * KV_A + 3 * NSA_HEADS + W_B + 2 * KV_B + 3 * W_C + FOX_HEADS


def _layer_norm(x, g, b):
    xf = x.astype(jnp.float32)
    mu = jnp.mean(xf, axis=-1, keepdims=True)
    var = jnp.mean(jnp.square(xf - mu), axis=-1, keepdims=True)
    return ((xf - mu) * lax.rsqrt(var + LN_EPS) * g + b).astype(x.dtype)

def _swiglu(x, w1, w2):
    gt, up = jnp.split(x @ w1, 2, axis=-1)
    return (jax.nn.silu(gt) * up) @ w2

def _t5_bucket(dist):
    n = jnp.maximum(dist, 0)
    exact = REL_BUCKETS // 2
    log_ratio = jnp.log(jnp.maximum(n, 1).astype(jnp.float32) / exact) / math.log(REL_MAX_DIST / exact)
    large = exact + (log_ratio * (REL_BUCKETS - exact)).astype(jnp.int32)
    return jnp.where(n < exact, n, jnp.minimum(large, REL_BUCKETS - 1))

def _masked_softmax(logits, mask):
    logits = jnp.where(mask, logits.astype(jnp.float32), -jnp.inf)
    m = jnp.max(logits, axis=-1, keepdims=True)
    m = jnp.where(jnp.isfinite(m), m, 0.0)
    p = jnp.exp(logits - m)
    return p / jnp.maximum(jnp.sum(p, axis=-1, keepdims=True), 1e-30)

def _split_cols(z):
    sizes = [W_A, 6 * KV_A, 3 * NSA_HEADS, W_B, KV_B, KV_B, W_C, W_C, W_C, FOX_HEADS]
    return jnp.split(z, np.cumsum(sizes)[:-1].tolist(), axis=-1)

def _compress(z, pe, w1, w2):
    B, S, G, dh = z.shape
    r = CMP_BLOCK // CMP_STRIDE
    n_chunk = S // CMP_STRIDE
    nc = n_chunk - r + 1
    zr = z.reshape(B, n_chunk, CMP_STRIDE, G, dh)
    blocks = jnp.concatenate([zr[:, j:j + nc] for j in range(r)], axis=2)
    blocks = blocks + pe[:, None, :]
    flat = blocks.transpose(0, 3, 1, 2, 4).reshape(B, G, nc, CMP_BLOCK * dh)
    return jax.nn.gelu(flat @ w1) @ w2

def _nsa(q_a, kv_a, g_a, pe_k, pe_v, ck_w1, ck_w2, cv_w1, cv_w2, rel_a):
    B, S, _ = q_a.shape
    G, HPG, dh = NSA_GROUPS, NSA_HEADS // NSA_GROUPS, HEAD_DIM
    nb = S // Q_BLOCK
    scale = HEAD_DIM ** -0.5
    q = q_a.reshape(B, S, G, HPG, dh).transpose(0, 2, 3, 1, 4)
    k_cmp, v_cmp, k_slc, v_slc, k_win, v_win = [z.reshape(B, S, G, dh) for z in jnp.split(kv_a, 6, axis=-1)]
    kc = _compress(k_cmp, pe_k, ck_w1, ck_w2)
    vc = _compress(v_cmp, pe_v, cv_w1, cv_w2)
    nc = kc.shape[2]
    ns = S // SEL_BLOCK
    n_sel = min(SEL_TOPK, ns)
    ks = k_slc.reshape(B, ns, SEL_BLOCK, G, dh).transpose(0, 3, 1, 2, 4)
    vs = v_slc.reshape(B, ns, SEL_BLOCK, G, dh).transpose(0, 3, 1, 2, 4)
    pad = ((0, 0), (0, 0), (NSA_WINDOW, 0), (0, 0))
    kw = jnp.pad(k_win.transpose(0, 2, 1, 3), pad)
    vw = jnp.pad(v_win.transpose(0, 2, 1, 3), pad)
    gates = jax.nn.sigmoid(g_a.astype(jnp.float32)).reshape(B, S, G, HPG, 3).transpose(0, 2, 3, 1, 4)
    rel_g = rel_a.reshape(G, HPG, REL_BUCKETS)
    c_start = jnp.arange(nc) * CMP_STRIDE
    c_end = c_start + (CMP_BLOCK - 1)
    s_start = jnp.arange(ns) * SEL_BLOCK
    overlap = ((c_start[:, None] < s_start[None] + SEL_BLOCK) & (c_end[:, None] >= s_start[None])).astype(jnp.float32)
    i_w = jnp.arange(Q_BLOCK)
    j_w = jnp.arange(Q_BLOCK + NSA_WINDOW)
    dist_w = NSA_WINDOW + i_w[:, None] - j_w[None]
    band_w = (dist_w >= 0) & (dist_w < NSA_WINDOW)
    bias_w = rel_g[:, :, _t5_bucket(dist_w)]
    blk = jnp.arange(ns)
    sel_off = jnp.arange(SEL_BLOCK)
    gather = jax.vmap(jax.vmap(lambda kb, ix: kb[ix]))
    lookup = jax.vmap(lambda tab, bk: jnp.moveaxis(tab[:, bk], 0, 1), in_axes=(0, 1), out_axes=1)

    def block(qb):
        q0 = qb * Q_BLOCK
        t = q0 + jnp.arange(Q_BLOCK)
        qq = lax.dynamic_slice_in_dim(q, q0, Q_BLOCK, axis=3)
        gg = lax.dynamic_slice_in_dim(gates, q0, Q_BLOCK, axis=3)
        s_c = jnp.einsum('bghqd,bgkd->bghqk', qq, kc, preferred_element_type=jnp.float32) * scale
        s_c = s_c + rel_g[:, :, _t5_bucket(t[:, None] - c_end[None])]
        p_c = _masked_softmax(s_c, c_end[None] <= t[:, None])
        o_c = jnp.einsum('bghqk,bgkd->bghqd', p_c.astype(vc.dtype), vc)
        imp = jnp.einsum('bghqk,kj->bgqj', p_c, overlap)
        cur = (t // SEL_BLOCK)[:, None]
        forced = (blk[None] == 0) | (blk[None] == cur) | (blk[None] == cur - 1)
        valid = blk[None] * SEL_BLOCK <= t[:, None]
        score = jnp.where(forced, jnp.inf, jnp.where(valid, imp, -jnp.inf))
        _, idx = lax.top_k(score, n_sel)
        k_sel = gather(ks, idx).reshape(B, G, Q_BLOCK, n_sel * SEL_BLOCK, dh)
        v_sel = gather(vs, idx).reshape(B, G, Q_BLOCK, n_sel * SEL_BLOCK, dh)
        pos = (idx[..., None] * SEL_BLOCK + sel_off).reshape(B, G, Q_BLOCK, n_sel * SEL_BLOCK)
        dist = t[:, None] - pos
        s_s = jnp.einsum('bghqd,bgqkd->bghqk', qq, k_sel, preferred_element_type=jnp.float32) * scale
        s_s = s_s + lookup(rel_g, _t5_bucket(dist))
        p_s = _masked_softmax(s_s, (dist >= 0)[:, :, None])
        o_s = jnp.einsum('bghqk,bgqkd->bghqd', p_s.astype(v_sel.dtype), v_sel)
        kwb = lax.dynamic_slice_in_dim(kw, q0, Q_BLOCK + NSA_WINDOW, axis=2)
        vwb = lax.dynamic_slice_in_dim(vw, q0, Q_BLOCK + NSA_WINDOW, axis=2)
        s_w = jnp.einsum('bghqd,bgkd->bghqk', qq, kwb, preferred_element_type=jnp.float32) * scale + bias_w
        mask_w = band_w & ((q0 - NSA_WINDOW + j_w) >= 0)[None]
        p_w = _masked_softmax(s_w, mask_w)
        o_w = jnp.einsum('bghqk,bgkd->bghqd', p_w.astype(vwb.dtype), vwb)
        return gg[..., 0:1] * o_c + gg[..., 1:2] * o_s + gg[..., 2:3] * o_w

    out = lax.map(block, jnp.arange(nb))
    return out.transpose(1, 0, 4, 2, 3, 5).reshape(B, S, W_A).astype(q_a.dtype)

def _swa_sink(q_b, k_b, v_b, sinks, rel_b):
    B, S, _ = q_b.shape
    G, HPG, dh, W = SWA_GROUPS, SWA_HEADS // SWA_GROUPS, HEAD_DIM, SWA_WINDOW
    nb = S // W
    scale = HEAD_DIM ** -0.5
    q = q_b.reshape(B, nb, W, G, HPG, dh)
    k = k_b.reshape(B, nb, W, G, dh)
    v = v_b.reshape(B, nb, W, G, dh)

    def with_prev(z):
        prev = jnp.pad(z[:, :-1], ((0, 0), (1, 0), (0, 0), (0, 0), (0, 0)))
        return jnp.concatenate([prev, z], axis=2)

    kk, vv = with_prev(k), with_prev(v)
    i = jnp.arange(W)
    j = jnp.arange(2 * W)
    dist = W + i[:, None] - j[None]
    band = (dist >= 0) & (dist < W)
    first = (jnp.arange(nb)[:, None] * W - W + j[None]) >= 0
    mask = band[None] & first[:, None, :]
    bias = rel_b.reshape(G, HPG, REL_BUCKETS)[:, :, _t5_bucket(dist)]
    logits = jnp.einsum('bnqghd,bnkgd->bghnqk', q, kk, preferred_element_type=jnp.float32) * scale
    logits = jnp.where(mask, logits + bias[:, :, None], -jnp.inf)
    sink = jnp.broadcast_to(sinks.astype(jnp.float32).reshape(1, G, HPG, 1, 1, 1), logits.shape[:-1] + (1,))
    p = jax.nn.softmax(jnp.concatenate([logits, sink], axis=-1), axis=-1)[..., :-1]
    o = jnp.einsum('bghnqk,bnkgd->bnqghd', p.astype(vv.dtype), vv)
    return o.reshape(B, S, W_B)

def _fox(q_c, k_c, v_c, f_c, b_f):
    B, S, _ = q_c.shape
    H, dh = FOX_HEADS, HEAD_DIM
    nb = S // Q_BLOCK
    scale = HEAD_DIM ** -0.5
    q = q_c.reshape(B, S, H, dh).transpose(0, 2, 1, 3)
    k = k_c.reshape(B, S, H, dh).transpose(0, 2, 1, 3)
    v = v_c.reshape(B, S, H, dh).transpose(0, 2, 1, 3)
    log_f = jax.nn.log_sigmoid((f_c + b_f).astype(jnp.float32))
    c = jnp.cumsum(log_f, axis=1).transpose(0, 2, 1)
    s_idx = jnp.arange(S)

    def block(qb):
        q0 = qb * Q_BLOCK
        t = q0 + jnp.arange(Q_BLOCK)
        qq = lax.dynamic_slice_in_dim(q, q0, Q_BLOCK, axis=2)
        cq = lax.dynamic_slice_in_dim(c, q0, Q_BLOCK, axis=2)
        logits = jnp.einsum('bhqd,bhkd->bhqk', qq, k, preferred_element_type=jnp.float32) * scale
        logits = logits + cq[..., None] - c[:, :, None, :]
        logits = jnp.where(s_idx[None] <= t[:, None], logits, -jnp.inf)
        p = jax.nn.softmax(logits, axis=-1)
        return jnp.einsum('bhqk,bhkd->bhqd', p.astype(v.dtype), v)

    out = lax.map(block, jnp.arange(nb))
    return out.transpose(1, 0, 3, 2, 4).reshape(B, S, W_C)

def _token_mix(h, w_in, pe_k, pe_v, ck_w1, ck_w2, cv_w1, cv_w2, sinks, b_f, rel_bias,
               w_br_a, w_br_b, w_br_c, w_gate, b_gate, w_out):
    B, S, D = h.shape
    q_a, kv_a, g_a, q_b, k_b, v_b, q_c, k_c, v_c, f_c = _split_cols(h @ w_in)
    rel_t = rel_bias.T
    o_a = _nsa(q_a, kv_a, g_a, pe_k, pe_v, ck_w1, ck_w2, cv_w1, cv_w2, rel_t[:NSA_HEADS])
    o_b = _swa_sink(q_b, k_b, v_b, sinks, rel_t[NSA_HEADS:])
    o_c = _fox(q_c, k_c, v_c, f_c, b_f)
    g = jax.nn.sigmoid(h @ w_gate + b_gate).reshape(B, S, N_BRANCH, D)
    merged = g[:, :, 0] * (o_a @ w_br_a) + g[:, :, 1] * (o_b @ w_br_b) + g[:, :, 2] * (o_c @ w_br_c)
    return merged @ w_out

def second_inputs(seed: int = 0) -> dict:
    key = jax.random.key(seed)
    keys = iter(jax.random.split(key, 32))
    L, D, F = DEPTH, D_MODEL, D_FF

    def nrm(shape, scale):
        return jax.random.normal(next(keys), shape, jnp.float32) * scale

    return {
        'x': nrm((BATCH, SEQ, D), 1.0),
        'rel_bias': nrm((REL_BUCKETS, NSA_HEADS + SWA_HEADS), 0.5),
        'ln1_g': 1.0 + nrm((L, D), 0.02),
        'ln1_b': nrm((L, D), 0.02),
        'ffn1_w1': nrm((L, D, 2 * F), D ** -0.5),
        'ffn1_w2': nrm((L, F, D), DN_BETA * F ** -0.5),
        'w_in': nrm((L, D, D_IN_2), D ** -0.5),
        'cmp_pe_k': nrm((L, CMP_BLOCK, HEAD_DIM), 0.1),
        'cmp_pe_v': nrm((L, CMP_BLOCK, HEAD_DIM), 0.1),
        'cmp_k_w1': nrm((L, CMP_BLOCK * HEAD_DIM, CMP_HIDDEN), (CMP_BLOCK * HEAD_DIM) ** -0.5),
        'cmp_k_w2': nrm((L, CMP_HIDDEN, HEAD_DIM), CMP_HIDDEN ** -0.5),
        'cmp_v_w1': nrm((L, CMP_BLOCK * HEAD_DIM, CMP_HIDDEN), (CMP_BLOCK * HEAD_DIM) ** -0.5),
        'cmp_v_w2': nrm((L, CMP_HIDDEN, HEAD_DIM), CMP_HIDDEN ** -0.5),
        'swa_sinks': nrm((L, SWA_HEADS), 1.0),
        'fox_b_f': FOX_GATE_BIAS + nrm((L, FOX_HEADS), 0.1),
        'w_br_a': nrm((L, W_A, D), W_A ** -0.5),
        'w_br_b': nrm((L, W_B, D), W_B ** -0.5),
        'w_br_c': nrm((L, W_C, D), W_C ** -0.5),
        'w_gate': nrm((L, D, N_BRANCH * D), D ** -0.5),
        'b_gate': nrm((L, N_BRANCH * D), 0.01),
        'w_out': nrm((L, D, D), DN_BETA * D ** -0.5),
        'ln2_g': 1.0 + nrm((L, D), 0.02),
        'ln2_b': nrm((L, D), 0.02),
        'ffn2_w1': nrm((L, D, 2 * F), D ** -0.5),
        'ffn2_w2': nrm((L, F, D), DN_BETA * F ** -0.5),
        'ln3_g': 1.0 + nrm((L, D), 0.02),
        'ln3_b': nrm((L, D), 0.02),
    }

def second_block(x, rel_bias, ln1_g, ln1_b, ffn1_w1, ffn1_w2, w_in, cmp_pe_k, cmp_pe_v,
              cmp_k_w1, cmp_k_w2, cmp_v_w1, cmp_v_w2, swa_sinks, fox_b_f,
              w_br_a, w_br_b, w_br_c, w_gate, b_gate, w_out, ln2_g, ln2_b,
              ffn2_w1, ffn2_w2, ln3_g, ln3_b):
    for l in range(DEPTH):
        x = _layer_norm(DN_ALPHA * x + 0.5 * _swiglu(x, ffn1_w1[l], ffn1_w2[l]), ln1_g[l], ln1_b[l])
        mix = _token_mix(x, w_in[l], cmp_pe_k[l], cmp_pe_v[l], cmp_k_w1[l], cmp_k_w2[l],
                         cmp_v_w1[l], cmp_v_w2[l], swa_sinks[l], fox_b_f[l], rel_bias,
                         w_br_a[l], w_br_b[l], w_br_c[l], w_gate[l], b_gate[l], w_out[l])
        x = _layer_norm(DN_ALPHA * x + mix, ln2_g[l], ln2_b[l])
        x = _layer_norm(DN_ALPHA * x + 0.5 * _swiglu(x, ffn2_w1[l], ffn2_w2[l]), ln3_g[l], ln3_b[l])
    return x


def setup_inputs(seed=0):
    out = dict(first_inputs(seed))
    for name, value in second_inputs(seed + 1).items():
        if name != "x":
            out[name + "_2"] = value
    return out


def reference(
    x, c, ctx, c_ctx, norm_g, w_ada, b_ada, w_in, conv_w, conv_b, cln_g, cln_b, w_proj_a,
    na_q_norm, na_k_norm, na_rpb, w_proj_b, wa_q_norm, wa_k_norm, wa_sink, w_proj_c, w_o,
    rel_bias_2, ln1_g_2, ln1_b_2, ffn1_w1_2, ffn1_w2_2, w_in_2, cmp_pe_k_2, cmp_pe_v_2,
    cmp_k_w1_2, cmp_k_w2_2, cmp_v_w1_2, cmp_v_w2_2, swa_sinks_2, fox_b_f_2, w_br_a_2, w_br_b_2,
    w_br_c_2, w_gate_2, b_gate_2, w_out_2, ln2_g_2, ln2_b_2, ffn2_w1_2, ffn2_w2_2, ln3_g_2,
    ln3_b_2,
):
    x = first_block(
        x, c, ctx, c_ctx, norm_g, w_ada, b_ada, w_in, conv_w, conv_b, cln_g, cln_b, w_proj_a,
        na_q_norm, na_k_norm, na_rpb, w_proj_b, wa_q_norm, wa_k_norm, wa_sink, w_proj_c, w_o,
    )
    return second_block(
        x, rel_bias_2, ln1_g_2, ln1_b_2, ffn1_w1_2, ffn1_w2_2, w_in_2, cmp_pe_k_2, cmp_pe_v_2,
        cmp_k_w1_2, cmp_k_w2_2, cmp_v_w1_2, cmp_v_w2_2, swa_sinks_2, fox_b_f_2, w_br_a_2,
        w_br_b_2, w_br_c_2, w_gate_2, b_gate_2, w_out_2, ln2_g_2, ln2_b_2, ffn2_w1_2, ffn2_w2_2,
        ln3_g_2, ln3_b_2,
    )


_drawn_inputs = setup_inputs


def setup_inputs(seed=0):
    import zlib

    import numpy as np

    out = dict(_drawn_inputs(seed))
    spreads = {}
    factors = {'ctx': 3.548,
     'norm_g': 8.0,
     'b_ada': 5.718,
     'conv_b': 8.0,
     'cln_g': 8.0,
     'cln_b': 8.0,
     'na_q_norm': 8.0,
     'na_k_norm': 8.0,
     'na_rpb': 8.0,
     'wa_q_norm': 8.0,
     'wa_k_norm': 8.0,
     'wa_sink': 8.0,
     'cmp_pe_k_2': 8.0,
     'cmp_pe_v_2': 7.578,
     'cmp_k_w1_2': 3.358,
     'cmp_k_w2_2': 3.446,
     'swa_sinks_2': 8.0,
     'fox_b_f_2': 64.0,
     'b_gate_2': 64.0}
    for name, (base, spread) in spreads.items():
        noise = np.random.default_rng([zlib.crc32(name.encode()), seed]).standard_normal(out[name].shape)
        drawn = base * np.exp(spread * noise) if base else spread * noise
        out[name] = jnp.asarray(drawn.astype(out[name].dtype))
    for name, factor in factors.items():
        out[name] = (out[name] * factor).astype(out[name].dtype)
    return out
```

```python
from contextlib import ExitStack

import numpy as np

import concourse.bass as bass
from concourse import mybir

F32 = mybir.dt.float32
F32R = mybir.dt.float32r
ALU = mybir.AluOpType
ACT = mybir.ActivationFunctionType
AX = mybir.AxisListType

P = 128
D = 1024
KT = D // P
S = 256
DEPTH = 2
DH = 64
HEADS = 8
GRID_W = 64
CONV_K = 31
PAD = CONV_K // 2
D_CONV = 512
D_FF = 2816
FT = D_FF // P
CB = 16
RING = 4
NC_CMP = 15
CMP_T = 32
BIG = 1e30
DN_ALPHA = (2 * DEPTH) ** 0.25
EPS = 1e-6
LN_EPS = 1e-5

A_VAL, A_GATE_IN, A_GATE, NQ, NK, NV, N_GATE, WQ, WK, WV, W_GATE, MERGE = (
    0, 512, 1024, 1536, 2048, 2560, 3072, 3584, 4096, 4224, 4352, 4864)
QA = 0
KCMP, VCMP, KSLC, VSLC, KWIN, VWIN = (512 + 128 * i for i in range(6))
GA = 1280
QB, KB, VB = 1304, 1816, 1944
QC, KC, VC, FC = 2072, 2584, 3096, 3608

ADA_CHUNKS = 12
GLU_CHUNKS = 4
QKV_CHUNKS = 10
GATE_CHUNKS = 2
MERGE_CHUNKS = 6
OUT_CHUNKS = 4
FFN_UP_CHUNKS = FT
FFN_DOWN_CHUNKS = FT // 2
MIX_CHUNKS = 17
CMP_CHUNKS = 4
CHUNKS1 = ADA_CHUNKS + GLU_CHUNKS + QKV_CHUNKS + 3 * (GATE_CHUNKS + MERGE_CHUNKS) + OUT_CHUNKS
CHUNKS2 = 2 * (FFN_UP_CHUNKS + FFN_DOWN_CHUNKS) + MIX_CHUNKS + CMP_CHUNKS + 3 * MERGE_CHUNKS + OUT_CHUNKS
CHUNKS = DEPTH * (CHUNKS1 + CHUNKS2)

def _columns(sizes):
    at, out = 0, {}
    for name, n in sizes:
        out[name] = (at, at + n)
        at += n
    return out, at


CONSTS, N_CONST = _columns([
    ("ident", 128), ("negid", 8), ("ones_model", 128), ("ones_conv", 128), ("head_mean", 128),
    ("rotate", 128), ("upto", 2 * 256), ("cos", 256), ("sin", 256), ("band", 2 * 256),
    ("causal", 256), ("causal_band", 256), ("cmp_mask", 2 * NC_CMP), ("na_mask", 64),
    ("flip", 128), ("flip_rows", 128), ("bucket", 511)])
VECS, N_VEC = _columns([
    ("norm_g", 8), ("b_ada", 24), ("conv_w", 4 * CONV_K), ("conv_b", 4), ("cln_g", 4), ("cln_b", 4),
    ("na_q", 1), ("na_k", 1), ("wa_q", 1), ("wa_k", 1), ("wa_sink", 8),
    ("ln1_g", 8), ("ln1_b", 8), ("ln2_g", 8), ("ln2_b", 8), ("ln3_g", 8), ("ln3_b", 8),
    ("b_gate", 24), ("pe_k", 16), ("pe_v", 16), ("sinks", 8), ("b_f", 8),
    ("k_w2", 2 * 128), ("v_w2", 2 * 64)])


class Count:

    def __init__(self, sem):
        self.sem, self.n = sem, 0


def build(nc, wstream, xT, ctxT, cT, consts, vecs, rpb, rel, out, dump=None):
    ctx = ExitStack()
    with ctx:
        names = {}

        def sb(name, shape, dt=F32, stack=ctx):
            names[name] = names.get(name, 0) + 1
            if names[name] > 1:
                name = f"{name}_{names[name]}"
            return stack.enter_context(nc.sbuf_tensor(name, shape, dt))

        def count(name):
            return Count(ctx.enter_context(nc.semaphore(name)))

        ring = sb("ring", [P, RING, CB * P])
        w_hi = sb("w_hi", [P, 2, CB * P], F32R)
        w_lo = sb("w_lo", [P, 2, CB * P], F32R)
        x = sb("x", [P, KT, 2 * S])
        x_hi = sb("x_hi", [P, KT, 2 * S], F32R)
        x_lo = sb("x_lo", [P, KT, 2 * S], F32R)
        cst = sb("cst", [P, N_CONST])
        vec = sb("vec", [P, DEPTH, N_VEC])
        psum = ctx.enter_context(nc.psum_tensor("psum", [P, 4096], F32))

        def const(name, rows=P):
            a, b = CONSTS[name]
            return cst[0:rows, a:b]

        def par(layer, name):
            a, b = VECS[name]
            return vec[:, layer, a:b]

        landed = [count("landed_even"), count("landed_odd")]
        hi_done = count("hi_done")
        split_done = count("split_done")
        chunk_done = count("chunk_done")
        acc_free = count("acc_free")
        loaded = count("loaded")
        step = count("step")
        read = count("read")
        mixed = count("mixed")
        gpart = count("gpart")
        hpart = count("hpart")
        lpart = count("lpart")
        conv_step = count("conv_step")
        stored = count("stored")
        g0 = [0]

        def load_ahead(sp, n):
            g = g0[0]

            def load(i, s):
                c = g + s + RING
                sp.wait_ge(split_done.sem, c - RING + 1 + 2 * i)
                sp.wait_ge(landed[c % 2].sem, 16 * (c // 2 + i))
                sp.dma_start(ring[:, (c + 2 * i) % RING, :], wstream[c + 2 * i]).then_inc(landed[c % 2].sem, 16)
            each_chunk(sp, min(n, CHUNKS + 1 - RING - g), load)

        def round_next(act, i, s):
            c = g0[0] + s + 1
            act.wait_ge(landed[c % 2].sem, 16 * (c // 2 + i + 1))
            if c > 1 or not isinstance(i, int) or i:
                act.wait_ge(chunk_done.sem, c - 1 + 2 * i)
            act.activation(w_hi[:, c % 2, :], ring[:, (c + 2 * i) % RING, :], ACT.Copy).then_inc(hi_done.sem, 1)

        def rest_next(dve, i, s):
            c = g0[0] + s + 1
            dve.wait_ge(hi_done.sem, c + 1 + 2 * i)
            dve.tensor_tensor(w_lo[:, c % 2, :], ring[:, (c + 2 * i) % RING, :],
                              w_hi[:, c % 2, :].bitcast(F32), ALU.subtract).then_inc(split_done.sem, 1)

        def each_chunk(eng, n, body):
            pairs = n // 2
            if pairs >= 4:
                lead = 0 if g0[0] else 1
                if lead:
                    body(0, 0)
                    body(0, 1)
                with eng.Fori(lead, pairs) as i:
                    body(i, 0)
                    body(i, 1)
            else:
                for i in range(pairs):
                    body(i, 0)
                    body(i, 1)
            if n % 2:
                body(pairs, 0)

        def acc(s, n, at=0):
            a = 2048 * ((g0[0] + s) % 2) + at
            return psum[:, a:a + n]

        def pe_begin(pe, i, s):
            c = g0[0] + s
            pe.wait_ge(split_done.sem, c + 1 + 2 * i)
            if c > 1 or not isinstance(i, int) or i:
                pe.wait_ge(acc_free.sem, c - 1 + 2 * i)

        def three(pe, o, w_cols, c, hi, lo, first, last):
            pe.matmul(o, w_hi[:, c, w_cols], hi, start=first, stop=False)
            pe.matmul(o, w_hi[:, c, w_cols], lo, start=False, stop=False)
            return pe.matmul(o, w_lo[:, c, w_cols], hi, start=False, stop=last)

        def pe_columns(pe, i, s, hi, lo, tok, kt=KT):
            pe_begin(pe, i, s)
            c = (g0[0] + s) % 2
            for m in range(CB // kt):
                for k in range(kt):
                    b = (m * kt + k) * P
                    mm = three(pe, acc(s, tok, m * tok), slice(b, b + P), c, hi(k), lo(k), k == 0, k == kt - 1)
            mm.then_inc(chunk_done.sem, 1)

        def pe_rows(pe, i, s, tok, cols):
            pe_begin(pe, i, s)
            c = (g0[0] + s) % 2
            for t in range(tok // P):
                for k in range(KT):
                    o = acc(s, cols, t * 256)
                    w = slice(k * 256, k * 256 + cols)
                    hi, lo = x_hi[:, k, t * P:t * P + P], x_lo[:, k, t * P:t * P + P]
                    pe.matmul(o, hi, w_hi[:, c, w], start=k == 0, stop=False)
                    pe.matmul(o, lo, w_hi[:, c, w], start=False, stop=False)
                    mm = pe.matmul(o, hi, w_lo[:, c, w], start=False, stop=k == KT - 1)
            mm.then_inc(chunk_done.sem, 1)

        def model_operand(tok):
            return (lambda k: x_hi[:, k, 0:tok]), (lambda k: x_lo[:, k, 0:tok])

        def used(n):
            g0[0] += n
            for c in (hi_done, split_done):
                c.n = g0[0] + 1
            for c in (chunk_done, acc_free):
                c.n = g0[0]


        def start_stage(c_hi, c_lo, c_in):
            with nc.Block() as block:
                @block.sync
                def _(sp):
                    for c in range(RING):
                        if c >= 2:
                            sp.wait_ge(landed[c % 2].sem, 16 * (c // 2))
                        sp.dma_start(ring[:, c, :], wstream[c]).then_inc(landed[c % 2].sem, 16)
                    sp.dma_start(x[:, :, 0:S], xT).then_inc(stored.sem, 16)
                    sp.dma_start(x[:, :, S:2 * S], ctxT).then_inc(stored.sem, 16)

                @block.scalar
                def _(act):
                    act.dma_start(c_in[:], cT).then_inc(loaded.sem, 16)
                    act.dma_start(vec[:], vecs).then_inc(loaded.sem, 16)
                    act.dma_start(cst[:], consts).then_inc(loaded.sem, 16)
                    act.wait_ge(landed[0].sem, 16)
                    act.activation(w_hi[:, 0, :], ring[:, 0, :], ACT.Copy).then_inc(hi_done.sem, 1)
                    act.wait_ge(loaded.sem, 48)
                    act.activation(c_in[:], c_in[:], ACT.Silu).then_inc(step.sem, 1)
                    act.wait_ge(step.sem, 1)
                    act.activation(c_hi[:], c_in[:], ACT.Copy).then_inc(step.sem, 1)

                @block.vector
                def _(dve):
                    dve.wait_ge(hi_done.sem, 1)
                    dve.tensor_tensor(w_lo[:, 0, :], ring[:, 0, :], w_hi[:, 0, :].bitcast(F32),
                                      ALU.subtract).then_inc(split_done.sem, 1)
                    dve.wait_ge(step.sem, 2)
                    dve.tensor_tensor(c_lo[:], c_in[:], c_hi[:].bitcast(F32), ALU.subtract).then_inc(step.sem, 1)
                    dve.wait_ge(stored.sem, 32)
            step.n, loaded.n, stored.n = 3, 48, 32

        def plain_stage(n, tok, take, kt=KT):
            with nc.Block() as block:
                @block.sync
                def _(sp):
                    load_ahead(sp, n)

                @block.tensor
                def _(pe):
                    hi, lo = model_operand(tok)
                    each_chunk(pe, n, lambda i, s: pe_columns(pe, i, s, hi, lo, tok))

                @block.scalar
                def _(act):
                    def chunk(i, s):
                        round_next(act, i, s)
                        o, func, scale = take(i, s)
                        act.wait_ge(chunk_done.sem, g0[0] + s + 1 + 2 * i)
                        act.activation(o, acc(s, 2 * tok).rearrange("p (m t) -> p m t", m=2), func,
                                       scale=scale).then_inc(acc_free.sem, 1)
                    each_chunk(act, n, chunk)

                @block.vector
                def _(dve):
                    each_chunk(dve, n, lambda i, s: rest_next(dve, i, s))
            used(n)

        def ada_stage(c_hi, c_lo, mod, layer):
            n = ADA_CHUNKS
            b_ada = par(layer, "b_ada")
            with nc.Block() as block:
                @block.sync
                def _(sp):
                    load_ahead(sp, n)

                @block.tensor
                def _(pe):
                    each_chunk(pe, n, lambda i, s: pe_columns(
                        pe, i, s, lambda k: c_hi[:, k, :], lambda k: c_lo[:, k, :], 2))

                @block.scalar
                def _(act):
                    each_chunk(act, n, lambda i, s: round_next(act, i, s))

                @block.vector
                def _(dve):
                    def chunk(i, s):
                        rest_next(dve, i, s)
                        dve.wait_ge(chunk_done.sem, g0[0] + s + 1 + 2 * i)
                        j = 2 * i + s
                        dve.tensor_tensor(
                            mod[:, 2 * j:2 * j + 2, :] if isinstance(j, int) else mod[:, bass.ds(2 * j, 2), :],
                            acc(s, 4).rearrange("p (m t) -> p m t", m=2),
                            (b_ada[:, 2 * j:2 * j + 2] if isinstance(j, int) else b_ada[:, bass.ds(2 * j, 2)]
                             ).unsqueeze(2).to_broadcast([P, 2, 2]), ALU.add).then_inc(acc_free.sem, 1)
                    each_chunk(dve, n, chunk)
            used(n)

        def model_norm_stage(mod, scales, layer, tok, scratch, rs):
            b = step.n
            segs = [(k, w) for k in range(KT) for w in range(tok // S)]
            ones = const("ones_model")
            with nc.Block() as block:
                @block.scalar
                def _(act):
                    act.activation(scratch[:, :, 0:tok], x[:, :, 0:tok], ACT.Square).then_inc(step.sem, 1)
                    act.wait_ge(step.sem, b + 3)
                    act.activation(rs[:, 0:tok], psum[:, 0:tok], ACT.Sqrt, bias=eps_col).then_inc(step.sem, 1)
                    for n, (k, w) in enumerate(segs):
                        act.wait_ge(step.sem, b + 5 + n + 1)
                        h = scratch[:, k, w * S:w * S + S]
                        act.activation(h, h, ACT.Identity, bias=mod[:, k, w:w + 1]).then_inc(read.sem, 1)
                    act.wait_ge(read.sem, read.n + len(segs))
                    act.activation(x_hi[:, :, 0:tok], scratch[:, :, 0:tok], ACT.Copy).then_inc(read.sem, 1)

                @block.tensor
                def _(pe):
                    pe.wait_ge(step.sem, b + 2)
                    for k in range(KT):
                        mm = pe.matmul(psum[:, 0:tok], ones, scratch[:, k, 0:tok], start=k == 0, stop=k == KT - 1)
                    mm.then_inc(step.sem, 1)

                @block.vector
                def _(dve):
                    dve.scalar_tensor_tensor(out=scales[:], in0=mod[:, KT:2 * KT, :], scalar=1.0,
                                             in1=par(layer, "norm_g").unsqueeze(2).to_broadcast([P, KT, 2]),
                                             op0=ALU.add, op1=ALU.mult).then_inc(step.sem, 1)
                    dve.wait_ge(step.sem, b + 4)
                    dve.reciprocal(rs[:, 0:tok], rs[:, 0:tok]).then_inc(step.sem, 1)
                    dve.wait_ge(step.sem, b + 5)
                    for k, w in segs:
                        t = slice(w * S, w * S + S)
                        dve.scalar_tensor_tensor(out=scratch[:, k, t], in0=x[:, k, t], scalar=scales[:, k, w:w + 1],
                                                 in1=rs[:, t], op0=ALU.mult, op1=ALU.mult).then_inc(step.sem, 1)
                    dve.wait_ge(read.sem, read.n + len(segs) + 1)
                    dve.tensor_tensor(x_lo[:, :, 0:tok], scratch[:, :, 0:tok], x_hi[:, :, 0:tok].bitcast(F32),
                                      ALU.subtract).then_inc(read.sem, 1)
            step.n += 5 + len(segs)
            read.n += len(segs) + 2

        def split_stage(src, hi, lo):
            b = step.n
            with nc.Block() as block:
                @block.scalar
                def _(act):
                    act.activation(hi, src, ACT.Copy).then_inc(step.sem, 1)

                @block.vector
                def _(dve):
                    dve.wait_ge(step.sem, b + 1)
                    dve.tensor_tensor(lo, src, hi.bitcast(F32), ALU.subtract).then_inc(step.sem, 1)
            step.n += 2

        def layer_norm_stage(src, nt, tok, ones, eps, gains, biases, func, scratch, rs, split=False):
            b = step.n
            with nc.Block() as block:
                @block.tensor
                def _(pe):
                    for k in range(nt):
                        mm = pe.matmul(psum[:, 0:tok], ones, src[:, k, 0:tok], start=k == 0, stop=k == nt - 1)
                    mm.then_inc(step.sem, 1)
                    pe.wait_ge(step.sem, b + 3)
                    for k in range(nt):
                        mm = pe.matmul(psum[:, 512:512 + tok], ones, scratch[:, k, 0:tok],
                                       start=k == 0, stop=k == nt - 1)
                    mm.then_inc(step.sem, 1)

                @block.vector
                def _(dve):
                    dve.wait_ge(step.sem, b + 1)
                    dve.tensor_tensor(src[:, 0:nt, 0:tok], src[:, 0:nt, 0:tok],
                                      psum[:, 0:tok].unsqueeze(1).to_broadcast([P, nt, tok]),
                                      ALU.subtract).then_inc(step.sem, 1)
                    dve.wait_ge(step.sem, b + 5)
                    dve.reciprocal(rs[:, 0:tok], rs[:, 0:tok]).then_inc(step.sem, 1)
                    dve.wait_ge(step.sem, b + 6)
                    dve.tensor_tensor(src[:, 0:nt, 0:tok], src[:, 0:nt, 0:tok],
                                      rs[:, 0:tok].unsqueeze(1).to_broadcast([P, nt, tok]),
                                      ALU.mult).then_inc(step.sem, 1)
                    if split:
                        dve.wait_ge(step.sem, b + 8 + nt)
                        dve.tensor_tensor(x_lo[:, 0:nt, 0:tok], src[:, 0:nt, 0:tok],
                                          x_hi[:, 0:nt, 0:tok].bitcast(F32), ALU.subtract).then_inc(step.sem, 1)

                @block.scalar
                def _(act):
                    act.wait_ge(step.sem, b + 2)
                    act.activation(scratch[:, 0:nt, 0:tok], src[:, 0:nt, 0:tok], ACT.Square).then_inc(step.sem, 1)
                    act.wait_ge(step.sem, b + 4)
                    act.activation(rs[:, 0:tok], psum[:, 512:512 + tok], ACT.Sqrt, bias=eps).then_inc(step.sem, 1)
                    act.wait_ge(step.sem, b + 7)
                    for k in range(nt):
                        act.activation(src[:, k, 0:tok], src[:, k, 0:tok], func, scale=gains[:, k:k + 1],
                                       bias=biases[:, k:k + 1]).then_inc(step.sem, 1)
                    if split:
                        act.wait_ge(step.sem, b + 7 + nt)
                        act.activation(x_hi[:, 0:nt, 0:tok], src[:, 0:nt, 0:tok], ACT.Copy).then_inc(step.sem, 1)
            step.n += 7 + nt + (2 if split else 0)

        scored = count("scored")
        plain_max = count("plain_max")
        biased = count("biased")
        shift = count("shift")
        exped = count("exped")
        small = count("small")
        scaled = count("scaled")
        turned = count("turned")
        turned_sb = count("turned_sb")
        summed = count("summed")
        taken = count("taken")

        def attention_stage(units, dst, T):
            U = len(units)
            base = {c: c.n for c in (scored, plain_max, biased, shift, exped, small, scaled, turned, turned_sb,
                                     summed, taken)}
            nplain = np.cumsum([1 if u["plain"] else 0 for u in units]).tolist()
            nbias = np.cumsum([1 if u["bias"] is not None else 0 for u in units]).tolist()
            nexp = np.cumsum([(u["bias"] is not None) + (u["plain"] > 0) + ("sink" in u) for u in units]).tolist()

            def smalls(u):
                e = (u["bias"] is not None) + (u["plain"] > 0) + ("sink" in u)
                return (e > 1) + ("floor" in u) + 1 + ("gate" in u)
            nsmall = np.cumsum([smalls(u) for u in units]).tolist()
            pairs = [u["pair"] for u in units]
            ends = [n for n in range(U) if n == U - 1 or pairs[n + 1] != pairs[n]]

            def after(c, counts, u):
                return base[c] + (counts[u] if u >= 0 else 0)

            def s_ps(u, a, n):
                return psum[:, (u % 3) * 512 + a:(u % 3) * 512 + a + n]

            def t_ps(u, n):
                return psum[:, 1536 + (u % 2) * 512:1536 + (u % 2) * 512 + n]

            def o_ps(pair):
                return psum[:, 2560 + (pair % 2) * 512:2560 + (pair % 2) * 512 + 2 * P]

            def blocks(u):
                n = u["nb"] + u["plain"]
                return [(a, min(P, n - a)) for a in range(0, n, P)]

            with ExitStack() as st, nc.Block() as block:
                sbias, prob, probT, mx, den, fac, neg = T

                @block.tensor
                def _(pe):
                    for t in range(U + 3):
                        if t < U:
                            u = units[t]
                            if t >= 3:
                                pe.wait_ge(exped.sem, after(exped, nexp, t - 3))
                                pe.wait_ge(plain_max.sem, after(plain_max, nplain, t - 3))
                                pe.wait_ge(biased.sem, after(biased, nbias, t - 3))
                            mms = [(u["q"], k, a) for k, a in u["keys"]]
                            n = u["nb"] + u["plain"]
                            extra = u.get("extra", [])
                            assert len(mms) == 1
                            mm = pe.matmul(s_ps(t, 0, n), mms[0][0], mms[0][1], start=True, stop=not extra)
                            for e, (l, r) in enumerate(extra):
                                mm = pe.matmul(s_ps(t, 0, n), l, r, start=False, stop=e == len(extra) - 1)
                            mm.then_inc(scored.sem, 1)
                        v = t - 2
                        if 0 <= v < U:
                            pe.wait_ge(scaled.sem, base[scaled] + v + 1)
                            if v >= 2:
                                pe.wait_ge(turned_sb.sem, base[turned_sb] + v - 1)
                            for a, w in blocks(units[v]):
                                mm = pe.transpose(psum[0:w, 1536 + (v % 2) * 512 + a:1536 + (v % 2) * 512 + a + P],
                                                  prob[:, v % 3, a:a + w], const("ident"))
                            mm.then_inc(turned.sem, 1)
                        v = t - 3
                        if 0 <= v < U:
                            u = units[v]
                            pe.wait_ge(turned_sb.sem, base[turned_sb] + v + 1)
                            if u["pair"] >= 2:
                                pe.wait_ge(taken.sem, base[taken] + u["pair"] - 1)
                            part, qt = u["part"], u["qt"]
                            o = o_ps(u["pair"])[part:part + DH, qt * P:qt * P + P]
                            bl = blocks(u)
                            for n, (a, w) in enumerate(bl):
                                mm = pe.matmul(o, u["vals"][n], probT[0:w, v % 2, a:a + P],
                                               start=u["first"] and n == 0, stop=u["last"] and n == len(bl) - 1)
                            mm.then_inc(summed.sem, 1)

                @block.vector
                def _(dve):
                    done = 0
                    for t in range(U + 3):
                        if t < U:
                            u = units[t]
                            nb, npl = u["nb"], u["plain"]
                            dve.wait_ge(scored.sem, base[scored] + t + 1)
                            if t >= 3:
                                dve.wait_ge(scaled.sem, base[scaled] + t - 2)
                            if npl:
                                dve.tensor_reduce(mx[:, t % 3, 0:1], s_ps(t, nb, npl), AX.X, ALU.max
                                                  ).then_inc(plain_max.sem, 1)
                                dve.wait_ge(plain_max.sem, after(plain_max, nplain, t))
                            if nb:
                                dve.tensor_tensor_reduce(sbias[:, t % 3, 0:nb], s_ps(t, 0, nb), u["bias"], 1.0,
                                                         mx[:, t % 3, 0:1] if npl else -3e38, ALU.add, ALU.max,
                                                         mx[:, t % 3, 1:2]).then_inc(biased.sem, 1)
                                dve.wait_ge(biased.sem, after(biased, nbias, t))
                            top = u["sink"] if "sink" in u else u.get("floor", -3e38)
                            dve.tensor_scalar(neg[:, t % 3, 0:1], mx[:, t % 3, (1 if nb else 0):(2 if nb else 1)],
                                              top, -1.0, ALU.max, ALU.mult).then_inc(shift.sem, 1)
                        v = t - 1
                        if 0 <= v < U:
                            u = units[v]
                            k = after(small, nsmall, v - 1)
                            e = (nexp[v] - (nexp[v - 1] if v else 0))
                            dve.wait_ge(exped.sem, after(exped, nexp, v))
                            src = den[:, v % 3, 0:1]
                            if e > 1:
                                dve.tensor_reduce(den[:, v % 3, 3:4], den[:, v % 3, 0:e], AX.X, ALU.add
                                                  ).then_inc(small.sem, 1)
                                k += 1
                                dve.wait_ge(small.sem, k)
                                src = den[:, v % 3, 3:4]
                            if "floor" in u:
                                dve.tensor_scalar(den[:, v % 3, 3:4], src, 1e-30, None, ALU.max).then_inc(small.sem, 1)
                                k += 1
                                dve.wait_ge(small.sem, k)
                                src = den[:, v % 3, 3:4]
                            dve.reciprocal(fac[:, v % 3, 0:1], src).then_inc(small.sem, 1)
                            k += 1
                            if "gate" in u:
                                dve.wait_ge(small.sem, k)
                                dve.tensor_scalar(fac[:, v % 3, 1:2], fac[:, v % 3, 0:1], u["gate"], None, ALU.mult
                                                  ).then_inc(small.sem, 1)
                        v = t - 3
                        if v in ends:
                            pair = units[v]["pair"]
                            dve.wait_ge(summed.sem, base[summed] + v + 1)
                            dve.tensor_copy(dst(pair), o_ps(pair)[:, 0:dst(pair).shape[1]]).then_inc(taken.sem, 1)

                @block.scalar
                def _(act):
                    for t in range(U + 3):
                        if t < U:
                            u = units[t]
                            nb, npl = u["nb"], u["plain"]
                            act.wait_ge(shift.sem, base[shift] + t + 1)
                            if t >= 3:
                                act.wait_ge(turned.sem, base[turned] + t - 2)
                                act.wait_ge(small.sem, after(small, nsmall, t - 3))
                            e = 0
                            if nb:
                                act.activation(prob[:, t % 3, 0:nb], sbias[:, t % 3, 0:nb], ACT.Exp,
                                               bias=neg[:, t % 3, 0:1], accum_out=den[:, t % 3, e:e + 1]
                                               ).then_inc(exped.sem, 1)
                                e += 1
                            if npl:
                                act.activation(prob[:, t % 3, nb:nb + npl], s_ps(t, nb, npl), ACT.Exp,
                                               bias=neg[:, t % 3, 0:1], accum_out=den[:, t % 3, e:e + 1]
                                               ).then_inc(exped.sem, 1)
                                e += 1
                            if "sink" in u:
                                act.activation(den[:, t % 3, e:e + 1], u["sink"], ACT.Exp,
                                               bias=neg[:, t % 3, 0:1]).then_inc(exped.sem, 1)
                        v = t - 2
                        if 0 <= v < U:
                            act.wait_ge(turned.sem, base[turned] + v + 1)
                            if v >= 2:
                                act.wait_ge(summed.sem, base[summed] + v - 1)
                            bl = blocks(units[v])
                            w = bl[-1][1]
                            n = len(bl) * P
                            act.activation(probT[0:w, v % 2, 0:n], psum[0:w, 1536 + (v % 2) * 512:
                                                                        1536 + (v % 2) * 512 + n],
                                           ACT.Copy).then_inc(turned_sb.sem, 1)

                @block.gpsimd
                def _(pool):
                    for v in range(U):
                        u = units[v]
                        n = u["nb"] + u["plain"]
                        pool.wait_ge(small.sem, after(small, nsmall, v))
                        f = fac[:, v % 3, 1:2] if "gate" in u else fac[:, v % 3, 0:1]
                        pool.tensor_scalar(prob[:, v % 3, 0:n], prob[:, v % 3, 0:n], f, None, ALU.mult
                                           ).then_inc(scaled.sem, 1)
            for c in (scored, shift, scaled, turned, turned_sb, summed):
                c.n += U
            plain_max.n += nplain[-1]
            biased.n += nbias[-1]
            exped.n += nexp[-1]
            small.n += nsmall[-1]
            taken.n += len(ends)

        def attention_buffers(st):
            return (sb("sbias", [P, 3, 256], stack=st), sb("prob", [P, 3, 512], stack=st),
                    sb("probT", [P, 2, 512], stack=st), sb("mx", [P, 3, 2], stack=st),
                    sb("den", [P, 3, 4], stack=st), sb("fac", [P, 3, 2], stack=st), sb("neg", [P, 3, 1], stack=st))

        def merge_stage(y, sg, prod, op_hi, op_lo, tok, first, bias=None):
            n = MERGE_CHUNKS
            rb, mb, hb = read.n, mixed.n, gpart.n
            with nc.Block() as block:
                @block.sync
                def _(sp):
                    load_ahead(sp, n)

                @block.tensor
                def _(pe):
                    hi, lo = model_operand(tok)
                    for j in range(n):
                        if j % 3 < 2:
                            pe_columns(pe, j // 2, j % 2, hi, lo, tok)
                        else:
                            pe_columns(pe, j // 2, j % 2, lambda k: op_hi[:, k, 0:tok],
                                       lambda k: op_lo[:, k, 0:tok], tok, kt=4)

                @block.scalar
                def _(act):
                    for j in range(n):
                        round_next(act, j // 2, j % 2)
                        if j % 3 == 2:
                            continue
                        act.wait_ge(chunk_done.sem, g0[0] + j + 1)
                        if j == 3:
                            act.wait_ge(acc_free.sem, g0[0] + 3)
                        if bias is None:
                            act.activation(sg[:, 2 * (j % 3):2 * (j % 3) + 2, 0:tok],
                                           acc(j % 2, 2 * tok).rearrange("p (m t) -> p m t", m=2),
                                           ACT.Sigmoid).then_inc(acc_free.sem, 1)
                        else:
                            for m in range(2):
                                col = 4 * (j // 3) + 2 * (j % 3) + m
                                a = act.activation(sg[:, 2 * (j % 3) + m, 0:tok], acc(j % 2, tok, m * tok),
                                                   ACT.Sigmoid, bias=bias[:, col:col + 1])
                                a.then_inc(acc_free.sem if m else gpart.sem, 1)

                @block.vector
                def _(dve):
                    for j in range(n):
                        rest_next(dve, j // 2, j % 2)
                        if j % 3 < 2:
                            continue
                        h = j // 3
                        dve.wait_ge(acc_free.sem, g0[0] + j)
                        dve.wait_ge(chunk_done.sem, g0[0] + j + 1)
                        a = acc(j % 2, 4 * tok).rearrange("p (m t) -> p m t", m=4)
                        dest = y[:, 4 * h:4 * h + 4, 0:tok] if first else prod[:, :, 0:tok]
                        if not first and h:
                            dve.wait_ge(mixed.sem, mb + 1)
                        dve.tensor_tensor(dest, a, sg[:, :, 0:tok], ALU.mult).then_inc(acc_free.sem, 1)
                        if not first:
                            dve.wait_ge(acc_free.sem, g0[0] + j + 1)
                            dve.tensor_tensor(y[:, 4 * h:4 * h + 4, 0:tok], y[:, 4 * h:4 * h + 4, 0:tok],
                                              prod[:, :, 0:tok], ALU.add).then_inc(mixed.sem, 1)
            if bias is not None:
                gpart.n += 4
            mixed.n += 0 if first else 2
            used(n)

        consts_small = sb("consts_small", [P, 2])
        eps_col, ln_eps_col = consts_small[:, 0:1], consts_small[:, 1:2]
        c_in = sb("c_in", [P, KT, 2])
        c_hi = sb("c_hi", [P, KT, 2], F32R)
        c_lo = sb("c_lo", [P, KT, 2], F32R)
        mod = sb("mod", [P, 3 * KT, 2])
        scales = sb("scales", [P, KT, 2])
        rs = sb("rs", [P, 2 * S])
        with nc.Block() as block:
            @block.vector
            def _(dve):
                dve.memset(eps_col, EPS)
                dve.memset(ln_eps_col, LN_EPS)
        start_stage(c_hi, c_lo, c_in)

        def probe(name, ap):
            if dump is None or name not in dump:
                return
            d = nc.dram_tensor("dbg_" + name, list(ap.shape), ap.dtype, kind="ExternalOutput").ap()
            with nc.Block() as block:
                @block.sync
                def _(sp):
                    sp.dma_start(d, ap).then_inc(stored.sem, 16)
                    sp.wait_ge(stored.sem, stored.n + 16)
            stored.n += 16

        def block1(layer):
            tok = 2 * S if layer == 0 else S
            sets = tok // S
            ada_stage(c_hi, c_lo, mod, layer)
            with ExitStack() as st:
                scratch = sb("scratch", [P, KT, 2 * S], stack=st)
                model_norm_stage(mod, scales, layer, 2 * S, scratch, rs)
            probe(f"h{layer}", x_hi[:].bitcast(F32))
            with ExitStack() as st:
                conv_out = sb("conv_out", [P, 4, 2 * S], stack=st)
                nq = sb("nq", [P, 4, 2 * S], stack=st)
                wq = sb("wq", [P, 4, 2 * S], stack=st)
                with ExitStack() as st2:
                    nk = sb("nk", [P, 4, 2 * S], stack=st2)
                    nv = sb("nv", [P, 4, 512], stack=st2)
                    wk = sb("wk", [P, 2, 2 * S], stack=st2)
                    wv = sb("wv", [P, 4, 128], stack=st2)
                    with ExitStack() as st3:
                        cpad = sb("cpad", [P, 4, 2, S + 2 * PAD], stack=st3)
                        glu_gate = sb("glu_gate", [P, 4, 2 * S], stack=st3)
                        glu_stage(cpad, glu_gate, tok)
                        qkv_stage(layer, tok, cpad, conv_out, nq, nk, nv, wq, wk, wv)
                    probe(f"conv{layer}", conv_out[:])
                    with ExitStack() as st3:
                        scratch = sb("scratch", [P, 4, 2 * S], stack=st3)
                        layer_norm_stage(conv_out, 4, tok, const("ones_conv"), eps_col, par(layer, "cln_g"),
                                         par(layer, "cln_b"), ACT.Silu, scratch, rs)
                    probe(f"convln{layer}", conv_out[:])
                    with ExitStack() as st3:
                        qk_norm_stage(layer, tok, nq, nk, wq, wk, st3)
                    probe(f"nq{layer}", nq[:])
                    probe(f"wq{layer}", wq[:])
                    probe(f"wk{layer}", wk[:])
                    with ExitStack() as st3:
                        na_bias = sb("na_bias", [P, HEADS, 6 * GRID_W], stack=st3)
                        bufs = attention_buffers(st3)
                        na_bias_stage(layer, na_bias)
                        attend1(layer, tok, nq, nk, nv, wq, wk, wv, na_bias, bufs)
                    probe(f"ona{layer}", nq[:])
                    probe(f"owa{layer}", wq[:])
                with ExitStack() as st2:
                    y = sb("y", [P, KT, 2 * S], stack=st2)
                    sg = sb("sg", [P, 4, 2 * S], stack=st2)
                    prod = sb("prod", [P, 4, 2 * S], stack=st2)
                    op_hi = sb("op_hi", [P, 4, 2 * S], F32R, stack=st2)
                    op_lo = sb("op_lo", [P, 4, 2 * S], F32R, stack=st2)
                    for n, branch in enumerate((conv_out, nq, wq)):
                        gate_stage(branch, prod, op_hi, op_lo, tok)
                        merge_stage(y, sg, prod, op_hi, op_lo, tok, n == 0)
                    probe(f"y{layer}", y[:])
                    split_stage(y[:, :, 0:tok], x_hi[:, :, 0:tok], x_lo[:, :, 0:tok])
            out_stage1(tok)
            probe(f"x{layer}", x[:])

        def glu_stage(cpad, glu_gate, tok):
            sets = tok // S
            n = GLU_CHUNKS
            rb = read.n
            with nc.Block() as block:
                @block.sync
                def _(sp):
                    load_ahead(sp, n)

                @block.tensor
                def _(pe):
                    hi, lo = model_operand(tok)
                    for j in range(n):
                        pe_columns(pe, j // 2, j % 2, hi, lo, tok)

                @block.scalar
                def _(act):
                    for j in range(n):
                        round_next(act, j // 2, j % 2)
                        act.wait_ge(chunk_done.sem, g0[0] + j + 1)
                        a = acc(j % 2, 2 * tok)
                        if j < 2:
                            for w in range(sets):
                                o = act.activation(
                                    cpad[:, 2 * j:2 * j + 2, w, PAD:PAD + S],
                                    a.rearrange("p (m t) -> p m t", m=2)[:, :, w * S:w * S + S], ACT.Copy)
                                o.then_inc(acc_free.sem if w == sets - 1 else gpart.sem, 1)
                        else:
                            act.activation(glu_gate[:, 2 * j - 4:2 * j - 2, 0:tok],
                                           a.rearrange("p (m t) -> p m t", m=2), ACT.Sigmoid
                                           ).then_inc(acc_free.sem, 1)

                @block.gpsimd
                def _(pool):
                    pool.memset(cpad[:, :, :, 0:PAD], 0.0)
                    pool.memset(cpad[:, :, :, PAD + S:], 0.0)

                @block.vector
                def _(dve):
                    for j in range(n):
                        rest_next(dve, j // 2, j % 2)
                        if j >= 2:
                            m = slice(2 * j - 4, 2 * j - 2)
                            dve.wait_ge(acc_free.sem, g0[0] + j + 1)
                            for w in range(sets):
                                v = cpad[:, m, w, PAD:PAD + S]
                                dve.tensor_tensor(v, v, glu_gate[:, m, w * S:w * S + S], ALU.mult
                                                  ).then_inc(read.sem, 1)
            read.n += 2 * sets
            if sets == 2:
                gpart.n += 2
            used(n)

        def qkv_stage(layer, tok, cpad, conv_out, nq, nk, nv, wq, wk, wv):
            sets = tok // S
            plan = [("c", 2 * S, nk[:, 0:2, :]), ("c", 2 * S, nk[:, 2:4, :]), ("c", 2 * S, wk[:, :, :]),
                    ("r", 2 * S, nv[:, :, 0:256]), ("r", 2 * S, nv[:, :, 256:512]), ("r", 2 * S, wv[:, :, :]),
                    ("c", tok, nq[:, 0:2, 0:tok]), ("c", tok, nq[:, 2:4, 0:tok]),
                    ("c", tok, wq[:, 0:2, 0:tok]), ("c", tok, wq[:, 2:4, 0:tok])]
            n = QKV_CHUNKS
            taps = [(ct, k) for k in range(CONV_K) for ct in range(4)]
            cuts = [round(len(taps) * j / n) for j in range(n + 1)]
            cb = conv_step.n
            w_conv = par(layer, "conv_w")
            b_conv = par(layer, "conv_b")
            with nc.Block() as block:
                @block.sync
                def _(sp):
                    load_ahead(sp, n)

                @block.tensor
                def _(pe):
                    for j, (kind, t, o) in enumerate(plan):
                        if kind == "c":
                            pe_columns(pe, j // 2, j % 2, *model_operand(t), t)
                        else:
                            pe_rows(pe, j // 2, j % 2, t, min(256, o.shape[2]))

                @block.scalar
                def _(act):
                    for j, (kind, t, o) in enumerate(plan):
                        round_next(act, j // 2, j % 2)
                        act.wait_ge(chunk_done.sem, g0[0] + j + 1)
                        if kind == "c":
                            a = acc(j % 2, 2 * t).rearrange("p (m t) -> p m t", m=2)
                        else:
                            a = acc(j % 2, 1024).rearrange("p (t c) -> p t c", t=4)[:, :, 0:o.shape[2]]
                        act.activation(o, a, ACT.Copy).then_inc(acc_free.sem, 1)

                @block.vector
                def _(dve):
                    for j in range(n):
                        rest_next(dve, j // 2, j % 2)
                        for c in range(cuts[j], cuts[j + 1]):
                            ct, k = taps[c]
                            src = cpad[:, ct, 0:sets, k:k + S]
                            o = conv_out[:, ct, 0:tok].rearrange("p (w t) -> p w t", w=sets)
                            wc = w_conv[:, ct * CONV_K + k:ct * CONV_K + k + 1]
                            if k == 0:
                                dve.tensor_scalar(o, src, wc, b_conv[:, ct:ct + 1], ALU.mult, ALU.add
                                                  ).then_inc(conv_step.sem, 1)
                            else:
                                dve.wait_ge(conv_step.sem, cb + c - 3)
                                dve.scalar_tensor_tensor(out=o, in0=src, scalar=wc, in1=o, op0=ALU.mult,
                                                         op1=ALU.add).then_inc(conv_step.sem, 1)
            conv_step.n += len(taps)
            used(n)

        def qk_norm_stage(layer, tok, nq, nk, wq, wk, st):
            gains = sb("gains", [P, 4], stack=st)
            tmp = sb("tmp", [P, 2, 4 * 2 * S], stack=st)
            items = [(nq, 4, tok, 0), (nk, 4, 2 * S, 1), (wq, 4, tok, 2), (wk, 2, 2 * S, 3)]
            b, rb, vb = step.n, read.n, mixed.n
            with nc.Block() as block:
                @block.scalar
                def _(act):
                    for e, (t, nt, tk, g) in enumerate(items):
                        v = tmp[:, e % 2, 0:nt * tk].rearrange("p (m t) -> p m t", m=nt)
                        if e >= 2:
                            act.wait_ge(mixed.sem, vb + 2 * (e - 1))
                        act.activation(v, t[:, 0:nt, 0:tk], ACT.Square).then_inc(step.sem, 1)
                        act.wait_ge(step.sem, b + 3 * e + 2)
                        act.activation(v, psum[:, 2048 * (e % 2):2048 * (e % 2) + nt * tk].rearrange(
                            "p (m t) -> p m t", m=nt), ACT.Sqrt, bias=eps_col).then_inc(step.sem, 1)

                @block.tensor
                def _(pe):
                    for e, (t, nt, tk, g) in enumerate(items):
                        pe.wait_ge(step.sem, b + 3 * e + 1)
                        for m in range(nt):
                            a = 2048 * (e % 2) + m * tk
                            mm = pe.matmul(psum[:, a:a + tk], const("head_mean"), tmp[:, e % 2, m * tk:m * tk + tk],
                                           start=True, stop=True)
                        mm.then_inc(step.sem, 1)
                    for e, (t, nt) in enumerate(((wq, 4), (wk, 2))):
                        pe.wait_ge(mixed.sem, vb + 2 * (3 + e))
                        for m in range(nt):
                            a = 2048 * e + m * S
                            mm = pe.matmul(psum[:, a:a + S], const("rotate"), t[:, m, 0:S], start=True, stop=True)
                        mm.then_inc(gpart.sem, 1)

                @block.vector
                def _(dve):
                    g0v = VECS["na_q"][0]
                    for a in (0, 2):
                        dve.tensor_scalar(gains[:, a:a + 1], vec[:, layer, g0v + a:g0v + a + 1], DH ** -0.5, None,
                                          ALU.mult).then_inc(read.sem, 1)
                        dve.tensor_copy(gains[:, a + 1:a + 2], vec[:, layer, g0v + a + 1:g0v + a + 2]
                                        ).then_inc(read.sem, 1)
                    dve.wait_ge(read.sem, rb + 4)
                    for e, (t, nt, tk, g) in enumerate(items):
                        v = tmp[:, e % 2, 0:nt * tk]
                        dve.wait_ge(step.sem, b + 3 * e + 3)
                        dve.reciprocal(v, v).then_inc(mixed.sem, 1)
                        dve.wait_ge(mixed.sem, vb + 2 * e + 1)
                        q = t[:, 0:nt, 0:tk]
                        dve.scalar_tensor_tensor(out=q, in0=q, scalar=gains[:, g:g + 1],
                                                 in1=v.rearrange("p (m t) -> p m t", m=nt), op0=ALU.mult,
                                                 op1=ALU.mult).then_inc(mixed.sem, 1)
                    for e, (t, nt) in enumerate(((wq, 4), (wk, 2))):
                        dve.wait_ge(gpart.sem, gpart.n + e + 1)
                        dve.wait_ge(mixed.sem, vb + 8 + 3 * e)
                        rot = tmp[:, 0, 0:nt * S].rearrange("p (m t) -> p m t", m=nt)
                        q = t[:, 0:nt, 0:S]
                        dve.tensor_tensor(rot, psum[:, 2048 * e:2048 * e + nt * S].rearrange(
                            "p (m t) -> p m t", m=nt), const("sin").unsqueeze(1).to_broadcast([P, nt, S]),
                            ALU.mult).then_inc(mixed.sem, 1)
                        dve.tensor_tensor(q, q, const("cos").unsqueeze(1).to_broadcast([P, nt, S]), ALU.mult
                                          ).then_inc(mixed.sem, 1)
                        dve.wait_ge(mixed.sem, vb + 8 + 3 * e + 2)
                        dve.tensor_tensor(q, q, rot, ALU.add).then_inc(mixed.sem, 1)
            step.n += 12
            read.n += 4
            mixed.n += 8 + 6
            gpart.n += 2

        def na_bias_stage(layer, na_bias):
            lb, b = loaded.n, step.n
            with nc.Block() as block:
                @block.sync
                def _(sp):
                    for a in range(2):
                        for h in range(HEADS):
                            off = ((layer * HEADS + h) * 15 + 5 - a) * 31 + 15 - (GRID_W - 1)
                            sp.dma_start(na_bias[a * GRID_W:(a + 1) * GRID_W, h, :].rearrange(
                                "p (e c) -> p e c", e=6),
                                bass.AP(rpb.tensor, off, [[1, GRID_W], [31, 6], [1, GRID_W]])
                            ).then_inc(loaded.sem, 16)

                @block.tensor
                def _(pe):
                    pe.wait_ge(loaded.sem, lb + 16 * 16)
                    flat = na_bias[:].rearrange("p h e -> p (h e)")
                    for a in range(0, HEADS * 6 * GRID_W, 512):
                        mm = pe.matmul(psum[:, a:a + 512], const("flip_rows"), flat[:, a:a + 512],
                                       start=True, stop=True)
                    mm.then_inc(step.sem, 1)

                @block.vector
                def _(dve):
                    dve.wait_ge(step.sem, b + 1)
                    dve.tensor_tensor(na_bias[:].rearrange("p h (e c) -> p (h e) c", c=GRID_W),
                                      psum[:, 0:HEADS * 6 * GRID_W].rearrange("p (n c) -> p n c", c=GRID_W),
                                      const("na_mask").unsqueeze(1).to_broadcast([P, 48, GRID_W]), ALU.add
                                      ).then_inc(step.sem, 1)
            loaded.n += 256
            step.n += 2

        def attend1(layer, tok, nq, nk, nv, wq, wk, wv, na_bias, bufs):
            def q_of(t, h, qt):
                b = DH * (h % 2)
                return t[b:b + DH, h // 2, qt * P:qt * P + P]

            units = []
            for h in range(HEADS):
                b = DH * (h % 2)
                for qt in range(2):
                    units.append(dict(
                        q=q_of(nq, h, qt), keys=[(nk[b:b + DH, h // 2, :], 0)], nb=256, plain=256,
                        bias=na_bias[:, h, (2 - 2 * qt) * GRID_W:(2 - 2 * qt) * GRID_W + 256],
                        vals=[nv[:, t, h * DH:h * DH + DH] for t in range(4)],
                        part=b, qt=qt, pair=h // 2, first=True, last=True))
            if layer == 0:
                ctx_attend(nq, nk, nv, lambda h: nk[DH * (h % 2):DH * (h % 2) + DH, h // 2, S:2 * S],
                           lambda h, t: nv[:, 2 + t, h * DH:h * DH + DH], None, bufs)
            attention_stage(units, lambda pair: nq[:, pair, 0:S], bufs)
            units = []
            for h in range(HEADS):
                b = DH * (h % 2)
                g = h // 4
                for qt in range(2):
                    units.append(dict(
                        q=q_of(wq, h, qt), keys=[(wk[b:b + DH, g, :], 0)], nb=256, plain=256,
                        bias=const("band")[:, qt * 256:qt * 256 + 256],
                        vals=[wv[:, t, g * DH:g * DH + DH] for t in range(4)],
                        part=b, qt=qt, pair=h // 2, first=True, last=True,
                        sink=par(layer, "wa_sink")[:, h:h + 1]))
            if layer == 0:
                ctx_attend(wq, wk, wv, lambda h: wk[DH * (h % 2):DH * (h % 2) + DH, h // 4, S:2 * S],
                           lambda h, t: wv[:, 2 + t, (h // 4) * DH:(h // 4) * DH + DH], par(layer, "wa_sink"), bufs)
            attention_stage(units, lambda pair: wq[:, pair, 0:S], bufs)

        def ctx_attend(q, k, v, key, val, sink, bufs):
            units = []
            for h in range(HEADS):
                b = DH * (h % 2)
                for qt in range(2):
                    u = dict(q=q[b:b + DH, h // 2, S + qt * P:S + qt * P + P], keys=[(key(h), 0)], nb=0, plain=256,
                             bias=None, vals=[val(h, 0), val(h, 1)], part=b, qt=qt, pair=h // 2, first=True,
                             last=True)
                    if sink is not None:
                        u["sink"] = sink[:, h:h + 1]
                    units.append(u)
            attention_stage(units, lambda pair: q[:, pair, S:2 * S], bufs)

        def gate_stage(branch, gate, op_hi, op_lo, tok):
            n = GATE_CHUNKS
            mb, hb = mixed.n, hpart.n
            with nc.Block() as block:
                @block.sync
                def _(sp):
                    load_ahead(sp, n)

                @block.tensor
                def _(pe):
                    for j in range(n):
                        pe_columns(pe, j // 2, j % 2, *model_operand(tok), tok)

                @block.scalar
                def _(act):
                    for j in range(n):
                        round_next(act, j // 2, j % 2)
                        act.wait_ge(chunk_done.sem, g0[0] + j + 1)
                        act.activation(gate[:, 2 * j:2 * j + 2, 0:tok],
                                       acc(j % 2, 2 * tok).rearrange("p (m t) -> p m t", m=2), ACT.Silu
                                       ).then_inc(acc_free.sem, 1)
                    for j in range(n):
                        m = slice(2 * j, 2 * j + 2)
                        act.wait_ge(mixed.sem, mb + j + 1)
                        act.activation(op_hi[:, m, 0:tok], branch[:, m, 0:tok], ACT.Copy).then_inc(hpart.sem, 1)

                @block.vector
                def _(dve):
                    for j in range(n):
                        rest_next(dve, j // 2, j % 2)
                    for j in range(n):
                        m = slice(2 * j, 2 * j + 2)
                        dve.wait_ge(acc_free.sem, g0[0] + j + 1)
                        dve.tensor_tensor(branch[:, m, 0:tok], branch[:, m, 0:tok], gate[:, m, 0:tok], ALU.mult
                                          ).then_inc(mixed.sem, 1)
                    for j in range(n):
                        m = slice(2 * j, 2 * j + 2)
                        dve.wait_ge(hpart.sem, hb + j + 1)
                        dve.tensor_tensor(op_lo[:, m, 0:tok], branch[:, m, 0:tok], op_hi[:, m, 0:tok].bitcast(F32),
                                          ALU.subtract).then_inc(lpart.sem, 1)
            mixed.n += n
            hpart.n += n
            lpart.n += n
            used(n)

        def out_stage1(tok):
            n = OUT_CHUNKS
            sets = tok // S
            with nc.Block() as block:
                @block.sync
                def _(sp):
                    load_ahead(sp, n)

                @block.tensor
                def _(pe):
                    for j in range(n):
                        pe_columns(pe, j // 2, j % 2, *model_operand(tok), tok)

                @block.scalar
                def _(act):
                    for j in range(n):
                        round_next(act, j // 2, j % 2)

                @block.vector
                def _(dve):
                    for j in range(n):
                        rest_next(dve, j // 2, j % 2)
                        dve.wait_ge(chunk_done.sem, g0[0] + j + 1)
                        for m in range(2):
                            for w in range(sets):
                                xs = x[:, 2 * j + m, w * S:w * S + S]
                                o = dve.scalar_tensor_tensor(
                                    out=xs, in0=acc(j % 2, S, m * tok + w * S),
                                    scalar=mod[:, 2 * KT + 2 * j + m, w:w + 1], in1=xs, op0=ALU.mult, op1=ALU.add)
                                o.then_inc(acc_free.sem if (m, w) == (1, sets - 1) else gpart.sem, 1)
            gpart.n += n * (2 * sets - 1)
            used(n)

        for layer in range(DEPTH):
            block1(layer)

        rel_bias = sb("rel_bias", [P, 2 * HEADS, 256])
        cmp_bias = sb("cmp_bias", [P, HEADS, 2, NC_CMP])
        table = nc.dram_tensor("bias_by_distance", [2 * HEADS, 511], F32).ap()

        def rel_bias_stage():
            b, lb, rb = step.n, loaded.n, read.n
            with ExitStack() as st:
                rel_sb = sb("rel_sb", [32, 2 * HEADS], stack=st)
                tab_sb = sb("tab_sb", [2 * HEADS, 511], stack=st)
                near = sb("near", [P, 2 * HEADS, 256], stack=st)
                ends = sb("ends", [P, HEADS, 353], stack=st)
                with nc.Block() as block:
                    @block.sync
                    def _(sp):
                        sp.dma_start(rel_sb[:], rel).then_inc(loaded.sem, 16)
                        sp.wait_ge(step.sem, b + 2)
                        sp.dma_start(table, tab_sb[:]).then_inc(loaded.sem, 16)
                        sp.wait_ge(loaded.sem, lb + 32)
                        for h in range(2 * HEADS):
                            sp.dma_start(near[:, h, :], bass.AP(table.tensor, h * 511, [[1, P], [1, 256]])
                                         ).then_inc(loaded.sem, 16)
                        for h in range(HEADS):
                            sp.dma_start(ends[:, h, :], bass.AP(table.tensor, h * 511 + 31, [[1, P], [1, 353]])
                                         ).then_inc(loaded.sem, 16)

                    @block.tensor
                    def _(pe):
                        pe.wait_ge(loaded.sem, lb + 16)
                        pe.matmul(psum[0:2 * HEADS, 0:511], rel_sb[:], const("bucket", 32), start=True, stop=True
                                  ).then_inc(step.sem, 1)
                        pe.wait_ge(loaded.sem, lb + 16 * 26)
                        for half in range(2):
                            if half:
                                pe.wait_ge(read.sem, rb + 1)
                            for k in range(4):
                                h = HEADS * half + 2 * k
                                mm = pe.matmul(psum[:, 512 * k:512 * k + 512], const("flip"), near[:, h:h + 2, :],
                                               start=True, stop=True)
                            mm.then_inc(step.sem, 1)
                        for qt in range(2):
                            at = P * (1 - qt)
                            mm = pe.matmul(psum[:, 2048 + 512 * qt:2048 + 512 * qt + HEADS * NC_CMP], const("flip"),
                                           ends[:, :, at:at + 225:16], start=True, stop=True)
                        mm.then_inc(step.sem, 1)

                    @block.scalar
                    def _(act):
                        act.wait_ge(step.sem, b + 1)
                        act.activation(tab_sb[:], psum[0:2 * HEADS, 0:511], ACT.Copy).then_inc(step.sem, 1)

                    @block.vector
                    def _(dve):
                        for half, mask in enumerate(("causal", "causal_band")):
                            dve.wait_ge(step.sem, b + 3 + half)
                            dve.tensor_tensor(rel_bias[:, HEADS * half:HEADS * (half + 1), :],
                                              psum[:, 0:2048].rearrange("p (h k) -> p h k", h=HEADS),
                                              const(mask).unsqueeze(1).to_broadcast([P, HEADS, 256]), ALU.add
                                              ).then_inc(read.sem, 1)
                        m = const("cmp_mask").rearrange("p (t c) -> p t c", t=2)
                        dve.wait_ge(step.sem, b + 5)
                        for qt in range(2):
                            dve.tensor_tensor(cmp_bias[:, :, qt, :], psum[:, 2048 + 512 * qt:2048 + 512 * qt +
                                                                          HEADS * NC_CMP].rearrange(
                                                  "p (h c) -> p h c", h=HEADS),
                                              m[:, qt, :].unsqueeze(1).to_broadcast([P, HEADS, NC_CMP]), ALU.add
                                              ).then_inc(read.sem, 1)
            step.n += 5
            loaded.n += 16 * 26
            read.n += 4

        def ffn_stage(layer, which):
            with ExitStack() as st:
                h_hi = sb("h_hi", [P, FT, S], F32R, stack=st)
                h_lo = sb("h_lo", [P, FT, S], F32R, stack=st)
                gate = sb("gate", [P, 2, S], stack=st)
                hid = sb("hid", [P, 2, S], stack=st)
                n = FFN_UP_CHUNKS
                rb, hb, lb = read.n, hpart.n, lpart.n
                with nc.Block() as block:
                    @block.sync
                    def _(sp):
                        load_ahead(sp, n)

                    @block.tensor
                    def _(pe):
                        hi, lo = model_operand(S)
                        each_chunk(pe, n, lambda i, s: pe_columns(pe, i, s, hi, lo, S))

                    @block.scalar
                    def _(act):
                        def chunk(i, s):
                            round_next(act, i, s)
                            act.wait_ge(chunk_done.sem, g0[0] + s + 1 + 2 * i)
                            act.wait_ge(acc_free.sem, g0[0] + s - 1 + 2 * i)
                            act.activation(gate[:, s, :], acc(s, S), ACT.Silu).then_inc(read.sem, 1)
                        each_chunk(act, n, chunk)

                    @block.vector
                    def _(dve):
                        def chunk(i, s):
                            rest_next(dve, i, s)
                            dve.wait_ge(read.sem, rb + s + 1 + 2 * i)
                            dve.wait_ge(lpart.sem, lb + s - 1 + 2 * i)
                            dve.scalar_tensor_tensor(out=hid[:, s, :], in0=acc(s, S, S), scalar=0.5,
                                                     in1=gate[:, s, :], op0=ALU.mult, op1=ALU.mult
                                                     ).then_inc(acc_free.sem, 1)
                        each_chunk(dve, n, chunk)

                    @block.gpsimd
                    def _(pool):
                        def chunk(i, s):
                            j = 2 * i + s
                            pool.wait_ge(acc_free.sem, g0[0] + s + 1 + 2 * i)
                            pool.tensor_copy(h_hi[:, j, :], hid[:, s, :]).then_inc(hpart.sem, 1)
                            pool.wait_ge(hpart.sem, hb + s + 1 + 2 * i)
                            pool.tensor_tensor(h_lo[:, j, :], hid[:, s, :], h_hi[:, j, :].bitcast(F32),
                                               ALU.subtract).then_inc(lpart.sem, 1)
                        each_chunk(pool, n, chunk)
                read.n += n
                hpart.n += n
                lpart.n += n
                used(n)
                n = FFN_DOWN_CHUNKS
                with nc.Block() as block:
                    @block.sync
                    def _(sp):
                        load_ahead(sp, n)

                    @block.tensor
                    def _(pe):
                        def chunk(i, s, first, last):
                            pe.wait_ge(split_done.sem, g0[0] + s + 1 + 2 * i)
                            c = (g0[0] + s) % 2
                            for k in range(2):
                                kt = 4 * i + 2 * s + k
                                for m in range(KT):
                                    b = (k * KT + m) * P
                                    o = psum[:, 512 * m:512 * m + S]
                                    pe.matmul(o, w_hi[:, c, b:b + P], h_hi[:, kt, :], start=first and k == 0,
                                              stop=False)
                                    pe.matmul(o, w_hi[:, c, b:b + P], h_lo[:, kt, :], start=False, stop=False)
                                    mm = pe.matmul(o, w_lo[:, c, b:b + P], h_hi[:, kt, :], start=False,
                                                   stop=last and k == 1)
                            mm.then_inc(chunk_done.sem, 1)
                        chunk(0, 0, True, False)
                        chunk(0, 1, False, False)
                        with pe.Fori(1, n // 2) as i:
                            chunk(i, 0, False, False)
                            chunk(i, 1, False, False)
                        chunk(n // 2, 0, False, True)

                    @block.scalar
                    def _(act):
                        each_chunk(act, n, lambda i, s: round_next(act, i, s))

                    @block.vector
                    def _(dve):
                        each_chunk(dve, n, lambda i, s: rest_next(dve, i, s))
                        dve.wait_ge(chunk_done.sem, g0[0] + n)
                        for m in range(4):
                            xs = x[:, 2 * m:2 * m + 2, 0:S]
                            o = dve.scalar_tensor_tensor(
                                out=xs, in0=xs, scalar=DN_ALPHA,
                                in1=psum[:, 1024 * m:1024 * m + 1024].rearrange("p (m t) -> p m t", m=2)[:, :, 0:S],
                                op0=ALU.mult, op1=ALU.add)
                            if m < 3:
                                o.then_inc(gpart.sem, 1)
                            else:
                                o.then_inc(acc_free.sem, n)
                gpart.n += 3
                used(n)
            norm2_stage(layer, which)

        def norm2_stage(layer, which):
            with ExitStack() as st:
                scratch = sb("scratch", [P, KT, S], stack=st)
                layer_norm_stage(x, KT, S, const("ones_model"), ln_eps_col, par(layer, f"ln{which}_g"),
                                 par(layer, f"ln{which}_b"), ACT.Identity, scratch, rs, split=True)

        def mix_stage(layer):
            with ExitStack() as st:
                oa = sb("oa", [P, 4, S], stack=st)
                ob = sb("ob", [P, 4, S], stack=st)
                oc = sb("oc", [P, 4, S], stack=st)
                with ExitStack() as st2:
                    kv_cmp = sb("kv_cmp", [P, 4, S], stack=st2)
                    k_slc = sb("k_slc", [P, 2, S], stack=st2)
                    k_win = sb("k_win", [P, 2, S], stack=st2)
                    v_sw = sb("v_sw", [P, 2, 256], stack=st2)
                    k_b = sb("k_b", [P, 2, S], stack=st2)
                    v_b = sb("v_b", [P, 2, 160], stack=st2)
                    k_c = sb("k_c", [P, 4, S], stack=st2)
                    v_c = sb("v_c", [P, 2, 512], stack=st2)
                    eighth = DH ** -0.5
                    plan = [("c", oa[:, 0:2, :], eighth), ("c", oa[:, 2:4, :], eighth),
                            ("c", kv_cmp[:, 0:2, :], 1.0), ("c", kv_cmp[:, 2:4, :], 1.0),
                            ("c", k_slc[:], 1.0), ("c", k_win[:], 1.0), ("r", v_sw[:], 1.0),
                            ("c", ob[:, 0:2, :], eighth), ("c", ob[:, 2:4, :], eighth), ("c", k_b[:], 1.0),
                            ("r", v_b[:], 1.0), ("c", oc[:, 0:2, :], eighth), ("c", oc[:, 2:4, :], eighth),
                            ("c", k_c[:, 0:2, :], 1.0), ("c", k_c[:, 2:4, :], 1.0), None, None]
                    plan[15:17] = [("r", v_c[:, :, 0:256], 1.0), ("r", v_c[:, :, 256:512], 1.0)]
                    project_stage(plan)
                    probe(f"vb{layer}", v_b[:])
                    kc = sb("kc", [P, 2, NC_CMP], stack=st2)
                    vc = sb("vc", [NC_CMP, 2, DH], stack=st2)
                    with ExitStack() as st3:
                        compress_stage(layer, kv_cmp, kc, vc, st3)
                    probe(f"kc{layer}", kc[:])
                    probe(f"vc{layer}", vc[:])
                    gates = sb("gates", [P, 2, 24], stack=st2)
                    c_row = sb("c_row", [HEADS, S], stack=st2)
                    with ExitStack() as st3:
                        forget_stage(layer, v_b, gates, c_row, st3)
                    probe(f"crow{layer}", c_row[:])
                    bufs = attention_buffers(st2)
                    attend2(layer, oa, ob, oc, k_slc, k_win, v_sw, k_b, v_b, k_c, v_c, kc, vc, gates, c_row, bufs)
                probe(f"oa{layer}", oa[:])
                probe(f"ob{layer}", ob[:])
                probe(f"oc{layer}", oc[:])
                with ExitStack() as st2:
                    y = sb("y", [P, KT, S], stack=st2)
                    sg = sb("sg", [P, 4, S], stack=st2)
                    prod = sb("prod", [P, 4, S], stack=st2)
                    op_hi = sb("op_hi", [P, 4, S], F32R, stack=st2)
                    op_lo = sb("op_lo", [P, 4, S], F32R, stack=st2)
                    for n, branch in enumerate((oa, ob, oc)):
                        split_stage(branch[:], op_hi[:], op_lo[:])
                        merge_stage(y, sg, prod, op_hi, op_lo, S, n == 0,
                                    bias=par(layer, "b_gate")[:, 8 * n:8 * n + 8])
                    split_stage(y[:], x_hi[:, :, 0:S], x_lo[:, :, 0:S])
            n = OUT_CHUNKS
            with nc.Block() as block:
                @block.sync
                def _(sp):
                    load_ahead(sp, n)

                @block.tensor
                def _(pe):
                    for j in range(n):
                        pe_columns(pe, j // 2, j % 2, *model_operand(S), S)

                @block.scalar
                def _(act):
                    for j in range(n):
                        round_next(act, j // 2, j % 2)

                @block.vector
                def _(dve):
                    for j in range(n):
                        rest_next(dve, j // 2, j % 2)
                        dve.wait_ge(chunk_done.sem, g0[0] + j + 1)
                        xs = x[:, 2 * j:2 * j + 2, 0:S]
                        dve.scalar_tensor_tensor(out=xs, in0=xs, scalar=DN_ALPHA,
                                                 in1=acc(j % 2, 2 * S).rearrange("p (m t) -> p m t", m=2),
                                                 op0=ALU.mult, op1=ALU.add).then_inc(acc_free.sem, 1)
            used(n)
            norm2_stage(layer, 2)

        def project_stage(plan):
            n = len(plan)
            with nc.Block() as block:
                @block.sync
                def _(sp):
                    load_ahead(sp, n)

                @block.tensor
                def _(pe):
                    for j, (kind, o, _) in enumerate(plan):
                        if kind == "c":
                            pe_columns(pe, j // 2, j % 2, *model_operand(S), S)
                        else:
                            pe_rows(pe, j // 2, j % 2, S, o.shape[2])

                @block.scalar
                def _(act):
                    for j, (kind, o, scale) in enumerate(plan):
                        round_next(act, j // 2, j % 2)
                        act.wait_ge(chunk_done.sem, g0[0] + j + 1)
                        a = acc(j % 2, 512).rearrange("p (m t) -> p m t", m=2)
                        if kind == "r":
                            a = a[:, :, 0:o.shape[2]]
                        act.activation(o, a, ACT.Copy, scale=scale).then_inc(acc_free.sem, 1)

                @block.vector
                def _(dve):
                    for j in range(n):
                        rest_next(dve, j // 2, j % 2)
            used(n)

        def compress_stage(layer, kv_cmp, kc, vc, st):
            flat = sb("flat", [P, 4, CMP_T // 2, NC_CMP], stack=st)
            f_hi = sb("f_hi", [P, 2, CMP_T // 2, 2 * NC_CMP + 2], F32R, stack=st)
            f_lo = sb("f_lo", [P, 2, CMP_T // 2, 2 * NC_CMP + 2], F32R, stack=st)
            hidden = sb("hidden", [P, 4, 2 * NC_CMP], stack=st)
            W = 2 * NC_CMP
            n = CMP_CHUNKS
            rb, hb, lb, b = read.n, hpart.n, lpart.n, step.n
            with nc.Block() as block:
                @block.sync
                def _(sp):
                    load_ahead(sp, n)

                @block.vector
                def _(dve):
                    for w in range(4):
                        pe_ = par(layer, "pe_k" if w < 2 else "pe_v")
                        for a in range(2):
                            r = slice(a * DH, a * DH + DH)
                            for half in range(2):
                                src = kv_cmp[r, w, :].rearrange("p (b t) -> p t b", t=16)
                                src = src[:, a:16:2, half:half + NC_CMP]
                                tp = slice(8 * half, 8 * half + 8)
                                dve.tensor_tensor(flat[r, w, tp, :], src,
                                                  pe_[r, tp].unsqueeze(2).to_broadcast([DH, 8, NC_CMP]), ALU.add
                                                  ).then_inc(read.sem, 1)
                    for w in range(2):
                        dve.wait_ge(hpart.sem, hb + 2 * (w + 1))
                        for g in range(2):
                            dve.tensor_tensor(f_lo[:, w, :, g * NC_CMP:(g + 1) * NC_CMP], flat[:, 2 * w + g, :, :],
                                              f_hi[:, w, :, g * NC_CMP:(g + 1) * NC_CMP].bitcast(F32), ALU.subtract
                                              ).then_inc(lpart.sem, 1)
                    for j in range(n):
                        rest_next(dve, j // 2, j % 2)
                    dve.wait_ge(step.sem, b + 1)
                    dve.tensor_copy(kc[:], psum[:, 0:W].rearrange("p (g c) -> p g c", g=2)).then_inc(step.sem, 1)
                    dve.wait_ge(step.sem, b + 3)
                    dve.tensor_copy(vc[:], psum[0:NC_CMP, 512:512 + 2 * DH].rearrange("p (g d) -> p g d", g=2)
                                    ).then_inc(step.sem, 1)

                @block.scalar
                def _(act):
                    act.wait_ge(read.sem, rb + 16)
                    for w in range(2):
                        for g in range(2):
                            act.activation(f_hi[:, w, :, g * NC_CMP:(g + 1) * NC_CMP], flat[:, 2 * w + g, :, :],
                                           ACT.Copy).then_inc(hpart.sem, 1)
                    for j in range(n):
                        round_next(act, j // 2, j % 2)
                        act.wait_ge(chunk_done.sem, g0[0] + j + 1)
                        act.activation(hidden[:, j, :], acc(j % 2, W), ACT.Gelu_apprx_tanh).then_inc(acc_free.sem, 1)

                @block.tensor
                def _(pe):
                    pe.wait_ge(lpart.sem, lb + 4)
                    for j in range(n):
                        pe_columns(pe, j // 2, j % 2, lambda k: f_hi[:, j // 2, k, 0:W],
                                   lambda k: f_lo[:, j // 2, k, 0:W], W, kt=CB)
                    pe.wait_ge(acc_free.sem, g0[0] + n)
                    for t in range(2):
                        mm = pe.matmul(psum[:, 0:W], par(layer, "k_w2")[:, t * P:t * P + P], hidden[:, t, :],
                                       start=t == 0, stop=t == 1)
                    mm.then_inc(step.sem, 1)
                    pe.wait_ge(step.sem, b + 2)
                    for g in range(2):
                        for t in range(2):
                            mm = pe.matmul(psum[0:NC_CMP, 512 + g * DH:512 + (g + 1) * DH],
                                           hidden[:, 2 + t, g * NC_CMP:(g + 1) * NC_CMP],
                                           par(layer, "v_w2")[:, t * DH:t * DH + DH], start=t == 0, stop=t == 1)
                    mm.then_inc(step.sem, 1)
            read.n += 16
            hpart.n += 4
            lpart.n += 4
            step.n += 4
            used(n)

        def forget_stage(layer, v_b, gates, c_row, st):
            z = sb("z", [P, 2, 3 * 8], stack=st)
            lf = sb("lf", [P, 2, 8], stack=st)
            b, rb = step.n, read.n
            with nc.Block() as block:
                @block.vector
                def _(dve):
                    zz, neg, ab = z[:, :, 0:8], z[:, :, 8:16], z[:, :, 16:24]
                    dve.tensor_tensor(zz, v_b[:, :, 152:160], par(layer, "b_f").unsqueeze(1).to_broadcast([P, 2, 8]),
                                      ALU.add).then_inc(step.sem, 1)
                    dve.wait_ge(step.sem, b + 1)
                    dve.tensor_scalar(neg, zz, 0.0, None, ALU.min).then_inc(step.sem, 1)
                    dve.wait_ge(step.sem, b + 2)
                    dve.scalar_tensor_tensor(out=ab, in0=neg, scalar=2.0, in1=zz, op0=ALU.mult, op1=ALU.subtract
                                             ).then_inc(step.sem, 1)
                    dve.wait_ge(step.sem, b + 5)
                    dve.tensor_tensor(lf[:], neg, ab, ALU.subtract).then_inc(step.sem, 1)
                    dve.wait_ge(step.sem, b + 7)
                    dve.tensor_copy(c_row[:], psum[0:HEADS, 0:S]).then_inc(step.sem, 1)

                @block.scalar
                def _(act):
                    ab = z[:, :, 16:24]
                    act.activation(gates[:], v_b[:, :, 128:152], ACT.Sigmoid).then_inc(read.sem, 1)
                    act.wait_ge(step.sem, b + 3)
                    act.activation(ab, ab, ACT.Exp).then_inc(step.sem, 1)
                    act.wait_ge(step.sem, b + 4)
                    act.activation(ab, ab, ACT.Ln, bias=1.0).then_inc(step.sem, 1)

                @block.tensor
                def _(pe):
                    pe.wait_ge(step.sem, b + 6)
                    for t in range(2):
                        mm = pe.matmul(psum[0:HEADS, 0:S], lf[:, t, :], const("upto")[:, t * S:t * S + S],
                                       start=t == 0, stop=t == 1)
                    mm.then_inc(step.sem, 1)
            step.n += 8
            read.n += 1

        def attend2(layer, oa, ob, oc, k_slc, k_win, v_sw, k_b, v_b, k_c, v_c, kc, vc, gates, c_row, bufs):
            def causal_bias(tile, qt):
                return tile if qt else tile[:, P:2 * P]

            units = []
            for h in range(HEADS):
                b, g = DH * (h % 2), h // 4
                for qt in range(2):
                    q = oa[b:b + DH, h // 2, qt * P:qt * P + P]
                    nk = P * (qt + 1)
                    common = dict(q=q, plain=0, part=b, qt=qt, pair=h // 2)
                    units.append(dict(common, keys=[(kc[b:b + DH, g, :], 0)], nb=NC_CMP,
                                      bias=cmp_bias[:, h, qt, :], vals=[vc[:, g, :]], first=True, last=False,
                                      gate=gates[:, qt, 3 * h:3 * h + 1], floor=-BIG / 10))
                    for n, k in enumerate((k_slc, k_win)):
                        units.append(dict(common, keys=[(k[b:b + DH, g, 0:nk], 0)], nb=nk,
                                          bias=causal_bias(rel_bias[:, h, :], qt),
                                          vals=[v_sw[:, t, n * P + g * DH:n * P + g * DH + DH] for t in range(qt + 1)],
                                          first=False, last=n == 1, gate=gates[:, qt, 3 * h + n + 1:3 * h + n + 2]))
            attention_stage(units, lambda pair: oa[:, pair, :], bufs)
            units = []
            for h in range(HEADS):
                b, g = DH * (h % 2), h // 4
                for qt in range(2):
                    nk = P * (qt + 1)
                    units.append(dict(q=ob[b:b + DH, h // 2, qt * P:qt * P + P], keys=[(k_b[b:b + DH, g, 0:nk], 0)],
                                      nb=nk, plain=0, part=b, qt=qt, pair=h // 2, first=True, last=True,
                                      bias=causal_bias(rel_bias[:, HEADS + h, :], qt),
                                      vals=[v_b[:, t, g * DH:g * DH + DH] for t in range(qt + 1)],
                                      sink=par(layer, "sinks")[:, h:h + 1]))
            attention_stage(units, lambda pair: ob[:, pair, :], bufs)
            units = []
            for h in range(HEADS):
                b = DH * (h % 2)
                for qt in range(2):
                    nk = P * (qt + 1)
                    extra = [(c_row[:, qt * P:qt * P + P], const("ident", HEADS)[:, h:h + 1].to_broadcast([HEADS, nk])),
                             (const("negid", HEADS)[:, h:h + 1].to_broadcast([HEADS, P]), c_row[:, 0:nk])]
                    units.append(dict(q=oc[b:b + DH, h // 2, qt * P:qt * P + P],
                                      keys=[(k_c[b:b + DH, h // 2, 0:nk], 0)], extra=extra,
                                      nb=nk, plain=0, part=b, qt=qt, pair=h // 2, first=True, last=True,
                                      bias=causal_bias(const("causal"), qt),
                                      vals=[v_c[:, t, h * DH:h * DH + DH] for t in range(qt + 1)]))
            attention_stage(units, lambda pair: oc[:, pair, :], bufs)

        rel_bias_stage()
        split_stage(x[:, :, 0:S], x_hi[:, :, 0:S], x_lo[:, :, 0:S])
        for layer in range(DEPTH):
            ffn_stage(layer, 1)
            probe(f"f{layer}", x[:])
            mix_stage(layer)
            probe(f"m{layer}", x[:])
            ffn_stage(layer, 3)
        with nc.Block() as block:
            @block.sync
            def _(sp):
                sp.dma_start(out, x[:, :, 0:S]).then_inc(stored.sem, 16)
                sp.wait_ge(stored.sem, stored.n + 16)



def _cols(w, cols):
    kt = w.shape[0] // P
    return w[:, cols].reshape(kt, P, -1, P).transpose(1, 2, 0, 3).reshape(P, -1)


def _rows(w, cols):
    a = np.zeros((w.shape[0], 256), w.dtype)
    a[:, :len(cols)] = w[:, cols]
    return a.reshape(-1, P, 256).transpose(1, 0, 2).reshape(P, -1)


def _r(a, n):
    return np.arange(a, a + n)


def _twice(a):
    return np.concatenate([_r(a, DH), _r(a, DH), _r(a + DH, DH), _r(a + DH, DH)])


def weight_stream(v):
    out = np.empty((CHUNKS + 1, P, CB * P), np.float32)
    out[CHUNKS] = 0.0
    n = 0

    def put(a):
        nonlocal n
        out[n] = a
        n += 1

    def span(w, a, m):
        for c in range(a, a + m, 256):
            put(_cols(w, _r(c, 256)))

    def merge(w_gate, at, w_proj):
        for h in range(2):
            span(w_gate, at + 512 * h, 512)
            put(_cols(w_proj, _r(512 * h, 512)))

    for l in range(DEPTH):
        w = v["w_in"][l]
        span(v["w_ada"][l], 0, 3 * D)
        span(w, A_VAL, 1024)
        span(w, NK, 512)
        put(_cols(w, _twice(WK)))
        for c in (0, 256):
            put(_rows(w, _r(NV + c, 256)))
        put(_rows(w, _r(WV, 128)))
        span(w, NQ, 512)
        span(w, WQ, 512)
        for b, (gate, proj) in enumerate(((A_GATE, "w_proj_a"), (N_GATE, "w_proj_b"), (W_GATE, "w_proj_c"))):
            span(w, gate, 512)
            merge(w, MERGE + D * b, v[proj][l])
        span(v["w_o"][l], 0, D)
    for l in range(DEPTH):
        def ffn(name):
            w1, w2 = v[name + "_w1_2"][l], v[name + "_w2_2"][l]
            for t in range(FT):
                put(_cols(w1, np.concatenate([_r(t * P, P), _r(D_FF + t * P, P)])))
            for c in range(FT // 2):
                put(w2[c * 256:(c + 1) * 256].reshape(2, P, KT, P).transpose(1, 0, 2, 3).reshape(P, -1))
        w = v["w_in_2"][l]
        ffn("ffn1")
        span(w, QA, 512)
        for c in (KCMP, VCMP, KSLC, KWIN):
            put(_cols(w, _twice(c)))
        put(_rows(w, np.concatenate([_r(VSLC, 128), _r(VWIN, 128)])))
        span(w, QB, 512)
        put(_cols(w, _twice(KB)))
        put(_rows(w, np.concatenate([_r(VB, 128), _r(GA, 24), _r(FC, 8)])))
        span(w, QC, 512)
        span(w, KC, 512)
        for c in (0, 256):
            put(_rows(w, _r(VC + c, 256)))
        for name in ("cmp_k_w1_2", "cmp_v_w1_2"):
            for t in range(2):
                put(_cols(v[name][l], _r(t * P, P)))
        for b, proj in enumerate(("w_br_a_2", "w_br_b_2", "w_br_c_2")):
            merge(v["w_gate_2"][l], D * b, v[proj][l])
        span(v["w_out_2"][l], 0, D)
        ffn("ffn2")
    assert n == CHUNKS
    return out


def small_parameters(v):
    out = np.zeros((P, DEPTH, N_VEC), np.float32)

    def put(l, name, a):
        s, e = VECS[name]
        out[:, l, s:e] = a

    def by_tile(a):
        return a.reshape(-1, P).T

    def everywhere(a):
        return np.broadcast_to(a, (P, a.shape[0]))

    for l in range(DEPTH):
        put(l, "norm_g", by_tile(v["norm_g"][l]))
        put(l, "b_ada", by_tile(v["b_ada"][l]))
        put(l, "conv_w", v["conv_w"][l].reshape(CONV_K, 4, P).transpose(2, 1, 0).reshape(P, -1))
        for name in ("conv_b", "cln_g", "cln_b"):
            put(l, name, by_tile(v[name][l]))
        for name, src in (("na_q", "na_q_norm"), ("na_k", "na_k_norm"), ("wa_q", "wa_q_norm"), ("wa_k", "wa_k_norm")):
            put(l, name, np.concatenate([v[src][l]] * 2)[:, None])
        put(l, "wa_sink", everywhere(v["wa_sink"][l]))
        for name in ("ln1_g", "ln1_b", "ln2_g", "ln2_b", "ln3_g", "ln3_b", "b_gate"):
            put(l, name, by_tile(v[name + "_2"][l]))
        for name, src in (("pe_k", "cmp_pe_k_2"), ("pe_v", "cmp_pe_v_2")):
            put(l, name, v[src][l].reshape(CMP_T // 2, P).T)
        put(l, "sinks", everywhere(v["swa_sinks_2"][l]))
        put(l, "b_f", everywhere(v["fox_b_f_2"][l]))
        w = v["cmp_k_w2_2"][l].reshape(2, P, DH).transpose(1, 0, 2)
        put(l, "k_w2", np.concatenate([w, w], axis=2).reshape(P, -1))
        put(l, "v_w2", v["cmp_v_w2_2"][l].reshape(2, P, DH).transpose(1, 0, 2).reshape(P, -1))
    return out


def constants():
    out = np.zeros((P, N_CONST), np.float32)

    def put(name, a):
        s, e = CONSTS[name]
        out[:a.shape[0], s:e] = a

    p = np.arange(P)
    put("ident", np.eye(P))
    put("negid", -np.eye(8))
    put("ones_model", np.full((P, P), 1.0 / D))
    put("ones_conv", np.full((P, P), 1.0 / D_CONV))
    put("head_mean", (p[:, None] // DH == p[None] // DH) / float(DH))
    rot = np.zeros((P, P))
    for m in range(P):
        if m % 32 < 16:
            rot[m + 16, m] = -1.0
        else:
            rot[m - 16, m] = 1.0
    put("rotate", rot)
    t = np.arange(S)
    put("upto", np.concatenate([(128 * s + p[:, None] <= t[None]) for s in range(2)], axis=1))
    inv = (np.float32(10000.0) ** (-np.arange(16, dtype=np.float32) / 16)).astype(np.float32)
    pos = np.stack([t // GRID_W, t % GRID_W]).astype(np.float32)
    ang = pos[(p % DH) // 32] * inv[p % 16][:, None]
    put("cos", np.cos(ang.astype(np.float64)))
    put("sin", np.sin(ang.astype(np.float64)))
    k = np.arange(S)
    put("band", np.concatenate([np.where(abs(128 * q + p[:, None] - k[None]) <= 128, 0.0, -BIG) for q in range(2)],
                               axis=1))
    dist = 128 + p[:, None] - k[None]
    put("causal", np.where(dist >= 0, 0.0, -BIG))
    put("causal_band", np.where((dist >= 0) & (dist < 128), 0.0, -BIG))
    ends = 16 * np.arange(NC_CMP) + CMP_T - 1
    put("cmp_mask", np.concatenate([np.where(ends[None] <= 128 * q + p[:, None], 0.0, -BIG) for q in range(2)],
                                   axis=1))
    j, c = p % GRID_W, np.arange(GRID_W)
    start = np.clip(j - 8, 0, GRID_W - 16)
    put("na_mask", np.where((c[None] >= start[:, None]) & (c[None] < start[:, None] + 16), 0.0, -BIG))
    put("flip", np.eye(P)[::-1])
    put("flip_rows", np.kron(np.eye(2), np.eye(GRID_W)[::-1]))
    n = np.maximum(255 - np.arange(511), 0)
    ratio = np.log(np.maximum(n, 1).astype(np.float32) / np.float32(16)) / np.float32(np.log(8.0))
    large = 16 + (ratio * np.float32(16)).astype(np.int32)
    bucket = np.where(n < 16, n, np.minimum(large, 31))
    put("bucket", (np.arange(32)[:, None] == bucket[None]))
    return out


def kernel(**inputs):
    import concourse.bacc as bacc
    from concourse.bass_utils import run_bass_kernel_spmd

    v = {k: np.asarray(a) for k, a in inputs.items()}

    def tiles(a):
        return np.ascontiguousarray(a.reshape(-1, KT, P).transpose(2, 1, 0))

    arrays = {
        "wstream": weight_stream(v),
        "xT": tiles(v["x"][0]),
        "ctxT": tiles(v["ctx"][0]),
        "cT": tiles(np.stack([v["c"][0], v["c_ctx"]])),
        "consts": constants(),
        "vecs": small_parameters(v),
        "rpb": np.ascontiguousarray(v["na_rpb"]).reshape(-1),
        "rel": np.ascontiguousarray(v["rel_bias_2"]),
    }
    nc = bacc.Bacc("TRN2", target_bir_lowering=False, num_devices=1)
    args = {k: nc.dram_tensor(k, a.shape, F32, kind="ExternalInput").ap() for k, a in arrays.items()}
    out = nc.dram_tensor("out", (P, KT, S), F32, kind="ExternalOutput").ap()
    build(nc, out=out, **args)
    r = run_bass_kernel_spmd(nc, [arrays], core_ids=[0])
    return np.ascontiguousarray(r.results[0]["out"].transpose(2, 1, 0)).reshape(1, S, D)
```

```python
from contextlib import ExitStack

import numpy as np

import concourse.bass as bass
from concourse import mybir

F32 = mybir.dt.float32
F32R = mybir.dt.float32r
ALU = mybir.AluOpType
ACT = mybir.ActivationFunctionType
AX = mybir.AxisListType

P = 128
D = 1024
KT = D // P
S = 256
DEPTH = 2
DH = 64
HEADS = 8
GRID_W = 64
CONV_K = 31
PAD = CONV_K // 2
D_CONV = 512
D_FF = 2816
FT = D_FF // P
CB = 16
HALF = CB * P // 2
RING = 4
NC_CMP = 15
CMP_T = 32
BIG = 1e30
DN_ALPHA = (2 * DEPTH) ** 0.25
EPS = 1e-6
LN_EPS = 1e-5

A_VAL, A_GATE_IN, A_GATE, NQ, NK, NV, N_GATE, WQ, WK, WV, W_GATE, MERGE = (
    0, 512, 1024, 1536, 2048, 2560, 3072, 3584, 4096, 4224, 4352, 4864)
QA = 0
KCMP, VCMP, KSLC, VSLC, KWIN, VWIN = (512 + 128 * i for i in range(6))
GA = 1280
QB, KB, VB = 1304, 1816, 1944
QC, KC, VC, FC = 2072, 2584, 3096, 3608

ADA_CHUNKS = 12
GLU_CHUNKS = 4
QKV_CHUNKS = 10
GATE_CHUNKS = 2
MERGE_CHUNKS = 6
OUT_CHUNKS = 4
FFN_UP_CHUNKS = FT
FFN_DOWN_CHUNKS = FT // 2
MIX_CHUNKS = 17
CMP_CHUNKS = 4
CHUNKS1 = ADA_CHUNKS + GLU_CHUNKS + QKV_CHUNKS + 3 * (GATE_CHUNKS + MERGE_CHUNKS) + OUT_CHUNKS
CHUNKS2 = 2 * (FFN_UP_CHUNKS + FFN_DOWN_CHUNKS) + MIX_CHUNKS + CMP_CHUNKS + 3 * MERGE_CHUNKS + OUT_CHUNKS
CHUNKS = DEPTH * (CHUNKS1 + CHUNKS2)

def _columns(sizes):
    at, out = 0, {}
    for name, n in sizes:
        out[name] = (at, at + n)
        at += n
    return out, at


CONSTS, N_CONST = _columns([
    ("ident", 128), ("ones_model", 128), ("ones_conv", 128), ("head_mean", 128),
    ("rotate", 128), ("upto", 2 * 256), ("cos", 256), ("sin", 256), ("band", 2 * 256), ("zeros", 256),
    ("causal", 256), ("causal_band", 256), ("cmp_mask", 2 * NC_CMP), ("na_mask", 64),
    ("flip", 128), ("fold", 2 * NC_CMP), ("flip_rows", 128), ("bucket", 511)])
N_RESIDENT = CONSTS["bucket"][0]
NA_COLS = HEADS * 6 * GRID_W
VECS, N_VEC = _columns([
    ("norm_g", 8), ("b_ada", 24), ("conv_w", 4 * CONV_K), ("conv_b", 4), ("cln_g", 4), ("cln_b", 4),
    ("na_q", 1), ("na_k", 1), ("wa_q", 1), ("wa_k", 1), ("wa_sink", 8),
    ("ln1_g", 8), ("ln1_b", 8), ("ln2_g", 8), ("ln2_b", 8), ("ln3_g", 8), ("ln3_b", 8),
    ("b_gate", 24), ("pe_k", 16), ("pe_v", 16), ("sinks", 8), ("b_f", 8),
    ("k_w2", 2 * 128), ("v_w2", 2 * 64)])


class Count:

    def __init__(self, sem):
        self.sem, self.n = sem, 0


def build(nc, wstream, xT, ctxT, cT, consts, vecs, rpb, rel, out):
    ctx = ExitStack()
    with ctx:
        names = {}

        def sb(name, shape, dt=F32, stack=ctx):
            names[name] = names.get(name, 0) + 1
            if names[name] > 1:
                name = f"{name}_{names[name]}"
            return stack.enter_context(nc.sbuf_tensor(name, shape, dt))

        def count(name):
            return Count(ctx.enter_context(nc.semaphore(name)))

        ring = sb("ring", [P, RING, CB * P])
        w_hi = sb("w_hi", [P, 2, CB * P], F32R)
        w_lo = sb("w_lo", [P, 2, CB * P], F32R)
        x = sb("x", [P, KT, 2 * S])
        x_hi = sb("x_hi", [P, KT, 2 * S], F32R)
        x_lo = sb("x_lo", [P, KT, 2 * S], F32R)
        cst = sb("cst", [P, N_RESIDENT])
        vec = sb("vec", [P, DEPTH, N_VEC])
        psum = ctx.enter_context(nc.psum_tensor("psum", [P, 4096], F32))

        def const(name, rows=P):
            a, b = CONSTS[name]
            return cst[0:rows, a:b]

        def par(layer, name):
            a, b = VECS[name]
            return vec[:, layer, a:b]

        landed = [count("landed_even"), count("landed_odd")]
        hi_done = count("hi_done")
        split_done = count("split_done")
        chunk_done = count("chunk_done")
        acc_free = count("acc_free")
        loaded = count("loaded")
        step = count("step")
        read = count("read")
        mixed = count("mixed")
        gpart = count("gpart")
        hpart = count("hpart")
        lpart = count("lpart")
        conv_step = count("conv_step")
        centred = count("centred")
        squared = count("squared")
        rooted = count("rooted")
        scaled_x = count("scaled_x")
        affine = count("affine")
        upper = count("upper")
        lower = count("lower")
        added = count("added")
        parted = count("parted")
        moved = count("moved")
        placed = [count("placed_even"), count("placed_odd")]
        stored = count("stored")
        g0 = [0]

        def load_ahead(sp, n):
            each_chunk(sp, min(n, CHUNKS + 1 - RING - g0[0]), lambda i, s: load_one(sp, i, s))

        def load_one(sp, i, s):
            c = g0[0] + s + RING
            sp.wait_ge(split_done.sem, 2 * (c - RING + 1) + 4 * i)
            sp.wait_ge(landed[c % 2].sem, 16 * (c // 2 + i))
            sp.dma_start(ring[:, (c + 2 * i) % RING, :], wstream[c + 2 * i]).then_inc(landed[c % 2].sem, 16)

        def round_next(act, i, s):
            c = g0[0] + s + 1
            act.wait_ge(landed[c % 2].sem, 16 * (c // 2 + i + 1))
            if c > 1 or not isinstance(i, int) or i:
                act.wait_ge(chunk_done.sem, c - 1 + 2 * i)
            for half in range(2):
                h = slice(half * HALF, (half + 1) * HALF)
                act.activation(w_hi[:, c % 2, h], ring[:, (c + 2 * i) % RING, h], ACT.Copy
                               ).then_inc(hi_done.sem, 1)

        def rest_next(dve, i, s):
            c = g0[0] + s + 1
            for half in range(2):
                h = slice(half * HALF, (half + 1) * HALF)
                dve.wait_ge(hi_done.sem, 2 * c + 1 + half + 4 * i)
                dve.tensor_tensor(w_lo[:, c % 2, h], ring[:, (c + 2 * i) % RING, h],
                                  w_hi[:, c % 2, h].bitcast(F32), ALU.subtract).then_inc(split_done.sem, 1)

        def each_chunk(eng, n, body):
            pairs = n // 2
            if pairs >= 4:
                lead = 0 if g0[0] else 1
                if lead:
                    body(0, 0)
                    body(0, 1)
                with eng.Fori(lead, pairs) as i:
                    body(i, 0)
                    body(i, 1)
            else:
                for i in range(pairs):
                    body(i, 0)
                    body(i, 1)
            if n % 2:
                body(pairs, 0)

        def columns(t, j, n):
            return t[:, bass.ds(j * n, n)]

        def acc(s, n, at=0):
            a = 2048 * ((g0[0] + s) % 2) + at
            return psum[:, a:a + n]

        def pe_half(pe, i, s, half):
            pe.wait_ge(split_done.sem, 2 * (g0[0] + s) + 1 + half + 4 * i)

        def pe_acc(pe, i, s):
            c = g0[0] + s
            if c > 1 or not isinstance(i, int) or i:
                pe.wait_ge(acc_free.sem, c - 1 + 2 * i)

        def three(pe, o, w_cols, c, hi, lo, first, last):
            pe.matmul(o, w_hi[:, c, w_cols], hi, start=first, stop=False)
            pe.matmul(o, w_hi[:, c, w_cols], lo, start=False, stop=False)
            return pe.matmul(o, w_lo[:, c, w_cols], hi, start=False, stop=last)

        def pe_columns(pe, i, s, hi, lo, tok, kt=KT, before=None):
            pe_acc(pe, i, s)
            c = (g0[0] + s) % 2
            for m in range(CB // kt):
                for k in range(kt):
                    n = m * kt + k
                    if n % (CB // 2) == 0:
                        pe_half(pe, i, s, 2 * n // CB)
                    if before and m == 0:
                        before(k)
                    mm = three(pe, acc(s, tok, m * tok), slice(n * P, n * P + P), c, hi(k), lo(k), k == 0,
                               k == kt - 1)
            mm.then_inc(chunk_done.sem, 1)

        def pe_rows(pe, i, s, tok, cols):
            pe_acc(pe, i, s)
            c = (g0[0] + s) % 2
            for t in range(tok // P):
                for k in range(KT):
                    if t == 0 and k % (KT // 2) == 0:
                        pe_half(pe, i, s, 2 * k // KT)
                    o = acc(s, cols, t * 256)
                    w = slice(k * 256, k * 256 + cols)
                    hi, lo = x_hi[:, k, t * P:t * P + P], x_lo[:, k, t * P:t * P + P]
                    pe.matmul(o, hi, w_hi[:, c, w], start=k == 0, stop=False)
                    pe.matmul(o, lo, w_hi[:, c, w], start=False, stop=False)
                    mm = pe.matmul(o, hi, w_lo[:, c, w], start=False, stop=k == KT - 1)
            mm.then_inc(chunk_done.sem, 1)

        def pe_stacked(pe, i, s, o, both, first, last):
            c = (g0[0] + s) % 2
            for k in range(KT):
                if k % (KT // 2) == 0:
                    pe_half(pe, i, s, 2 * k // KT)
                w = slice(k * 256, k * 256 + 256)
                pe.matmul(o, both(k), w_hi[:, c, w], start=first and k == 0, stop=False)
                mm = pe.matmul(o, both(k), w_lo[:, c, w], start=False, stop=last and k == KT - 1)
            mm.then_inc(chunk_done.sem, 1)

        def model_operand(tok):
            return (lambda k: x_hi[:, k, 0:tok]), (lambda k: x_lo[:, k, 0:tok])

        def used(n):
            g0[0] += n


        def start_stage(c_in):
            with nc.Block() as block:
                @block.sync
                def _(sp):
                    for c in range(RING):
                        if c >= 2:
                            sp.wait_ge(landed[c % 2].sem, 16 * (c // 2))
                        sp.dma_start(ring[:, c, :], wstream[c]).then_inc(landed[c % 2].sem, 16)
                    sp.dma_start(x[:, :, 0:S], xT).then_inc(stored.sem, 16)
                    sp.dma_start(x[:, :, S:2 * S], ctxT).then_inc(stored.sem, 16)

                @block.scalar
                def _(act):
                    act.dma_start(c_in[:], cT).then_inc(loaded.sem, 16)
                    act.dma_start(vec[:], vecs).then_inc(loaded.sem, 16)
                    act.dma_start(cst[:], consts[:, 0:N_RESIDENT]).then_inc(loaded.sem, 16)
                    act.wait_ge(landed[0].sem, 16)
                    for half in range(2):
                        h = slice(half * HALF, (half + 1) * HALF)
                        act.activation(w_hi[:, 0, h], ring[:, 0, h], ACT.Copy).then_inc(hi_done.sem, 1)
                    act.wait_ge(loaded.sem, 48)
                    act.activation(c_in[:], c_in[:], ACT.Silu).then_inc(step.sem, 1)

                @block.vector
                def _(dve):
                    for half in range(2):
                        h = slice(half * HALF, (half + 1) * HALF)
                        dve.wait_ge(hi_done.sem, 1 + half)
                        dve.tensor_tensor(w_lo[:, 0, h], ring[:, 0, h], w_hi[:, 0, h].bitcast(F32),
                                          ALU.subtract).then_inc(split_done.sem, 1)
                    dve.wait_ge(stored.sem, 32)
            step.n, loaded.n, stored.n = 1, 48, 32

        def mod_stage(mod, rows, layer):
            b = step.n
            b_ada = par(layer, "b_ada")
            with nc.Block() as block:
                @block.tensor
                def _(pe):
                    for t in range(3 * KT):
                        mm = pe.transpose(psum[:, 4 * t:4 * t + 4], rows[:, t * P:t * P + P], const("ident")[0:4, 0:4])
                    mm.then_inc(step.sem, 1)

                @block.vector
                def _(dve):
                    v = psum[:, 0:12 * KT].rearrange("p (t c) -> p t c", c=4)
                    dve.wait_ge(step.sem, b + 1)
                    dve.tensor_tensor(mod[:], v[:, :, 0:2], b_ada.unsqueeze(2).to_broadcast([P, 3 * KT, 2]), ALU.add
                                      ).then_inc(step.sem, 1)
                    dve.wait_ge(step.sem, b + 2)
                    dve.tensor_tensor(mod[:], v[:, :, 2:4], mod[:], ALU.add).then_inc(step.sem, 1)
            step.n += 3

        def ada_stage(c_both, rows):
            n = ADA_CHUNKS
            b = step.n
            with nc.Block() as block:
                @block.vector
                def _(dve):
                    dve.memset(c_both[:].bitcast(F32), 0.0).then_inc(step.sem, 1)
                    dve.wait_ge(step.sem, b + 1)
                    dve.tensor_copy(c_both[:, :, 0:2], c_in[:]).then_inc(step.sem, 1)
                    dve.wait_ge(step.sem, b + 2)
                    dve.tensor_tensor(c_both[:, :, 2:4], c_in[:], c_both[:, :, 0:2].bitcast(F32), ALU.subtract
                                      ).then_inc(step.sem, 1)
            step.n += 3
            with nc.Block() as block:
                @block.sync
                def _(sp):
                    load_ahead(sp, n)

                @block.tensor
                def _(pe):
                    def chunk(i, s):
                        pe_acc(pe, i, s)
                        pe_stacked(pe, i, s, acc(s, 256), lambda k: c_both[:, k, :], True, True)
                    each_chunk(pe, n, chunk)

                @block.scalar
                def _(act):
                    def chunk(i, s):
                        round_next(act, i, s)
                        act.wait_ge(chunk_done.sem, g0[0] + s + 1 + 2 * i)
                        act.activation(columns(rows, 2 * i + s, 256), acc(s, 256)[0:4, :], ACT.Copy
                                       ).then_inc(acc_free.sem, 1)
                    each_chunk(act, n, chunk)

                @block.vector
                def _(dve):
                    each_chunk(dve, n, lambda i, s: rest_next(dve, i, s))
            used(n)

        def inverse_root(act, mean_square, rs, eps):
            act.activation(rs, mean_square, ACT.Ln, bias=eps).then_inc(rooted.sem, 1)
            act.wait_ge(rooted.sem, rooted.n + 1)
            act.activation(rs, rs, ACT.Exp, scale=-0.5).then_inc(rooted.sem, 1)
            rooted.n += 2

        def model_norm_stage(mod, scales, layer, tok, scratch, rs):
            b, q0, s0, a0, u0, r0 = step.n, squared.n, scaled_x.n, affine.n, upper.n, rooted.n
            sets = tok // S
            ones = const("ones_model")
            with nc.Block() as block:
                @block.scalar
                def _(act):
                    for k in range(KT):
                        act.activation(scratch[:, k, 0:tok], x[:, k, 0:tok], ACT.Square).then_inc(squared.sem, 1)
                    act.wait_ge(step.sem, b + 2)
                    inverse_root(act, psum[:, 0:tok], rs[:, 0:tok], eps_col)
                    for k in range(KT):
                        act.wait_ge(scaled_x.sem, s0 + k + 1)
                        for w in range(sets):
                            h = scratch[:, k, w * S:w * S + S]
                            act.activation(h, h, ACT.Identity, scale=scales[:, k, w:w + 1],
                                           bias=mod[:, k, w:w + 1]).then_inc(affine.sem, 1)
                        act.wait_ge(affine.sem, a0 + sets * (k + 1))
                        act.activation(x_hi[:, k, 0:tok], scratch[:, k, 0:tok], ACT.Copy).then_inc(upper.sem, 1)

                @block.tensor
                def _(pe):
                    for k in range(KT):
                        pe.wait_ge(squared.sem, q0 + k + 1)
                        mm = pe.matmul(psum[:, 0:tok], ones, scratch[:, k, 0:tok], start=k == 0, stop=k == KT - 1)
                    mm.then_inc(step.sem, 1)

                @block.vector
                def _(dve):
                    dve.scalar_tensor_tensor(out=scales[:], in0=mod[:, KT:2 * KT, :], scalar=1.0,
                                             in1=par(layer, "norm_g").unsqueeze(2).to_broadcast([P, KT, 2]),
                                             op0=ALU.add, op1=ALU.mult).then_inc(step.sem, 1)
                    dve.wait_ge(rooted.sem, r0 + 2)
                    for k in range(KT + 2):
                        if k < KT:
                            dve.tensor_tensor(scratch[:, k, 0:tok], x[:, k, 0:tok], rs[:, 0:tok], ALU.mult
                                              ).then_inc(scaled_x.sem, 1)
                        j = k - 2
                        if j >= 0:
                            dve.wait_ge(upper.sem, u0 + j + 1)
                            dve.tensor_tensor(x_lo[:, j, 0:tok], scratch[:, j, 0:tok],
                                              x_hi[:, j, 0:tok].bitcast(F32), ALU.subtract).then_inc(lower.sem, 1)
            step.n += 2
            squared.n += KT
            scaled_x.n += KT
            affine.n += sets * KT
            upper.n += KT
            lower.n += KT

        def split_stage(src, hi, lo):
            b = step.n
            with nc.Block() as block:
                @block.scalar
                def _(act):
                    act.activation(hi, src, ACT.Copy).then_inc(step.sem, 1)

                @block.vector
                def _(dve):
                    dve.wait_ge(step.sem, b + 1)
                    dve.tensor_tensor(lo, src, hi.bitcast(F32), ALU.subtract).then_inc(step.sem, 1)
            step.n += 2

        def layer_norm_stage(src, nt, tok, ones, eps, gains, biases, func, scratch, rs, split=False):
            b, c0, q0, r0, s0, a0, u0 = step.n, centred.n, squared.n, rooted.n, scaled_x.n, affine.n, upper.n
            with nc.Block() as block:
                @block.tensor
                def _(pe):
                    for k in range(nt):
                        mm = pe.matmul(psum[:, 0:tok], ones, src[:, k, 0:tok], start=k == 0, stop=k == nt - 1)
                    mm.then_inc(step.sem, 1)
                    for k in range(nt):
                        pe.wait_ge(squared.sem, q0 + k + 1)
                        mm = pe.matmul(psum[:, 512:512 + tok], ones, scratch[:, k, 0:tok],
                                       start=k == 0, stop=k == nt - 1)
                    mm.then_inc(step.sem, 1)

                @block.vector
                def _(dve):
                    dve.wait_ge(step.sem, b + 1)
                    for k in range(nt):
                        dve.tensor_tensor(src[:, k, 0:tok], src[:, k, 0:tok], psum[:, 0:tok],
                                          ALU.subtract).then_inc(centred.sem, 1)
                    dve.wait_ge(rooted.sem, r0 + 2)
                    for k in range(nt + 2):
                        if k < nt:
                            dve.tensor_tensor(src[:, k, 0:tok], src[:, k, 0:tok], rs[:, 0:tok], ALU.mult
                                              ).then_inc(scaled_x.sem, 1)
                        j = k - 2
                        if split and j >= 0:
                            dve.wait_ge(upper.sem, u0 + j + 1)
                            dve.tensor_tensor(x_lo[:, j, 0:tok], src[:, j, 0:tok],
                                              x_hi[:, j, 0:tok].bitcast(F32), ALU.subtract).then_inc(lower.sem, 1)

                @block.scalar
                def _(act):
                    for k in range(nt):
                        act.wait_ge(centred.sem, c0 + k + 1)
                        act.activation(scratch[:, k, 0:tok], src[:, k, 0:tok], ACT.Square).then_inc(squared.sem, 1)
                    act.wait_ge(step.sem, b + 2)
                    inverse_root(act, psum[:, 512:512 + tok], rs[:, 0:tok], eps)
                    for k in range(nt):
                        act.wait_ge(scaled_x.sem, s0 + k + 1)
                        act.activation(src[:, k, 0:tok], src[:, k, 0:tok], func, scale=gains[:, k:k + 1],
                                       bias=biases[:, k:k + 1]).then_inc(affine.sem, 1)
                        if split:
                            act.wait_ge(affine.sem, a0 + k + 1)
                            act.activation(x_hi[:, k, 0:tok], src[:, k, 0:tok], ACT.Copy).then_inc(upper.sem, 1)
            step.n += 2
            for c in (centred, squared, scaled_x, affine):
                c.n += nt
            if split:
                upper.n += nt
                lower.n += nt

        scored = count("scored")
        sunk = count("sunk")
        biased = count("biased")
        shift = count("shift")
        exped = count("exped")
        small = count("small")
        scaled = count("scaled")
        turned = count("turned")
        turned_sb = count("turned_sb")
        summed = count("summed")
        taken = count("taken")

        def attention_stage(units, dst, T, bring_back=None):
            U = len(units)
            base = {c: c.n for c in (scored, biased, sunk, shift, exped, small, scaled, turned, turned_sb,
                                     summed, taken)}
            nsunk = np.cumsum([1 if "sink" in u else 0 for u in units]).tolist()
            nsmall = np.cumsum([1 + ("floor" in u) for u in units]).tolist()
            pairs = [u["pair"] for u in units]
            ends = [n for n in range(U) if n == U - 1 or pairs[n + 1] != pairs[n]]

            def after(c, counts, u):
                return base[c] + (counts[u] if u >= 0 else 0)

            def s_ps(u, a, n):
                return psum[:, (u % 3) * 512 + a:(u % 3) * 512 + a + n]

            def t_ps(u, n):
                return psum[:, 1536 + (u % 2) * 512:1536 + (u % 2) * 512 + n]

            def o_ps(pair):
                return psum[:, 2560 + (pair % 2) * 512:2560 + (pair % 2) * 512 + 2 * P]

            def blocks(u):
                n = u["n"]
                return [(a, min(P, n - a)) for a in range(0, n, P)]

            with ExitStack() as st, nc.Block() as block:
                prob, probT, mx, den, fac, neg = T

                @block.sync
                def _(sp):
                    if bring_back:
                        sp.dma_start(x_hi[:, :, 0:bring_back].bitcast(F32), kept_hi[:, :, 0:bring_back]).then_inc(stored.sem, 16)
                        sp.dma_start(x_lo[:, :, 0:bring_back].bitcast(F32), kept_lo[:, :, 0:bring_back]).then_inc(stored.sem, 16)
                        sp.wait_ge(stored.sem, stored.n + 32)

                @block.tensor
                def _(pe):
                    for t in range(U + 4):
                        if t < U:
                            u = units[t]
                            if t >= 3:
                                pe.wait_ge(biased.sem, base[biased] + t - 2)
                            o = s_ps(t, 0, u["keys"][0].shape[1])
                            pe.matmul(o, u["q"], u["keys"][0], start=True, stop=False)
                            mm = pe.matmul(o, u["q"], u["keys"][1], start=False, stop=True)
                            mm.then_inc(scored.sem, 1)
                        v = t - 3
                        if 0 <= v < U:
                            pe.wait_ge(scaled.sem, base[scaled] + v + 1)
                            if v >= 2:
                                pe.wait_ge(turned_sb.sem, base[turned_sb] + v - 1)
                            for a, w in blocks(units[v]):
                                mm = pe.transpose(psum[0:w, 1536 + (v % 2) * 512 + a:1536 + (v % 2) * 512 + a + P],
                                                  prob[:, v % 4, a:a + w], const("ident"))
                            mm.then_inc(turned.sem, 1)
                        v = t - 4
                        if 0 <= v < U:
                            u = units[v]
                            pe.wait_ge(turned_sb.sem, base[turned_sb] + v + 1)
                            if u["pair"] >= 2:
                                pe.wait_ge(taken.sem, base[taken] + u["pair"] - 1)
                            part, qt = u["part"], u["qt"]
                            o = o_ps(u["pair"])[part:part + DH, qt * P:qt * P + P]
                            bl = blocks(u)
                            for n, (a, w) in enumerate(bl):
                                mm = pe.matmul(o, u["vals"][n], probT[0:w, v % 2, a:a + P],
                                               start=u["first"] and n == 0, stop=u["last"] and n == len(bl) - 1)
                            mm.then_inc(summed.sem, 1)

                @block.vector
                def _(dve):
                    for t in range(U + 4):
                        v = t - 1
                        if t < U:
                            u = units[t]
                            n = u["n"]
                            if t >= 4:
                                dve.wait_ge(turned.sem, base[turned] + t - 3)
                            if "sink" in u:
                                dve.tensor_copy(prob[:, t % 4, n:n + 1], u["sink"]).then_inc(sunk.sem, 1)
                            o, s_in = prob[:, t % 4, 0:n], s_ps(t, 0, n)
                            if n > 256:
                                o = o.rearrange("p (a k) -> p a k", k=256)
                                s_in = s_in.rearrange("p (a k) -> p a k", k=256)
                            dve.wait_ge(scored.sem, base[scored] + t + 1)
                            dve.tensor_tensor_reduce(o, s_in, u["bias"], 1.0, -3e38, ALU.add, ALU.max,
                                                     mx[:, t % 4, 0:1]).then_inc(biased.sem, 1)
                        if 0 <= v < U:
                            k = after(small, nsmall, v - 1)
                            dve.wait_ge(exped.sem, base[exped] + v + 1)
                            src = den[:, v % 3, 0:1]
                            if "floor" in units[v]:
                                dve.tensor_scalar(den[:, v % 3, 1:2], src, 1e-30, None, ALU.max).then_inc(small.sem, 1)
                                k += 1
                                dve.wait_ge(small.sem, k)
                                src = den[:, v % 3, 1:2]
                            dve.reciprocal(fac[:, v % 3, 0:1], src).then_inc(small.sem, 1)
                        if t < U:
                            dve.wait_ge(biased.sem, base[biased] + t + 1)
                            dve.tensor_scalar(neg[:, t % 4, 0:1], mx[:, t % 4, 0:1],
                                              u["sink"] if "sink" in u else u.get("floor", -3e38), -1.0,
                                              ALU.max, ALU.mult).then_inc(shift.sem, 1)
                        if 0 <= v < U:
                            u = units[v]
                            n = u["n"]
                            dve.wait_ge(small.sem, k + 1)
                            dve.tensor_scalar(prob[:, v % 4, 0:n], prob[:, v % 4, 0:n], fac[:, v % 3, 0:1],
                                              u.get("gate"), ALU.mult, ALU.mult if "gate" in u else ALU.bypass
                                              ).then_inc(scaled.sem, 1)
                        v = t - 4
                        if v in ends:
                            pair = units[v]["pair"]
                            dve.wait_ge(summed.sem, base[summed] + v + 1)
                            dve.tensor_copy(dst(pair), o_ps(pair)[:, 0:dst(pair).shape[1]]).then_inc(taken.sem, 1)

                @block.scalar
                def _(act):
                    for t in range(U + 4):
                        if t < U:
                            u = units[t]
                            n = u["n"] + ("sink" in u)
                            act.wait_ge(shift.sem, base[shift] + t + 1)
                            if "sink" in u:
                                act.wait_ge(sunk.sem, after(sunk, nsunk, t))
                            if t >= 3:
                                act.wait_ge(small.sem, after(small, nsmall, t - 3))
                            act.activation(prob[:, t % 4, 0:n], prob[:, t % 4, 0:n], ACT.Exp,
                                           bias=neg[:, t % 4, 0:1], accum_out=den[:, t % 3, 0:1]
                                           ).then_inc(exped.sem, 1)
                        v = t - 3
                        if 0 <= v < U:
                            act.wait_ge(turned.sem, base[turned] + v + 1)
                            if v >= 2:
                                act.wait_ge(summed.sem, base[summed] + v - 1)
                            bl = blocks(units[v])
                            w = bl[-1][1]
                            n = len(bl) * P
                            act.activation(probT[0:w, v % 2, 0:n], psum[0:w, 1536 + (v % 2) * 512:
                                                                        1536 + (v % 2) * 512 + n],
                                           ACT.Copy).then_inc(turned_sb.sem, 1)

            for c in (scored, biased, shift, exped, scaled, turned, turned_sb, summed):
                c.n += U
            stored.n += 32 if bring_back else 0
            sunk.n += nsunk[-1]
            small.n += nsmall[-1]
            taken.n += len(ends)

        def attention_buffers(st, keys):
            return (sb("prob", [P, 4, keys + 1], stack=st), sb("probT", [P, 2, keys], stack=st),
                    sb("mx", [P, 4, 1], stack=st), sb("den", [P, 3, 2], stack=st), sb("fac", [P, 3, 1], stack=st),
                    sb("neg", [P, 4, 1], stack=st))

        def merge_stage(branches, y, sg, prod, op_hi, op_lo, tok, gated, bias, take_out):
            seq = []
            for b in range(3):
                if gated:
                    seq += [("gate", b, 0), ("gate", b, 1)]
                for h in range(2):
                    seq += [("merge", b, 2 * h), ("merge", b, 2 * h + 1), ("proj", b, h)]
            seq += [("out", 0, i) for i in range(OUT_CHUNKS)]
            n = len(seq)
            u0, l0, m0, a0, w0 = upper.n, lower.n, mixed.n, added.n, gpart.n
            per_branch = 2

            def chunk(kind, b, i):
                return g0[0] + seq.index((kind, b, i))

            def adds(b, h, piece):
                return a0 + 4 * (b - 1) + 2 * h + piece + 1

            with nc.Block() as block:
                @block.sync
                def _(sp):
                    load_ahead(sp, n)

                @block.tensor
                def _(pe):
                    for j, (kind, b, i) in enumerate(seq):
                        if kind == "proj":
                            def parts_made(k):
                                if k % 2 == 0:
                                    pe.wait_ge(lower.sem, l0 + per_branch * b + k // 2 + 1)
                            pe_columns(pe, j // 2, j % 2, lambda k: op_hi[:, k, 0:tok],
                                       lambda k: op_lo[:, k, 0:tok], tok, kt=4, before=parts_made)
                        elif kind == "out":
                            def y_made(k):
                                if k in (0, 4, 6):
                                    pe.wait_ge(lower.sem, l0 + 3 * per_branch + (0, 4, 6).index(k) + 1)
                            pe_columns(pe, j // 2, j % 2, *model_operand(tok), tok, before=None if i else y_made)
                        else:
                            pe_columns(pe, j // 2, j % 2, *model_operand(tok), tok)

                @block.scalar
                def _(act):
                    for j, (kind, b, i) in enumerate(seq):
                        round_next(act, j // 2, j % 2)
                        if (kind, i) == ("merge", 0):
                            if b:
                                act.wait_ge(chunk_done.sem, chunk("proj", b - 1, 1) + 1)
                            for h in range(2):
                                m = slice(2 * h, 2 * h + 2)
                                if gated:
                                    act.wait_ge(mixed.sem, m0 + 2 * b + h + 1)
                                act.activation(op_hi[:, m, 0:tok], branches[b][:, m, 0:tok], ACT.Copy
                                               ).then_inc(upper.sem, 1)
                        if kind in ("gate", "merge"):
                            act.wait_ge(chunk_done.sem, g0[0] + j + 1)
                            if j:
                                act.wait_ge(acc_free.sem, g0[0] + j)
                        if kind == "gate":
                            if b >= 2:
                                act.wait_ge(added.sem, adds(b - 1, 1, 1))
                            act.activation(prod[:, 2 * i:2 * i + 2, 0:tok],
                                           acc(j % 2, 2 * tok).rearrange("p (m t) -> p m t", m=2), ACT.Silu
                                           ).then_inc(acc_free.sem, 1)
                        elif kind == "merge" and bias is None:
                            act.activation(sg[:, 2 * (i % 2):2 * (i % 2) + 2, 0:tok],
                                           acc(j % 2, 2 * tok).rearrange("p (m t) -> p m t", m=2),
                                           ACT.Sigmoid).then_inc(acc_free.sem, 1)
                        elif kind == "merge":
                            for m in range(2):
                                act.activation(sg[:, 2 * (i % 2) + m, 0:tok], acc(j % 2, tok, m * tok),
                                               ACT.Sigmoid, bias=bias[:, 8 * b + 2 * i + m:8 * b + 2 * i + m + 1]
                                               ).then_inc((gpart, acc_free)[m].sem, 1)
                        elif (kind, b, i) == ("proj", 2, 1):
                            act.wait_ge(chunk_done.sem, g0[0] + j)
                            for part, m in enumerate((slice(0, 4), slice(4, 6), slice(6, 8))):
                                act.wait_ge(added.sem, adds(2, 1 if part else 0, max(part - 1, 0) if part else 1))
                                act.activation(x_hi[:, m, 0:tok], y[:, m, 0:tok], ACT.Copy).then_inc(upper.sem, 1)

                @block.vector
                def _(dve):
                    def y_lower(part, m):
                        dve.wait_ge(upper.sem, u0 + 3 * per_branch + part + 1)
                        dve.tensor_tensor(x_lo[:, m, 0:tok], y[:, m, 0:tok], x_hi[:, m, 0:tok].bitcast(F32),
                                          ALU.subtract).then_inc(lower.sem, 1)

                    inner = 0
                    for j, (kind, b, i) in enumerate(seq):
                        rest_next(dve, j // 2, j % 2)
                        if kind == "gate":
                            m = slice(2 * i, 2 * i + 2)
                            dve.wait_ge(acc_free.sem, g0[0] + j + 1)
                            dve.tensor_tensor(branches[b][:, m, 0:tok], branches[b][:, m, 0:tok], prod[:, m, 0:tok],
                                              ALU.mult).then_inc(mixed.sem, 1)
                        if (kind, i) == ("merge", 0):
                            for h in range(2):
                                m = slice(2 * h, 2 * h + 2)
                                dve.wait_ge(upper.sem, u0 + per_branch * b + h + 1)
                                dve.tensor_tensor(op_lo[:, m, 0:tok], branches[b][:, m, 0:tok],
                                                  op_hi[:, m, 0:tok].bitcast(F32), ALU.subtract
                                                  ).then_inc(lower.sem, 1)
                        if kind == "proj":
                            if (b, i) == (2, 1):
                                y_lower(0, slice(0, 4))
                            dve.wait_ge(acc_free.sem, g0[0] + j)
                            dve.wait_ge(chunk_done.sem, g0[0] + j + 1)
                            if gated and b:
                                dve.wait_ge(mixed.sem, m0 + 2 * b + 2)
                            for piece in range(2):
                                m = slice(2 * piece, 2 * piece + 2)
                                a = acc(j % 2, 2 * tok, 2 * tok * piece).rearrange("p (m t) -> p m t", m=2)
                                dest = y[:, 4 * i + 2 * piece:4 * i + 2 * piece + 2, 0:tok]
                                if b and (b, i) != (1, 0):
                                    dve.wait_ge(added.sem, adds(b, i, piece) - 2)
                                dve.tensor_tensor(prod[:, m, 0:tok] if b else dest, a, sg[:, m, 0:tok], ALU.mult
                                                  ).then_inc((parted, acc_free)[piece].sem, 1)
                                inner += 1 - piece
                            for piece in range(2 if b else 0):
                                m = slice(2 * piece, 2 * piece + 2)
                                dest = y[:, 4 * i + 2 * piece:4 * i + 2 * piece + 2, 0:tok]
                                if piece:
                                    dve.wait_ge(acc_free.sem, g0[0] + j + 1)
                                else:
                                    dve.wait_ge(parted.sem, parted.n + inner)
                                dve.tensor_tensor(dest, dest, prod[:, m, 0:tok], ALU.add).then_inc(added.sem, 1)
                            if (b, i) == (2, 1):
                                y_lower(1, slice(4, 6))
                                y_lower(2, slice(6, 8))
                        if kind == "out":
                            take_out(dve, j, i)
            parted.n += 6
            added.n += 8
            mixed.n += 6 if gated else 0
            upper.n += 9
            lower.n += 9
            gpart.n += 0 if bias is None else 12
            used(n)

        kept_hi = nc.dram_tensor("kept_hi", [P, KT, 2 * S], F32).ap()
        kept_lo = nc.dram_tensor("kept_lo", [P, KT, 2 * S], F32).ap()
        consts_small = sb("consts_small", [P, 2])
        eps_col, ln_eps_col = consts_small[:, 0:1], consts_small[:, 1:2]
        c_in = sb("c_in", [P, KT, 2])
        mod = sb("mod", [P, 3 * KT, 2])
        scales = sb("scales", [P, KT, 2])
        rs = sb("rs", [P, 2 * S])
        with nc.Block() as block:
            @block.vector
            def _(dve):
                dve.memset(eps_col, EPS)
                dve.memset(ln_eps_col, LN_EPS)
        start_stage(c_in)

        def block1(layer):
            tok = 2 * S if layer == 0 else S
            sets = tok // S
            with ExitStack() as st:
                rows = sb("rows", [4, 3 * D], stack=st)
                c_both = sb("c_both", [P, KT, P], F32R, stack=st)
                ada_stage(c_both, rows)
                mod_stage(mod, rows, layer)
            with ExitStack() as st:
                scratch = sb("scratch", [P, KT, 2 * S], stack=st)
                model_norm_stage(mod, scales, layer, 2 * S, scratch, rs)
            with ExitStack() as st:
                conv_out = sb("conv_out", [P, 4, 2 * S], stack=st)
                nq = sb("nq", [P, 4, 2 * S], stack=st)
                wq = sb("wq", [P, 4, 2 * S], stack=st)
                with ExitStack() as st2:
                    nv = sb("nv", [P, 4, 512], stack=st2)
                    wk = sb("wk", [P, 2, 2 * S], stack=st2)
                    wv = sb("wv", [P, 4, 128], stack=st2)
                    with ExitStack() as st4:
                        nk = sb("nk", [P, 4, 2 * S], stack=st4)
                        with ExitStack() as st3:
                            cpad = sb("cpad", [P, 4, 2, S + 2 * PAD], stack=st3)
                            glu_gate = sb("glu_gate", [P, 4, 2 * S], stack=st3)
                            glu_stage(cpad, glu_gate, tok)
                            qkv_stage(layer, tok, cpad, conv_out, nq, nk, nv, wq, wk, wv)
                        with ExitStack() as st3:
                            scratch = sb("scratch", [P, 4, 2 * S], stack=st3)
                            layer_norm_stage(conv_out, 4, tok, const("ones_conv"), eps_col, par(layer, "cln_g"),
                                             par(layer, "cln_b"), ACT.Silu, scratch, rs)
                        with ExitStack() as st3:
                            qk_norm_stage(layer, tok, nq, nk, wq, wk, st3)
                        with ExitStack() as st3:
                            parts = [sb("kpart", [P, 4, 2 * S], F32R, stack=st3)[:] for _ in range(2)]
                            stack_stage([(nk[:], "k", (x_hi[:], x_lo[:]), parts)])
                    attend1(layer, tok, nq, nv, wq, wk, wv)
                with ExitStack() as st2:
                    y = sb("y", [P, KT, 2 * S], stack=st2)
                    sg = sb("sg", [P, 4, 2 * S], stack=st2)
                    prod = sb("prod", [P, 4, 2 * S], stack=st2)
                    op_hi = sb("op_hi", [P, 4, 2 * S], F32R, stack=st2)
                    op_lo = sb("op_lo", [P, 4, 2 * S], F32R, stack=st2)

                    def take_out(dve, j, i):
                        dve.wait_ge(chunk_done.sem, g0[0] + j + 1)
                        for m in range(2):
                            for w in range(sets):
                                xs = x[:, 2 * i + m, w * S:w * S + S]
                                dve.scalar_tensor_tensor(
                                    out=xs, in0=acc(j % 2, S, m * tok + w * S),
                                    scalar=mod[:, 2 * KT + 2 * i + m, w:w + 1], in1=xs, op0=ALU.mult, op1=ALU.add
                                ).then_inc((acc_free if (m, w) == (1, sets - 1) else parted).sem, 1)
                    merge_stage((conv_out, nq, wq), y, sg, prod, op_hi, op_lo, tok, True, None, take_out)
                    parted.n += OUT_CHUNKS * (2 * sets - 1)

        def glu_stage(cpad, glu_gate, tok):
            sets = tok // S
            n = GLU_CHUNKS
            rb = read.n
            with nc.Block() as block:
                @block.sync
                def _(sp):
                    load_ahead(sp, n)

                @block.tensor
                def _(pe):
                    hi, lo = model_operand(tok)
                    for j in range(n):
                        pe_columns(pe, j // 2, j % 2, hi, lo, tok)

                @block.scalar
                def _(act):
                    for j in range(n):
                        round_next(act, j // 2, j % 2)
                        act.wait_ge(chunk_done.sem, g0[0] + j + 1)
                        a = acc(j % 2, 2 * tok)
                        if j < 2:
                            for w in range(sets):
                                o = act.activation(
                                    cpad[:, 2 * j:2 * j + 2, w, PAD:PAD + S],
                                    a.rearrange("p (m t) -> p m t", m=2)[:, :, w * S:w * S + S], ACT.Copy)
                                o.then_inc(acc_free.sem if w == sets - 1 else gpart.sem, 1)
                        else:
                            act.activation(glu_gate[:, 2 * j - 4:2 * j - 2, 0:tok],
                                           a.rearrange("p (m t) -> p m t", m=2), ACT.Sigmoid
                                           ).then_inc(acc_free.sem, 1)

                @block.gpsimd
                def _(pool):
                    pool.memset(cpad[:, :, :, 0:PAD], 0.0)
                    pool.memset(cpad[:, :, :, PAD + S:], 0.0)

                @block.vector
                def _(dve):
                    for j in range(n):
                        rest_next(dve, j // 2, j % 2)
                        if j >= 2:
                            m = slice(2 * j - 4, 2 * j - 2)
                            dve.wait_ge(acc_free.sem, g0[0] + j + 1)
                            for w in range(sets):
                                v = cpad[:, m, w, PAD:PAD + S]
                                dve.tensor_tensor(v, v, glu_gate[:, m, w * S:w * S + S], ALU.mult
                                                  ).then_inc(read.sem, 1)
            read.n += 2 * sets
            if sets == 2:
                gpart.n += 2
            used(n)

        def qkv_stage(layer, tok, cpad, conv_out, nq, nk, nv, wq, wk, wv):
            sets = tok // S
            plan = [("c", 2 * S, nk[:, 0:2, :]), ("c", 2 * S, nk[:, 2:4, :]), ("c", 2 * S, wk[:, :, :]),
                    ("r", 2 * S, nv[:, :, 0:256]), ("r", 2 * S, nv[:, :, 256:512]), ("r", 2 * S, wv[:, :, :]),
                    ("c", tok, nq[:, 0:2, 0:tok]), ("c", tok, nq[:, 2:4, 0:tok]),
                    ("c", tok, wq[:, 0:2, 0:tok]), ("c", tok, wq[:, 2:4, 0:tok])]
            n = QKV_CHUNKS
            taps = [(ct, k) for k in range(CONV_K) for ct in range(4)]
            cuts = [round(len(taps) * j / n) for j in range(n + 1)]
            cb = conv_step.n
            w_conv = par(layer, "conv_w")
            b_conv = par(layer, "conv_b")
            with nc.Block() as block:
                @block.sync
                def _(sp):
                    load_ahead(sp, n)

                @block.tensor
                def _(pe):
                    for j, (kind, t, o) in enumerate(plan):
                        if kind == "c":
                            pe_columns(pe, j // 2, j % 2, *model_operand(t), t)
                        else:
                            pe_rows(pe, j // 2, j % 2, t, min(256, o.shape[2]))

                @block.scalar
                def _(act):
                    for j, (kind, t, o) in enumerate(plan):
                        round_next(act, j // 2, j % 2)
                        act.wait_ge(chunk_done.sem, g0[0] + j + 1)
                        if kind == "c":
                            a = acc(j % 2, 2 * t).rearrange("p (m t) -> p m t", m=2)
                        else:
                            a = acc(j % 2, 1024).rearrange("p (t c) -> p t c", t=4)[:, :, 0:o.shape[2]]
                        act.activation(o, a, ACT.Copy).then_inc(acc_free.sem, 1)

                @block.vector
                def _(dve):
                    for j in range(n):
                        rest_next(dve, j // 2, j % 2)
                        for c in range(cuts[j], cuts[j + 1]):
                            ct, k = taps[c]
                            src = cpad[:, ct, 0:sets, k:k + S]
                            o = conv_out[:, ct, 0:tok].rearrange("p (w t) -> p w t", w=sets)
                            wc = w_conv[:, ct * CONV_K + k:ct * CONV_K + k + 1]
                            if k == 0:
                                dve.tensor_scalar(o, src, wc, b_conv[:, ct:ct + 1], ALU.mult, ALU.add
                                                  ).then_inc(conv_step.sem, 1)
                            else:
                                dve.wait_ge(conv_step.sem, cb + c - 3)
                                dve.scalar_tensor_tensor(out=o, in0=src, scalar=wc, in1=o, op0=ALU.mult,
                                                         op1=ALU.add).then_inc(conv_step.sem, 1)
            conv_step.n += len(taps)
            used(n)

        def qk_norm_stage(layer, tok, nq, nk, wq, wk, st):
            gains = sb("gains", [P, 4], stack=st)
            tmp = sb("tmp", [P, 2, 4 * 2 * S], stack=st)
            items = [(nq, 4, tok, 0), (nk, 4, 2 * S, 1), (wq, 4, tok, 2), (wk, 2, 2 * S, 3)]
            b, q0, rb, vb, r0, gb = step.n, squared.n, read.n, mixed.n, rooted.n, gpart.n
            with nc.Block() as block:
                @block.sync
                def _(sp):
                    sp.dma_start(kept_hi[:, :, 0:tok], x_hi[:, :, 0:tok].bitcast(F32)).then_inc(stored.sem, 16)
                    sp.dma_start(kept_lo[:, :, 0:tok], x_lo[:, :, 0:tok].bitcast(F32)).then_inc(stored.sem, 16)
                    sp.wait_ge(stored.sem, stored.n + 32)
                @block.scalar
                def _(act):
                    def squares(e):
                        t, nt, tk, g = items[e]
                        if e >= 2:
                            act.wait_ge(mixed.sem, vb + e - 1)
                        act.activation(tmp[:, e % 2, 0:nt * tk].rearrange("p (m t) -> p m t", m=nt),
                                       t[:, 0:nt, 0:tk], ACT.Square).then_inc(squared.sem, 1)

                    squares(0)
                    squares(1)
                    for e, (t, nt, tk, g) in enumerate(items):
                        act.wait_ge(step.sem, b + e + 1)
                        inverse_root(act, psum[:, 2048 * (e % 2):2048 * (e % 2) + nt * tk],
                                     tmp[:, e % 2, 0:nt * tk], eps_col)
                        if e + 2 < len(items):
                            squares(e + 2)

                @block.tensor
                def _(pe):
                    for e, (t, nt, tk, g) in enumerate(items):
                        pe.wait_ge(squared.sem, q0 + e + 1)
                        for m in range(nt):
                            a = 2048 * (e % 2) + m * tk
                            mm = pe.matmul(psum[:, a:a + tk], const("head_mean"), tmp[:, e % 2, m * tk:m * tk + tk],
                                           start=True, stop=True)
                        mm.then_inc(step.sem, 1)
                    for e, (t, nt) in enumerate(((wq, 4), (wk, 2))):
                        pe.wait_ge(mixed.sem, vb + 3 + e)
                        for m in range(nt):
                            a = 2048 * e + m * S
                            mm = pe.matmul(psum[:, a:a + S], const("rotate"), t[:, m, 0:S], start=True, stop=True)
                        mm.then_inc(gpart.sem, 1)

                @block.vector
                def _(dve):
                    g0v = VECS["na_q"][0]
                    for a in (0, 2):
                        dve.tensor_scalar(gains[:, a:a + 1], vec[:, layer, g0v + a:g0v + a + 1], DH ** -0.5, None,
                                          ALU.mult).then_inc(read.sem, 1)
                        dve.tensor_copy(gains[:, a + 1:a + 2], vec[:, layer, g0v + a + 1:g0v + a + 2]
                                        ).then_inc(read.sem, 1)
                    dve.wait_ge(read.sem, rb + 4)
                    for e, (t, nt, tk, g) in enumerate(items):
                        dve.wait_ge(rooted.sem, r0 + 2 * e + 2)
                        q = t[:, 0:nt, 0:tk]
                        dve.scalar_tensor_tensor(out=q, in0=q, scalar=gains[:, g:g + 1],
                                                 in1=tmp[:, e % 2, 0:nt * tk].rearrange("p (m t) -> p m t", m=nt),
                                                 op0=ALU.mult, op1=ALU.mult).then_inc(mixed.sem, 1)
                    for e, (t, nt) in enumerate(((wq, 4), (wk, 2))):
                        dve.wait_ge(gpart.sem, gb + e + 1)
                        dve.wait_ge(mixed.sem, vb + 4 + 3 * e)
                        rot = tmp[:, 0, 0:nt * S].rearrange("p (m t) -> p m t", m=nt)
                        q = t[:, 0:nt, 0:S]
                        dve.tensor_tensor(rot, psum[:, 2048 * e:2048 * e + nt * S].rearrange(
                            "p (m t) -> p m t", m=nt), const("sin").unsqueeze(1).to_broadcast([P, nt, S]),
                            ALU.mult).then_inc(mixed.sem, 1)
                        dve.tensor_tensor(q, q, const("cos").unsqueeze(1).to_broadcast([P, nt, S]), ALU.mult
                                          ).then_inc(mixed.sem, 1)
                        dve.wait_ge(mixed.sem, vb + 4 + 3 * e + 2)
                        dve.tensor_tensor(q, q, rot, ALU.add).then_inc(mixed.sem, 1)
            step.n += 4
            squared.n += 4
            read.n += 4
            mixed.n += 4 + 6
            gpart.n += 2
            stored.n += 32

        def stack_stage(jobs, bias_of=None):
            lb, b, u0, l0 = loaded.n, step.n, upper.n, lower.n
            bias_loads = 16 * 16 if bias_of else 0
            with nc.Block() as block:
                @block.sync
                def _(sp):
                    if bias_of:
                        layer, na_bias = bias_of
                        for a in range(2):
                            for h in range(HEADS):
                                off = ((layer * HEADS + h) * 15 + 5 - a) * 31 + 15 - (GRID_W - 1)
                                sp.dma_start(na_bias[a * GRID_W:(a + 1) * GRID_W, h * 6 * GRID_W:(h + 1) * 6 * GRID_W
                                                     ].rearrange("p (e c) -> p e c", e=6),
                                    bass.AP(rpb.tensor, off, [[1, GRID_W], [31, 6], [1, GRID_W]])
                                ).then_inc(loaded.sem, 16)
                    n = 0
                    for e, (src, kind, outs, bufs) in enumerate(jobs):
                        if kind == "kk":
                            continue
                        for part, sem, done in ((0, upper, u0), (1, lower, l0)):
                            sp.wait_ge(sem.sem, done + e + 1)
                            for half in ((part,) if kind == "q" else (0, 1)):
                                o = (outs[0] if kind == "q" else outs[part]).rearrange(
                                    "p (t two) n -> p t two n", two=2)
                                for two in range(2):
                                    sp.dma_start(o[DH * half:DH * half + DH, :, two, :].bitcast(F32),
                                                 bufs[part][DH * two:DH * two + DH].bitcast(F32)
                                                 ).then_inc(moved.sem, 16)
                                    n += 16
                    if n:
                        sp.wait_ge(moved.sem, moved.n + n)
                    moved.n += n

                @block.scalar
                def _(act):
                    for src, kind, outs, bufs in jobs:
                        act.activation(outs[0] if kind == "kk" else bufs[0], src, ACT.Copy).then_inc(upper.sem, 1)

                @block.tensor
                def _(pe):
                    if bias_of:
                        pe.wait_ge(loaded.sem, lb + bias_loads)
                        for a in range(0, NA_COLS, 512):
                            mm = pe.matmul(psum[:, a:a + 512], const("flip_rows"), bias_of[1][:, a:a + 512],
                                           start=True, stop=True)
                        mm.then_inc(step.sem, 1)

                @block.vector
                def _(dve):
                    for e, (src, kind, outs, bufs) in enumerate(jobs):
                        hi, lo = outs if kind == "kk" else bufs
                        dve.wait_ge(upper.sem, u0 + e + 1)
                        dve.tensor_tensor(lo, src, hi.bitcast(F32), ALU.subtract).then_inc(lower.sem, 1)
                    if bias_of:
                        dve.memset(bias_of[1][:, NA_COLS:], 0.0)
                        dve.wait_ge(step.sem, b + 1)
                        dve.tensor_tensor(bias_of[1][:, 0:NA_COLS].rearrange("p (n c) -> p n c", c=GRID_W),
                                          psum[:, 0:NA_COLS].rearrange("p (n c) -> p n c", c=GRID_W),
                                          const("na_mask").unsqueeze(1).to_broadcast([P, 48, GRID_W]), ALU.add
                                          ).then_inc(step.sem, 1)
            loaded.n += bias_loads
            step.n += 2 if bias_of else 0
            upper.n += len(jobs)
            lower.n += len(jobs)

        def attend1(layer, tok, nq, nv, wq, wk, wv):
            def before_zeros(t, at, zeros):
                return bass.AP(t.tensor, t.offset + at, [list(t.ap[0]), [zeros - at, 2], [1, 256]])

            def units_of(qs, kk, vals, span, group, bias, sink):
                units = []
                for h in range(HEADS):
                    for qt in range(2):
                        u = dict(q=qs[:, h, qt * P:qt * P + P], keys=[k[:, h // group, span] for k in kk],
                                 n=span.stop - span.start, bias=bias(h, qt),
                                 vals=vals(h), part=DH * (h % 2), qt=qt, pair=h // 2, first=True, last=True)
                        if sink is not None:
                            u["sink"] = sink[:, h:h + 1]
                        units.append(u)
                return units

            def val(h, t):
                return wv[:, t, (h // 4) * DH:(h // 4) * DH + DH]

            def branch(jobs, src, qs, dst, make_units, bias_of=None, bring_back=None):
                with ExitStack() as st:
                    stack_stage(jobs + [(src, "q", (qs[:],), query_parts(st))], bias_of)
                with ExitStack() as st:
                    attention_stage(make_units(), dst, attention_buffers(st, 2 * S), bring_back)

            with ExitStack() as st:
                qs = sb("qs", [P, HEADS, S], F32R, stack=st)
                if layer == 0:
                    branch([], nq[:, :, S:2 * S], qs, lambda pair: nq[:, pair, S:2 * S], lambda: units_of(
                        qs, (x_hi, x_lo), lambda h: [nv[:, 2 + t, h * DH:h * DH + DH] for t in range(2)],
                        slice(S, 2 * S), 1, lambda h, qt: const("zeros"), None))
                na_bias = sb("na_bias", [P, NA_COLS + 256], stack=st)
                branch([], nq[:, :, 0:S], qs, lambda pair: nq[:, pair, 0:S], lambda: units_of(
                    qs, (x_hi, x_lo), lambda h: [nv[:, t, h * DH:h * DH + DH] for t in range(4)],
                    slice(0, 2 * S), 1,
                    lambda h, qt: before_zeros(na_bias[:], (6 * h + 2 - 2 * qt) * GRID_W, NA_COLS), None),
                    bias_of=(layer, na_bias))
            with ExitStack() as st:
                qs = sb("qs", [P, HEADS, S], F32R, stack=st)
                kk = [sb("kk", [P, 2, 2 * S], F32R, stack=st) for _ in range(2)]
                sink = par(layer, "wa_sink")
                jobs = [(wk[:], "kk", (kk[0][:], kk[1][:]), None)]
                if layer == 0:
                    branch(jobs, wq[:, :, S:2 * S], qs, lambda pair: wq[:, pair, S:2 * S], lambda: units_of(
                        qs, kk, lambda h: [val(h, 2), val(h, 3)], slice(S, 2 * S), 4,
                        lambda h, qt: const("zeros"), sink))
                    jobs = []
                branch(jobs, wq[:, :, 0:S], qs, lambda pair: wq[:, pair, 0:S], lambda: units_of(
                    qs, kk, lambda h: [val(h, t) for t in range(4)], slice(0, 2 * S), 4,
                    lambda h, qt: before_zeros(cst[:], CONSTS["band"][0] + 256 * qt, CONSTS["zeros"][0]), sink),
                    bring_back=tok)

        def query_parts(st):
            return [sb("part", [P, 4, S], F32R, stack=st)[:] for _ in range(2)]

        for layer in range(DEPTH):
            block1(layer)

        rel_bias = sb("rel_bias", [P, 2 * HEADS, 256])
        cmp_bias = sb("cmp_bias", [P, HEADS, 2, NC_CMP])
        table = nc.dram_tensor("bias_by_distance", [2 * HEADS, 511], F32).ap()

        def rel_bias_stage():
            b, lb, rb = step.n, loaded.n, read.n
            with ExitStack() as st:
                rel_sb = sb("rel_sb", [32, 2 * HEADS], stack=st)
                bucket = sb("bucket", [32, 511], stack=st)
                tab_sb = sb("tab_sb", [2 * HEADS, 511], stack=st)
                near = sb("near", [P, 2 * HEADS, 256], stack=st)
                ends = sb("ends", [P, HEADS, 353], stack=st)
                with nc.Block() as block:
                    @block.sync
                    def _(sp):
                        sp.dma_start(rel_sb[:], rel).then_inc(loaded.sem, 16)
                        sp.dma_start(bucket[:], consts[0:32, N_RESIDENT:N_CONST]).then_inc(loaded.sem, 16)
                        sp.wait_ge(step.sem, b + 2)
                        sp.dma_start(table, tab_sb[:]).then_inc(loaded.sem, 16)
                        sp.wait_ge(loaded.sem, lb + 48)
                        for h in range(2 * HEADS):
                            sp.dma_start(near[:, h, :], bass.AP(table.tensor, h * 511, [[1, P], [1, 256]])
                                         ).then_inc(loaded.sem, 16)
                        for h in range(HEADS):
                            sp.dma_start(ends[:, h, :], bass.AP(table.tensor, h * 511 + 31, [[1, P], [1, 353]])
                                         ).then_inc(loaded.sem, 16)

                    @block.tensor
                    def _(pe):
                        pe.wait_ge(loaded.sem, lb + 32)
                        pe.matmul(psum[0:2 * HEADS, 0:511], rel_sb[:], bucket[:], start=True, stop=True
                                  ).then_inc(step.sem, 1)
                        pe.wait_ge(loaded.sem, lb + 16 * 27)
                        for half in range(2):
                            if half:
                                pe.wait_ge(read.sem, rb + 1)
                            for k in range(4):
                                h = HEADS * half + 2 * k
                                mm = pe.matmul(psum[:, 512 * k:512 * k + 512], const("flip"), near[:, h:h + 2, :],
                                               start=True, stop=True)
                            mm.then_inc(step.sem, 1)
                        for qt in range(2):
                            at = P * (1 - qt)
                            mm = pe.matmul(psum[:, 2048 + 512 * qt:2048 + 512 * qt + HEADS * NC_CMP], const("flip"),
                                           ends[:, :, at:at + 225:16], start=True, stop=True)
                        mm.then_inc(step.sem, 1)

                    @block.scalar
                    def _(act):
                        act.wait_ge(step.sem, b + 1)
                        act.activation(tab_sb[:], psum[0:2 * HEADS, 0:511], ACT.Copy).then_inc(step.sem, 1)

                    @block.vector
                    def _(dve):
                        for half, mask in enumerate(("causal", "causal_band")):
                            dve.wait_ge(step.sem, b + 3 + half)
                            dve.tensor_tensor(rel_bias[:, HEADS * half:HEADS * (half + 1), :],
                                              psum[:, 0:2048].rearrange("p (h k) -> p h k", h=HEADS),
                                              const(mask).unsqueeze(1).to_broadcast([P, HEADS, 256]), ALU.add
                                              ).then_inc(read.sem, 1)
                        m = const("cmp_mask").rearrange("p (t c) -> p t c", t=2)
                        dve.wait_ge(step.sem, b + 5)
                        for qt in range(2):
                            dve.tensor_tensor(cmp_bias[:, :, qt, :], psum[:, 2048 + 512 * qt:2048 + 512 * qt +
                                                                          HEADS * NC_CMP].rearrange(
                                                  "p (h c) -> p h c", h=HEADS),
                                              m[:, qt, :].unsqueeze(1).to_broadcast([P, HEADS, NC_CMP]), ALU.add
                                              ).then_inc(read.sem, 1)
            step.n += 5
            loaded.n += 16 * 27
            read.n += 4

        def ffn_stage(layer, which):
            with ExitStack() as st:
                h_hi = sb("h_hi", [P, FT, S], F32R, stack=st)
                h_lo = sb("h_lo", [P, FT, S], F32R, stack=st)
                gate = sb("gate", [P, 2, S], stack=st)
                hid = sb("hid", [P, 2, S], stack=st)
                n = FFN_UP_CHUNKS
                rb, hb, lb = read.n, upper.n, lower.n
                with nc.Block() as block:
                    @block.sync
                    def _(sp):
                        load_ahead(sp, n)

                    @block.tensor
                    def _(pe):
                        hi, lo = model_operand(S)
                        each_chunk(pe, n, lambda i, s: pe_columns(pe, i, s, hi, lo, S))

                    @block.scalar
                    def _(act):
                        def chunk(i, s):
                            round_next(act, i, s)
                            act.wait_ge(chunk_done.sem, g0[0] + s + 1 + 2 * i)
                            act.wait_ge(acc_free.sem, g0[0] + s - 1 + 2 * i)
                            act.activation(gate[:, s, :], acc(s, S), ACT.Silu).then_inc(read.sem, 1)
                        each_chunk(act, n, chunk)

                    @block.vector
                    def _(dve):
                        def chunk(i, s):
                            rest_next(dve, i, s)
                            dve.wait_ge(read.sem, rb + s + 1 + 2 * i)
                            dve.wait_ge(lower.sem, lb + s - 1 + 2 * i)
                            dve.scalar_tensor_tensor(out=hid[:, s, :], in0=acc(s, S, S), scalar=0.5,
                                                     in1=gate[:, s, :], op0=ALU.mult, op1=ALU.mult
                                                     ).then_inc(acc_free.sem, 1)
                        each_chunk(dve, n, chunk)

                    @block.gpsimd
                    def _(pool):
                        def chunk(i, s):
                            j = 2 * i + s
                            pool.wait_ge(acc_free.sem, g0[0] + s + 1 + 2 * i)
                            pool.tensor_copy(h_hi[:, j, :], hid[:, s, :]).then_inc(upper.sem, 1)
                            pool.wait_ge(upper.sem, hb + s + 1 + 2 * i)
                            pool.tensor_tensor(h_lo[:, j, :], hid[:, s, :], h_hi[:, j, :].bitcast(F32),
                                               ALU.subtract).then_inc(lower.sem, 1)
                        each_chunk(pool, n, chunk)
                read.n += n
                upper.n += n
                lower.n += n
                used(n)
                n = FFN_DOWN_CHUNKS
                with nc.Block() as block:
                    @block.sync
                    def _(sp):
                        load_ahead(sp, n)

                    @block.tensor
                    def _(pe):
                        def chunk(i, s, first, last):
                            c = (g0[0] + s) % 2
                            for k in range(2):
                                pe_half(pe, i, s, k)
                                kt = 4 * i + 2 * s + k
                                for m in range(KT):
                                    b = (k * KT + m) * P
                                    o = psum[:, 512 * m:512 * m + S]
                                    pe.matmul(o, w_hi[:, c, b:b + P], h_hi[:, kt, :], start=first and k == 0,
                                              stop=False)
                                    pe.matmul(o, w_hi[:, c, b:b + P], h_lo[:, kt, :], start=False, stop=False)
                                    mm = pe.matmul(o, w_lo[:, c, b:b + P], h_hi[:, kt, :], start=False,
                                                   stop=last and k == 1)
                            mm.then_inc(chunk_done.sem, 1)
                        chunk(0, 0, True, False)
                        chunk(0, 1, False, False)
                        with pe.Fori(1, n // 2) as i:
                            chunk(i, 0, False, False)
                            chunk(i, 1, False, False)
                        chunk(n // 2, 0, False, True)

                    @block.scalar
                    def _(act):
                        each_chunk(act, n, lambda i, s: round_next(act, i, s))

                    @block.vector
                    def _(dve):
                        each_chunk(dve, n, lambda i, s: rest_next(dve, i, s))
                        dve.wait_ge(chunk_done.sem, g0[0] + n)
                        for m in range(4):
                            xs = x[:, 2 * m:2 * m + 2, 0:S]
                            o = dve.scalar_tensor_tensor(
                                out=xs, in0=xs, scalar=DN_ALPHA,
                                in1=psum[:, 1024 * m:1024 * m + 1024].rearrange("p (m t) -> p m t", m=2)[:, :, 0:S],
                                op0=ALU.mult, op1=ALU.add)
                            if m < 3:
                                o.then_inc(gpart.sem, 1)
                            else:
                                o.then_inc(acc_free.sem, n)
                gpart.n += 3
                used(n)
            norm2_stage(layer, which)

        def norm2_stage(layer, which):
            with ExitStack() as st:
                scratch = sb("scratch", [P, KT, S], stack=st)
                layer_norm_stage(x, KT, S, const("ones_model"), ln_eps_col, par(layer, f"ln{which}_g"),
                                 par(layer, f"ln{which}_b"), ACT.Identity, scratch, rs, split=True)

        def mix_stage(layer):
            with ExitStack() as st:
                kv_cmp = x[:, 0:4, S:]
                oa = x[:, 0:4, S:]
                v_c = x[:, 4:8, S:]
                kkf = (x_hi[:, :, S:], x_lo[:, :, S:])
                ob = sb("ob", [P, 4, S], stack=st)
                oc = sb("oc", [P, 4, S], stack=st)
                eighth = DH ** -0.5
                with ExitStack() as st2:
                    v_b = sb("v_b", [P, 2, 160], stack=st2)
                    gates = sb("gates", [P, 2, 24], stack=st2)
                    with ExitStack() as st3:
                        qs = sb("qs", [P, HEADS, S], F32R, stack=st3)
                        kks = [sb("kks", [P, 2, S], F32R, stack=st3) for _ in range(2)]
                        kkw = [sb("kkw", [P, 2, S], F32R, stack=st3) for _ in range(2)]
                        v_sw = sb("v_sw", [P, 2, 256], stack=st3)
                        kkc = [sb("kkc", [P, 2, NC_CMP + 1], F32R, stack=st3) for _ in range(2)]
                        vc = sb("vc", [NC_CMP, 2, DH], stack=st3)
                        project_stage([("q", qs[:, 0:4, :], eighth), ("q", qs[:, 4:8, :], eighth),
                                       ("c", kv_cmp[:, 0:2, :], 1.0), ("c", kv_cmp[:, 2:4, :], 1.0),
                                       ("kk", (kks[0][:], kks[1][:]), 1.0), ("kk", (kkw[0][:], kkw[1][:]), 1.0),
                                       ("r", v_sw[:], 1.0), ("r", v_b[:], 1.0)])
                        with ExitStack() as st4:
                            compress_stage(layer, kv_cmp, kkc, vc, v_b, gates, st4)
                        with ExitStack() as st4:
                            bufs = attention_buffers(st4, S)
                            attend_nsa(layer, oa, qs, kkc, kks, kkw, v_sw, vc, gates, bufs)
                    qs = [sb("qs", [P, HEADS, S], F32R, stack=st2) for _ in range(2)]
                    kkb = [sb("kkb", [P, 2, S], F32R, stack=st2) for _ in range(2)]
                    project_stage([("q", qs[0][:, 0:4, :], eighth), ("q", qs[0][:, 4:8, :], eighth),
                                   ("kk", (kkb[0][:], kkb[1][:]), 1.0),
                                   ("q", qs[1][:, 0:4, :], eighth), ("q", qs[1][:, 4:8, :], eighth),
                                   ("k", (kkf[0][:, 0:4, :], kkf[1][:, 0:4, :]), 1.0),
                                   ("k", (kkf[0][:, 4:8, :], kkf[1][:, 4:8, :]), 1.0),
                                   ("r", v_c[:, 0:4:2, :], 1.0), ("r", v_c[:, 1:4:2, :], 1.0)])
                    fox_bias = [sb("fox_bias", [P, HEADS, P * (qt + 1)], stack=st2) for qt in range(2)]
                    with ExitStack() as st3:
                        forget_stage(layer, v_b, fox_bias, st3)
                    bufs = attention_buffers(st2, S)
                    attend_others(layer, ob, oc, qs, kkb, kkf, v_b, v_c, fox_bias, bufs)
                with ExitStack() as st2:
                    y = sb("y", [P, KT, S], stack=st2)
                    sg = sb("sg", [P, 4, S], stack=st2)
                    prod = sb("prod", [P, 4, S], stack=st2)
                    op_hi = sb("op_hi", [P, 4, S], F32R, stack=st2)
                    op_lo = sb("op_lo", [P, 4, S], F32R, stack=st2)

                    def take_out(dve, j, i):
                        xs = x[:, 2 * i:2 * i + 2, 0:S]
                        dve.wait_ge(chunk_done.sem, g0[0] + j + 1)
                        dve.scalar_tensor_tensor(out=xs, in0=xs, scalar=DN_ALPHA,
                                                 in1=acc(j % 2, 2 * S).rearrange("p (m t) -> p m t", m=2),
                                                 op0=ALU.mult, op1=ALU.add).then_inc(acc_free.sem, 1)
                    merge_stage((oa, ob, oc), y, sg, prod, op_hi, op_lo, S, False, par(layer, "b_gate"), take_out)
            norm2_stage(layer, 2)

        def project_stage(plan):
            n = len(plan)
            u0, p0 = upper.n, [p.n for p in placed]
            halves = [j for j, (kind, _, _) in enumerate(plan) if kind not in "cr"]
            moves = [j for j in halves if plan[j][0] != "kk"]
            copies = {"q": 4, "k": 8}

            def moved_by(m):
                return p0[m % 2] + 16 * sum(copies[plan[j][0]] for j in moves[m % 2:m + 1:2])

            with ExitStack() as st, nc.Block() as block:
                part = [[sb("part", [P, 2, S], F32R, stack=st) for _ in range(2)] for _ in range(2)]

                @block.sync
                def _(sp):
                    def move(j):
                        if j not in moves:
                            return
                        kind, outs, _ = plan[j]
                        m, e = moves.index(j), halves.index(j)
                        if m >= 2:
                            sp.wait_ge(placed[m % 2].sem, moved_by(m - 2))
                        for p in range(2):
                            if p == 0:
                                sp.wait_ge(upper.sem, u0 + e + 1)
                            else:
                                sp.wait_ge(acc_free.sem, g0[0] + j + 1)
                            for half in ((p,) if kind == "q" else (0, 1)):
                                o = (outs if kind == "q" else outs[p]).rearrange("p (t two) n -> p t two n", two=2)
                                for two in range(2):
                                    sp.dma_start(o[DH * half:DH * half + DH, :, two, :].bitcast(F32),
                                                 part[m % 2][p][DH * two:DH * two + DH].bitcast(F32)
                                                 ).then_inc(placed[m % 2].sem, 16)

                    loads = min(n, CHUNKS + 1 - RING - g0[0])
                    for j in range(n):
                        if j < loads:
                            load_one(sp, j // 2, j % 2)
                        if j:
                            move(j - 1)
                    move(n - 1)
                    for m in range(max(len(moves) - 2, 0), len(moves)):
                        sp.wait_ge(placed[m % 2].sem, moved_by(m))

                @block.tensor
                def _(pe):
                    for j, (kind, o, _) in enumerate(plan):
                        if kind == "r":
                            pe_rows(pe, j // 2, j % 2, S, o.shape[2])
                        else:
                            pe_columns(pe, j // 2, j % 2, *model_operand(S), S)

                @block.scalar
                def _(act):
                    for j, (kind, o, scale) in enumerate(plan):
                        round_next(act, j // 2, j % 2)
                        act.wait_ge(chunk_done.sem, g0[0] + j + 1)
                        act.wait_ge(acc_free.sem, g0[0] + j)
                        a = acc(j % 2, 512).rearrange("p (m t) -> p m t", m=2)
                        if kind in "cr":
                            act.activation(o, a[:, :, 0:o.shape[2]], ACT.Copy, scale=scale).then_inc(acc_free.sem, 1)
                            continue
                        hi = o[0] if kind == "kk" else part[moves.index(j) % 2][0][:]
                        if kind != "kk" and moves.index(j) >= 2:
                            m = moves.index(j)
                            act.wait_ge(placed[m % 2].sem, moved_by(m - 2))
                        act.activation(hi, a, ACT.Copy, scale=scale).then_inc(upper.sem, 1)

                @block.vector
                def _(dve):
                    for j, (kind, o, scale) in enumerate(plan):
                        rest_next(dve, j // 2, j % 2)
                        if kind in "cr":
                            continue
                        a = acc(j % 2, 512).rearrange("p (m t) -> p m t", m=2)
                        hi, lo = o if kind == "kk" else [t[:] for t in part[moves.index(j) % 2]]
                        dve.wait_ge(upper.sem, u0 + halves.index(j) + 1)
                        if kind != "kk" and moves.index(j) >= 2:
                            m = moves.index(j)
                            dve.wait_ge(placed[m % 2].sem, moved_by(m - 2))
                        dve.scalar_tensor_tensor(out=lo, in0=a, scalar=scale, in1=hi.bitcast(F32), op0=ALU.mult,
                                                 op1=ALU.subtract).then_inc(acc_free.sem, 1)
            upper.n += len(halves)
            for m in range(max(len(moves) - 2, 0), len(moves)):
                placed[m % 2].n = moved_by(m)
            used(n)

        def compress_stage(layer, kv_cmp, kkc, vc, v_b, gates, st):
            flat = sb("flat", [P, 4, CMP_T // 2, NC_CMP], stack=st)
            both = sb("both", [P, 2, CMP_T // 2, P], F32R, stack=st)
            rows = sb("rows", [DH, 2, 256], stack=st)
            hidden = sb("hidden", [P, 4, 2 * NC_CMP], stack=st)
            W = 2 * NC_CMP
            n = CMP_CHUNKS
            rb, hb, lb, b, gb = read.n, hpart.n, lpart.n, step.n, gpart.n

            def o_of(w):
                return psum[:, 1024 + 512 * w:1024 + 512 * w + 256]

            with nc.Block() as block:
                @block.sync
                def _(sp):
                    load_ahead(sp, n)

                @block.gpsimd
                def _(pool):
                    pool.memset(both[:].bitcast(F32), 0.0).then_inc(gpart.sem, 1)

                @block.vector
                def _(dve):
                    for part in kkc:
                        dve.memset(part[:, :, NC_CMP:].bitcast(F32), 0.0)
                    for w in range(4):
                        pe_ = par(layer, "pe_k" if w < 2 else "pe_v")
                        for a in range(2):
                            r = slice(a * DH, a * DH + DH)
                            for half in range(2):
                                src = kv_cmp[r, w, :].rearrange("p (b t) -> p t b", t=16)
                                src = src[:, a:16:2, half:half + NC_CMP]
                                tp = slice(8 * half, 8 * half + 8)
                                dve.tensor_tensor(flat[r, w, tp, :], src,
                                                  pe_[r, tp].unsqueeze(2).to_broadcast([DH, 8, NC_CMP]), ALU.add
                                                  ).then_inc(read.sem, 1)
                    for w in range(2):
                        for g in range(2):
                            dve.wait_ge(hpart.sem, hb + 2 * w + g + 1)
                            dve.tensor_tensor(both[:, w, :, 32 + g * NC_CMP:32 + (g + 1) * NC_CMP],
                                              flat[:, 2 * w + g, :, :],
                                              both[:, w, :, g * NC_CMP:(g + 1) * NC_CMP].bitcast(F32), ALU.subtract
                                              ).then_inc(lpart.sem, 1)
                    for j in range(n):
                        rest_next(dve, j // 2, j % 2)
                    dve.wait_ge(step.sem, b + 4)
                    dve.tensor_tensor(kkc[1][:, :, 0:NC_CMP], psum[:, 0:W].rearrange("p (g c) -> p g c", g=2),
                                      kkc[0][:, :, 0:NC_CMP].bitcast(F32), ALU.subtract).then_inc(step.sem, 1)
                    dve.tensor_copy(vc[:], psum[0:NC_CMP, 512:512 + 2 * DH].rearrange("p (g d) -> p g d", g=2)
                                    ).then_inc(step.sem, 1)

                @block.scalar
                def _(act):
                    act.activation(gates[:], v_b[:, :, 128:152], ACT.Sigmoid)
                    act.wait_ge(read.sem, rb + 16)
                    act.wait_ge(gpart.sem, gb + 1)
                    for w in range(2):
                        for g in range(2):
                            act.activation(both[:, w, :, g * NC_CMP:(g + 1) * NC_CMP], flat[:, 2 * w + g, :, :],
                                           ACT.Copy).then_inc(hpart.sem, 1)
                    for j in range(n):
                        round_next(act, j // 2, j % 2)
                        if j % 2:
                            act.wait_ge(chunk_done.sem, g0[0] + j + 1)
                            act.activation(rows[:, j // 2, :], o_of(j // 2)[0:DH, :], ACT.Copy
                                           ).then_inc(acc_free.sem, 2)
                    act.wait_ge(step.sem, b + 1)
                    act.activation(hidden[:], psum[:, 2048:2048 + 4 * W].rearrange("p (j c) -> p j c", j=4),
                                   ACT.Gelu_apprx_tanh).then_inc(step.sem, 1)
                    act.wait_ge(step.sem, b + 3)
                    act.activation(kkc[0][:, :, 0:NC_CMP], psum[:, 0:W].rearrange("p (g c) -> p g c", g=2), ACT.Copy
                                   ).then_inc(step.sem, 1)

                @block.tensor
                def _(pe):
                    pe.wait_ge(lpart.sem, lb + 4)
                    for j in range(n):
                        w = j // 2
                        pe_stacked(pe, w, j % 2, o_of(w), lambda k: both[:, w, KT * (j % 2) + k, :], j % 2 == 0,
                                   j % 2 == 1)
                    pe.wait_ge(acc_free.sem, g0[0] + n)
                    for w in range(2):
                        for t in range(2):
                            at = 2048 + (2 * w + t) * W
                            mm = pe.matmul(psum[:, at:at + W], rows[:, w, t * P:t * P + P], const("fold", DH),
                                           start=True, stop=True)
                    mm.then_inc(step.sem, 1)
                    pe.wait_ge(step.sem, b + 2)
                    for t in range(2):
                        mm = pe.matmul(psum[:, 0:W], par(layer, "k_w2")[:, t * P:t * P + P], hidden[:, t, :],
                                       start=t == 0, stop=t == 1)
                    for g in range(2):
                        for t in range(2):
                            mm = pe.matmul(psum[0:NC_CMP, 512 + g * DH:512 + (g + 1) * DH],
                                           hidden[:, 2 + t, g * NC_CMP:(g + 1) * NC_CMP],
                                           par(layer, "v_w2")[:, t * DH:t * DH + DH], start=t == 0, stop=t == 1)
                    mm.then_inc(step.sem, 1)
            gpart.n += 1
            read.n += 16
            hpart.n += 4
            lpart.n += 4
            step.n += 6
            used(n)

        def forget_stage(layer, v_b, fox_bias, st):
            z = sb("z", [P, 2, 3 * 8], stack=st)
            lf = sb("lf", [P, 2, 2 * 8], stack=st)
            c_col = sb("c_col", [P, 2, 8], stack=st)
            b, rb, m0 = step.n, read.n, mixed.n
            upto = const("upto")
            with nc.Block() as block:
                @block.vector
                def _(dve):
                    zz, neg, ab = z[:, :, 0:8], z[:, :, 8:16], z[:, :, 16:24]
                    dve.tensor_tensor(zz, v_b[:, :, 152:160], par(layer, "b_f").unsqueeze(1).to_broadcast([P, 2, 8]),
                                      ALU.add).then_inc(step.sem, 1)
                    dve.wait_ge(step.sem, b + 1)
                    dve.tensor_scalar(neg, zz, 0.0, None, ALU.min).then_inc(step.sem, 1)
                    dve.wait_ge(step.sem, b + 2)
                    dve.scalar_tensor_tensor(out=ab, in0=neg, scalar=2.0, in1=zz, op0=ALU.mult, op1=ALU.subtract
                                             ).then_inc(step.sem, 1)
                    dve.wait_ge(step.sem, b + 5)
                    dve.tensor_tensor(lf[:, :, 0:8], neg, ab, ALU.subtract).then_inc(step.sem, 1)
                    dve.tensor_tensor(lf[:, :, 8:16], ab, neg, ALU.subtract).then_inc(step.sem, 1)
                    dve.wait_ge(step.sem, b + 8)
                    dve.tensor_copy(c_col[:], psum[:, 0:16].rearrange("p (t h) -> p t h", t=2)).then_inc(step.sem, 1)
                    dve.wait_ge(step.sem, b + 9)
                    for h in range(HEADS):
                        dve.wait_ge(read.sem, rb + h + 1)
                        for qt in range(2):
                            nk = P * (qt + 1)
                            dve.scalar_tensor_tensor(
                                out=fox_bias[qt][:, h, 0:nk], in0=psum[:, 512 * (1 + h % 4):512 * (1 + h % 4) + nk],
                                scalar=c_col[:, qt, h:h + 1],
                                in1=const("causal") if qt else const("causal")[:, P:2 * P],
                                op0=ALU.add, op1=ALU.add).then_inc(mixed.sem, 1)

                @block.scalar
                def _(act):
                    ab = z[:, :, 16:24]
                    act.wait_ge(step.sem, b + 3)
                    act.activation(ab, ab, ACT.Exp).then_inc(step.sem, 1)
                    act.wait_ge(step.sem, b + 4)
                    act.activation(ab, ab, ACT.Ln, bias=1.0).then_inc(step.sem, 1)

                @block.tensor
                def _(pe):
                    pe.wait_ge(step.sem, b + 7)
                    for qt in range(2):
                        for t in range(qt + 1):
                            mm = pe.matmul(psum[:, 8 * qt:8 * qt + 8], upto[:, t * S + qt * P:t * S + qt * P + P],
                                           lf[:, t, 0:8], start=t == 0, stop=t == qt)
                    mm.then_inc(step.sem, 1)
                    for h in range(HEADS):
                        if h >= 4:
                            pe.wait_ge(mixed.sem, m0 + 2 * (h - 3))
                        for t in range(2):
                            mm = pe.matmul(psum[:, 512 * (1 + h % 4):512 * (1 + h % 4) + S],
                                           lf[:, t, 8 + h:9 + h].to_broadcast([P, P]), upto[:, t * S:t * S + S],
                                           start=t == 0, stop=t == 1)
                        mm.then_inc(read.sem, 1)
            step.n += 9
            read.n += HEADS
            mixed.n += 2 * HEADS

        def causal_bias(tile, qt):
            return tile if qt else tile[:, P:2 * P]

        def attend_nsa(layer, oa, qs, kkc, kks, kkw, v_sw, vc, gates, bufs):
            units = []
            for h in range(HEADS):
                g = h // 4
                for qt in range(2):
                    nk = P * (qt + 1)
                    common = dict(q=qs[:, h, qt * P:qt * P + P], part=DH * (h % 2), qt=qt, pair=h // 2)
                    units.append(dict(common, keys=[k[:, g, :] for k in kkc], n=NC_CMP,
                                      bias=cmp_bias[:, h, qt, :], vals=[vc[:, g, :]], first=True, last=False,
                                      gate=gates[:, qt, 3 * h:3 * h + 1], floor=-BIG / 10))
                    for n, kk in enumerate((kks, kkw)):
                        units.append(dict(common, keys=[k[:, g, :] for k in kk], n=nk,
                                          bias=causal_bias(rel_bias[:, h, :], qt),
                                          vals=[v_sw[:, t, n * P + g * DH:n * P + g * DH + DH] for t in range(qt + 1)],
                                          first=False, last=n == 1, gate=gates[:, qt, 3 * h + n + 1:3 * h + n + 2]))
            attention_stage(units, lambda pair: oa[:, pair, :], bufs)

        def attend_others(layer, ob, oc, qs, kkb, kkf, v_b, v_c, fox_bias, bufs):
            units = []
            for h in range(HEADS):
                g = h // 4
                for qt in range(2):
                    units.append(dict(q=qs[0][:, h, qt * P:qt * P + P], keys=[k[:, g, :] for k in kkb],
                                      n=P * (qt + 1), part=DH * (h % 2), qt=qt, pair=h // 2, first=True,
                                      last=True, bias=causal_bias(rel_bias[:, HEADS + h, :], qt),
                                      vals=[v_b[:, t, g * DH:g * DH + DH] for t in range(qt + 1)],
                                      sink=par(layer, "sinks")[:, h:h + 1]))
            attention_stage(units, lambda pair: ob[:, pair, :], bufs)
            units = []
            for h in range(HEADS):
                for qt in range(2):
                    units.append(dict(q=qs[1][:, h, qt * P:qt * P + P], keys=[k[:, h, :] for k in kkf],
                                      n=P * (qt + 1), part=DH * (h % 2), qt=qt, pair=h // 2, first=True,
                                      last=True, bias=fox_bias[qt][:, h, 0:P * (qt + 1)],
                                      vals=[v_c[:, 2 * t + h // 4, (h % 4) * DH:(h % 4) * DH + DH]
                                           for t in range(qt + 1)]))
            attention_stage(units, lambda pair: oc[:, pair, :], bufs)

        rel_bias_stage()
        split_stage(x[:, :, 0:S], x_hi[:, :, 0:S], x_lo[:, :, 0:S])
        for layer in range(DEPTH):
            ffn_stage(layer, 1)
            mix_stage(layer)
            ffn_stage(layer, 3)
        with nc.Block() as block:
            @block.sync
            def _(sp):
                sp.dma_start(out, x[:, :, 0:S]).then_inc(stored.sem, 16)
                sp.wait_ge(stored.sem, stored.n + 16)



def _cols(w, cols):
    kt = w.shape[0] // P
    return w[:, cols].reshape(kt, P, -1, P).transpose(1, 2, 0, 3).reshape(P, -1)


def _rows(w, cols):
    a = np.zeros((w.shape[0], 256), w.dtype)
    a[:, :len(cols)] = w[:, cols]
    return a.reshape(-1, P, 256).transpose(1, 0, 2).reshape(P, -1)


def _r(a, n):
    return np.arange(a, a + n)


def _twice(a):
    return np.concatenate([_r(a, DH), _r(a, DH), _r(a + DH, DH), _r(a + DH, DH)])


def weight_stream(v):
    out = np.empty((CHUNKS + 1, P, CB * P), np.float32)
    out[CHUNKS] = 0.0
    n = 0

    def put(a):
        nonlocal n
        out[n] = a
        n += 1

    def span(w, a, m):
        for c in range(a, a + m, 256):
            put(_cols(w, _r(c, 256)))

    def merge(w_gate, at, w_proj):
        for h in range(2):
            span(w_gate, at + 512 * h, 512)
            put(_cols(w_proj, _r(512 * h, 512)))

    for l in range(DEPTH):
        w = v["w_in"][l]
        for c in range(0, 3 * D, 256):
            put(_rows(v["w_ada"][l], _r(c, 256)))
        span(w, A_VAL, 1024)
        span(w, NK, 512)
        put(_cols(w, _twice(WK)))
        for c in (0, 256):
            put(_rows(w, _r(NV + c, 256)))
        put(_rows(w, _r(WV, 128)))
        span(w, NQ, 512)
        span(w, WQ, 512)
        for b, (gate, proj) in enumerate(((A_GATE, "w_proj_a"), (N_GATE, "w_proj_b"), (W_GATE, "w_proj_c"))):
            span(w, gate, 512)
            merge(w, MERGE + D * b, v[proj][l])
        span(v["w_o"][l], 0, D)
    for l in range(DEPTH):
        def ffn(name):
            w1, w2 = v[name + "_w1_2"][l], v[name + "_w2_2"][l]
            for t in range(FT):
                put(_cols(w1, np.concatenate([_r(t * P, P), _r(D_FF + t * P, P)])))
            for c in range(FT // 2):
                put(w2[c * 256:(c + 1) * 256].reshape(2, P, KT, P).transpose(1, 0, 2, 3).reshape(P, -1))
        w = v["w_in_2"][l]
        ffn("ffn1")
        span(w, QA, 512)
        for c in (KCMP, VCMP, KSLC, KWIN):
            put(_cols(w, _twice(c)))
        put(_rows(w, np.concatenate([_r(VSLC, 128), _r(VWIN, 128)])))
        put(_rows(w, np.concatenate([_r(VB, 128), _r(GA, 24), _r(FC, 8)])))
        for name in ("cmp_k_w1_2", "cmp_v_w1_2"):
            for t in range(2):
                put(_rows(v[name][l][t * D:(t + 1) * D], _r(0, 256)))
        span(w, QB, 512)
        put(_cols(w, _twice(KB)))
        span(w, QC, 512)
        span(w, KC, 512)
        for c in (0, 256):
            put(_rows(w, _r(VC + c, 256)))
        for b, proj in enumerate(("w_br_a_2", "w_br_b_2", "w_br_c_2")):
            merge(v["w_gate_2"][l], D * b, v[proj][l])
        span(v["w_out_2"][l], 0, D)
        ffn("ffn2")
    assert n == CHUNKS
    return out


def small_parameters(v):
    out = np.zeros((P, DEPTH, N_VEC), np.float32)

    def put(l, name, a):
        s, e = VECS[name]
        out[:, l, s:e] = a

    def by_tile(a):
        return a.reshape(-1, P).T

    def everywhere(a):
        return np.broadcast_to(a, (P, a.shape[0]))

    for l in range(DEPTH):
        put(l, "norm_g", by_tile(v["norm_g"][l]))
        put(l, "b_ada", by_tile(v["b_ada"][l]))
        put(l, "conv_w", v["conv_w"][l].reshape(CONV_K, 4, P).transpose(2, 1, 0).reshape(P, -1))
        for name in ("conv_b", "cln_g", "cln_b"):
            put(l, name, by_tile(v[name][l]))
        for name, src in (("na_q", "na_q_norm"), ("na_k", "na_k_norm"), ("wa_q", "wa_q_norm"), ("wa_k", "wa_k_norm")):
            put(l, name, np.concatenate([v[src][l]] * 2)[:, None])
        put(l, "wa_sink", everywhere(v["wa_sink"][l]))
        for name in ("ln1_g", "ln1_b", "ln2_g", "ln2_b", "ln3_g", "ln3_b", "b_gate"):
            put(l, name, by_tile(v[name + "_2"][l]))
        for name, src in (("pe_k", "cmp_pe_k_2"), ("pe_v", "cmp_pe_v_2")):
            put(l, name, v[src][l].reshape(CMP_T // 2, P).T)
        put(l, "sinks", everywhere(v["swa_sinks_2"][l]))
        put(l, "b_f", everywhere(v["fox_b_f_2"][l]))
        w = v["cmp_k_w2_2"][l].reshape(2, P, DH).transpose(1, 0, 2)
        put(l, "k_w2", np.concatenate([w, w], axis=2).reshape(P, -1))
        put(l, "v_w2", v["cmp_v_w2_2"][l].reshape(2, P, DH).transpose(1, 0, 2).reshape(P, -1))
    return out


def constants():
    out = np.zeros((P, N_CONST), np.float32)

    def put(name, a):
        s, e = CONSTS[name]
        out[:a.shape[0], s:e] = a

    p = np.arange(P)
    put("ident", np.eye(P))
    put("ones_model", np.full((P, P), 1.0 / D))
    put("ones_conv", np.full((P, P), 1.0 / D_CONV))
    put("head_mean", (p[:, None] // DH == p[None] // DH) / float(DH))
    rot = np.zeros((P, P))
    for m in range(P):
        if m % 32 < 16:
            rot[m + 16, m] = -1.0
        else:
            rot[m - 16, m] = 1.0
    put("rotate", rot)
    t = np.arange(S)
    put("upto", np.concatenate([(128 * s + p[:, None] <= t[None]) for s in range(2)], axis=1))
    inv = (np.float32(10000.0) ** (-np.arange(16, dtype=np.float32) / 16)).astype(np.float32)
    pos = np.stack([t // GRID_W, t % GRID_W]).astype(np.float32)
    ang = pos[(p % DH) // 32] * inv[p % 16][:, None]
    put("cos", np.cos(ang.astype(np.float64)))
    put("sin", np.sin(ang.astype(np.float64)))
    k = np.arange(S)
    put("band", np.concatenate([np.where(abs(128 * q + p[:, None] - k[None]) <= 128, 0.0, -BIG) for q in range(2)],
                               axis=1))
    dist = 128 + p[:, None] - k[None]
    put("causal", np.where(dist >= 0, 0.0, -BIG))
    put("causal_band", np.where((dist >= 0) & (dist < 128), 0.0, -BIG))
    ends = 16 * np.arange(NC_CMP) + CMP_T - 1
    put("cmp_mask", np.concatenate([np.where(ends[None] <= 128 * q + p[:, None], 0.0, -BIG) for q in range(2)],
                                   axis=1))
    j, c = p % GRID_W, np.arange(GRID_W)
    start = np.clip(j - 8, 0, GRID_W - 16)
    put("na_mask", np.where((c[None] >= start[:, None]) & (c[None] < start[:, None] + 16), 0.0, -BIG))
    put("flip", np.eye(P)[::-1])
    put("fold", np.concatenate([np.eye(32), np.eye(32)])[:, :2 * NC_CMP])
    put("flip_rows", np.kron(np.eye(2), np.eye(GRID_W)[::-1]))
    n = np.maximum(255 - np.arange(511), 0)
    ratio = np.log(np.maximum(n, 1).astype(np.float32) / np.float32(16)) / np.float32(np.log(8.0))
    large = 16 + (ratio * np.float32(16)).astype(np.int32)
    bucket = np.where(n < 16, n, np.minimum(large, 31))
    put("bucket", (np.arange(32)[:, None] == bucket[None]))
    return out


def kernel(**inputs):
    import concourse.bacc as bacc
    from concourse.bass_utils import run_bass_kernel_spmd

    v = {k: np.asarray(a) for k, a in inputs.items()}

    def tiles(a):
        return np.ascontiguousarray(a.reshape(-1, KT, P).transpose(2, 1, 0))

    arrays = {
        "wstream": weight_stream(v),
        "xT": tiles(v["x"][0]),
        "ctxT": tiles(v["ctx"][0]),
        "cT": tiles(np.stack([v["c"][0], v["c_ctx"]])),
        "consts": constants(),
        "vecs": small_parameters(v),
        "rpb": np.ascontiguousarray(v["na_rpb"]).reshape(-1),
        "rel": np.ascontiguousarray(v["rel_bias_2"]),
    }
    nc = bacc.Bacc("TRN2", target_bir_lowering=False, num_devices=1)
    args = {k: nc.dram_tensor(k, a.shape, F32, kind="ExternalInput").ap() for k, a in arrays.items()}
    out = nc.dram_tensor("out", (P, KT, S), F32, kind="ExternalOutput").ap()
    build(nc, out=out, **args)
    r = run_bass_kernel_spmd(nc, [arrays], core_ids=[0])
    return np.ascontiguousarray(r.results[0]["out"].transpose(2, 1, 0)).reshape(1, S, D)
```

```python
from contextlib import ExitStack

import numpy as np

import concourse.bass as bass
from concourse import mybir

F32 = mybir.dt.float32
F32R = mybir.dt.float32r
ALU = mybir.AluOpType
ACT = mybir.ActivationFunctionType
AX = mybir.AxisListType

P = 128
D = 1024
KT = D // P
S = 256
DEPTH = 2
DH = 64
HEADS = 8
GRID_W = 64
CONV_K = 31
PAD = CONV_K // 2
D_CONV = 512
D_FF = 2816
FT = D_FF // P
CB = 16
HALF = CB * P // 2
RING = 4
NC_CMP = 15
CMP_T = 32
BIG = 1e30
DN_ALPHA = (2 * DEPTH) ** 0.25
EPS = 1e-6
LN_EPS = 1e-5

A_VAL, A_GATE_IN, A_GATE, NQ, NK, NV, N_GATE, WQ, WK, WV, W_GATE, MERGE = (
    0, 512, 1024, 1536, 2048, 2560, 3072, 3584, 4096, 4224, 4352, 4864)
QA = 0
KCMP, VCMP, KSLC, VSLC, KWIN, VWIN = (512 + 128 * i for i in range(6))
GA = 1280
QB, KB, VB = 1304, 1816, 1944
QC, KC, VC, FC = 2072, 2584, 3096, 3608

ADA_CHUNKS = 12
GLU_CHUNKS = 4
QKV_CHUNKS = 10
GATE_CHUNKS = 2
MERGE_CHUNKS = 6
OUT_CHUNKS = 4
FFN_UP_CHUNKS = FT
FFN_DOWN_CHUNKS = FT // 2
MIX_CHUNKS = 17
CMP_CHUNKS = 4
CHUNKS1 = ADA_CHUNKS + GLU_CHUNKS + QKV_CHUNKS + 3 * (GATE_CHUNKS + MERGE_CHUNKS) + OUT_CHUNKS
CHUNKS2 = 2 * (FFN_UP_CHUNKS + FFN_DOWN_CHUNKS) + MIX_CHUNKS + CMP_CHUNKS + 3 * MERGE_CHUNKS + OUT_CHUNKS
CHUNKS = DEPTH * (CHUNKS1 + CHUNKS2)

def _columns(sizes):
    at, out = 0, {}
    for name, n in sizes:
        out[name] = (at, at + n)
        at += n
    return out, at


CONSTS, N_CONST = _columns([
    ("ident", 128), ("ones_model", 128), ("ones_conv", 128), ("head_mean", 128),
    ("rotate", 128), ("upto", 2 * 256), ("cos", 256), ("sin", 256), ("band", 2 * 256), ("zeros", 256),
    ("causal", 256), ("causal_band", 256), ("cmp_mask", 2 * NC_CMP), ("na_mask", 64),
    ("flip", 128), ("fold", 2 * NC_CMP), ("flip_rows", 128), ("bucket", 511)])
N_RESIDENT = CONSTS["bucket"][0]
RUN = 5 * 31 + GRID_W
NA_COLS = HEADS * 6 * GRID_W
VECS, N_VEC = _columns([
    ("norm_g", 8), ("b_ada", 24), ("conv_w", 4 * CONV_K), ("conv_b", 4), ("cln_g", 4), ("cln_b", 4),
    ("na_q", 1), ("na_k", 1), ("wa_q", 1), ("wa_k", 1), ("wa_sink", 8),
    ("ln1_g", 8), ("ln1_b", 8), ("ln2_g", 8), ("ln2_b", 8), ("ln3_g", 8), ("ln3_b", 8),
    ("b_gate", 24), ("pe_k", 16), ("pe_v", 16), ("sinks", 8), ("b_f", 8),
    ("k_w2", 2 * 128), ("v_w2", 2 * 64)])


class Count:

    def __init__(self, sem):
        self.sem, self.n = sem, 0


def build(nc, wstream, xT, ctxT, cT, consts, vecs, rpb, rel, out):
    ctx = ExitStack()
    with ctx:
        names = {}

        def sb(name, shape, dt=F32, stack=ctx):
            names[name] = names.get(name, 0) + 1
            if names[name] > 1:
                name = f"{name}_{names[name]}"
            return stack.enter_context(nc.sbuf_tensor(name, shape, dt))

        def count(name):
            return Count(ctx.enter_context(nc.semaphore(name)))

        ring = sb("ring", [P, RING, CB * P])
        w_hi = sb("w_hi", [P, 2, CB * P], F32R)
        w_lo = sb("w_lo", [P, 2, CB * P], F32R)
        x = sb("x", [P, KT, 2 * S])
        x_hi = sb("x_hi", [P, KT, 2 * S], F32R)
        x_lo = sb("x_lo", [P, KT, 2 * S], F32R)
        cst = sb("cst", [P, N_RESIDENT])
        vec = sb("vec", [P, DEPTH, N_VEC])
        psum = ctx.enter_context(nc.psum_tensor("psum", [P, 4096], F32))

        def const(name, rows=P):
            a, b = CONSTS[name]
            return cst[0:rows, a:b]

        def par(layer, name):
            a, b = VECS[name]
            return vec[:, layer, a:b]

        landed = [count("landed_even"), count("landed_odd")]
        hi_done = count("hi_done")
        split_done = count("split_done")
        chunk_done = count("chunk_done")
        acc_free = count("acc_free")
        loaded = count("loaded")
        step = count("step")
        read = count("read")
        mixed = count("mixed")
        gpart = count("gpart")
        hpart = count("hpart")
        lpart = count("lpart")
        conv_step = count("conv_step")
        centred = count("centred")
        squared = count("squared")
        rooted = count("rooted")
        scaled_x = count("scaled_x")
        affine = count("affine")
        upper = count("upper")
        lower = count("lower")
        added = count("added")
        parted = count("parted")
        normed = count("normed")
        rotated = count("rotated")
        sined = count("sined")
        cosined = count("cosined")
        finished = count("finished")
        moved = count("moved")
        placed = [count("placed_even"), count("placed_odd")]
        stored = count("stored")
        g0 = [0]

        def load_ahead(sp, n):
            each_chunk(sp, min(n, CHUNKS + 1 - RING - g0[0]), lambda i, s: load_one(sp, i, s))

        def load_one(sp, i, s):
            c = g0[0] + s + RING
            sp.wait_ge(split_done.sem, 2 * (c - RING + 1) + 4 * i)
            sp.wait_ge(landed[c % 2].sem, 16 * (c // 2 + i))
            sp.dma_start(ring[:, (c + 2 * i) % RING, :], wstream[c + 2 * i]).then_inc(landed[c % 2].sem, 16)

        def round_next(act, i, s):
            c = g0[0] + s + 1
            act.wait_ge(landed[c % 2].sem, 16 * (c // 2 + i + 1))
            if c > 1 or not isinstance(i, int) or i:
                act.wait_ge(chunk_done.sem, c - 1 + 2 * i)
            for half in range(2):
                h = slice(half * HALF, (half + 1) * HALF)
                act.activation(w_hi[:, c % 2, h], ring[:, (c + 2 * i) % RING, h], ACT.Copy
                               ).then_inc(hi_done.sem, 1)

        def rest_next(dve, i, s):
            c = g0[0] + s + 1
            for half in range(2):
                h = slice(half * HALF, (half + 1) * HALF)
                dve.wait_ge(hi_done.sem, 2 * c + 1 + half + 4 * i)
                dve.tensor_tensor(w_lo[:, c % 2, h], ring[:, (c + 2 * i) % RING, h],
                                  w_hi[:, c % 2, h].bitcast(F32), ALU.subtract).then_inc(split_done.sem, 1)

        def each_chunk(eng, n, body):
            pairs = n // 2
            if pairs >= 4:
                lead = 0 if g0[0] else 1
                if lead:
                    body(0, 0)
                    body(0, 1)
                with eng.Fori(lead, pairs) as i:
                    body(i, 0)
                    body(i, 1)
            else:
                for i in range(pairs):
                    body(i, 0)
                    body(i, 1)
            if n % 2:
                body(pairs, 0)

        def columns(t, j, n):
            return t[:, bass.ds(j * n, n)]

        def acc(s, n, at=0):
            a = 2048 * ((g0[0] + s) % 2) + at
            return psum[:, a:a + n]

        def pe_half(pe, i, s, half):
            pe.wait_ge(split_done.sem, 2 * (g0[0] + s) + 1 + half + 4 * i)

        def pe_acc(pe, i, s):
            c = g0[0] + s
            if c > 1 or not isinstance(i, int) or i:
                pe.wait_ge(acc_free.sem, c - 1 + 2 * i)

        def three(pe, o, w_cols, c, hi, lo, first, last):
            pe.matmul(o, w_hi[:, c, w_cols], hi, start=first, stop=False)
            pe.matmul(o, w_hi[:, c, w_cols], lo, start=False, stop=False)
            return pe.matmul(o, w_lo[:, c, w_cols], hi, start=False, stop=last)

        def pe_columns(pe, i, s, hi, lo, tok, kt=KT, before=None):
            pe_acc(pe, i, s)
            c = (g0[0] + s) % 2
            for m in range(CB // kt):
                for k in range(kt):
                    n = m * kt + k
                    if n % (CB // 2) == 0:
                        pe_half(pe, i, s, 2 * n // CB)
                    if before and m == 0:
                        before(k)
                    mm = three(pe, acc(s, tok, m * tok), slice(n * P, n * P + P), c, hi(k), lo(k), k == 0,
                               k == kt - 1)
            mm.then_inc(chunk_done.sem, 1)

        def pe_rows(pe, i, s, tok, cols):
            pe_acc(pe, i, s)
            c = (g0[0] + s) % 2
            for t in range(tok // P):
                for k in range(KT):
                    if t == 0 and k % (KT // 2) == 0:
                        pe_half(pe, i, s, 2 * k // KT)
                    o = acc(s, cols, t * 256)
                    w = slice(k * 256, k * 256 + cols)
                    hi, lo = x_hi[:, k, t * P:t * P + P], x_lo[:, k, t * P:t * P + P]
                    pe.matmul(o, hi, w_hi[:, c, w], start=k == 0, stop=False)
                    pe.matmul(o, lo, w_hi[:, c, w], start=False, stop=False)
                    mm = pe.matmul(o, hi, w_lo[:, c, w], start=False, stop=k == KT - 1)
            mm.then_inc(chunk_done.sem, 1)

        def pe_stacked(pe, i, s, o, both, first, last):
            c = (g0[0] + s) % 2
            for k in range(KT):
                if k % (KT // 2) == 0:
                    pe_half(pe, i, s, 2 * k // KT)
                w = slice(k * 256, k * 256 + 256)
                pe.matmul(o, both(k), w_hi[:, c, w], start=first and k == 0, stop=False)
                mm = pe.matmul(o, both(k), w_lo[:, c, w], start=False, stop=last and k == KT - 1)
            mm.then_inc(chunk_done.sem, 1)

        def model_operand(tok):
            return (lambda k: x_hi[:, k, 0:tok]), (lambda k: x_lo[:, k, 0:tok])

        def used(n):
            g0[0] += n


        def start_stage(c_in):
            with nc.Block() as block:
                @block.sync
                def _(sp):
                    for c in range(RING):
                        if c >= 2:
                            sp.wait_ge(landed[c % 2].sem, 16 * (c // 2))
                        sp.dma_start(ring[:, c, :], wstream[c]).then_inc(landed[c % 2].sem, 16)

                @block.scalar
                def _(act):
                    act.dma_start(c_in[:], cT).then_inc(loaded.sem, 16)
                    act.wait_ge(landed[0].sem, 16)
                    for half in range(2):
                        h = slice(half * HALF, (half + 1) * HALF)
                        act.activation(w_hi[:, 0, h], ring[:, 0, h], ACT.Copy).then_inc(hi_done.sem, 1)
                    act.wait_ge(loaded.sem, 16)
                    act.activation(c_in[:], c_in[:], ACT.Silu).then_inc(step.sem, 1)

                @block.vector
                def _(dve):
                    for half in range(2):
                        h = slice(half * HALF, (half + 1) * HALF)
                        dve.wait_ge(hi_done.sem, 1 + half)
                        dve.tensor_tensor(w_lo[:, 0, h], ring[:, 0, h], w_hi[:, 0, h].bitcast(F32),
                                          ALU.subtract).then_inc(split_done.sem, 1)
            step.n, loaded.n = 1, 16

        def mod_stage(mod, rows, layer):
            b = step.n
            b_ada = par(layer, "b_ada")
            with nc.Block() as block:
                @block.tensor
                def _(pe):
                    pe.wait_ge(loaded.sem, loaded.n)
                    for t in range(3 * KT):
                        mm = pe.transpose(psum[:, 4 * t:4 * t + 4], rows[:, t * P:t * P + P], const("ident")[0:4, 0:4])
                    mm.then_inc(step.sem, 1)

                @block.vector
                def _(dve):
                    v = psum[:, 0:12 * KT].rearrange("p (t c) -> p t c", c=4)
                    dve.wait_ge(loaded.sem, loaded.n)
                    dve.wait_ge(step.sem, b + 1)
                    dve.tensor_tensor(mod[:], v[:, :, 0:2], b_ada.unsqueeze(2).to_broadcast([P, 3 * KT, 2]), ALU.add
                                      ).then_inc(step.sem, 1)
                    dve.wait_ge(step.sem, b + 2)
                    dve.tensor_tensor(mod[:], v[:, :, 2:4], mod[:], ALU.add).then_inc(step.sem, 1)
            step.n += 3

        def ada_stage(c_both, rows, layer):
            n = ADA_CHUNKS
            b = step.n
            with nc.Block() as block:
                @block.vector
                def _(dve):
                    dve.memset(c_both[:].bitcast(F32), 0.0).then_inc(step.sem, 1)
                    dve.wait_ge(step.sem, b + 1)
                    dve.tensor_copy(c_both[:, :, 0:2], c_in[:]).then_inc(step.sem, 1)
                    dve.wait_ge(step.sem, b + 2)
                    dve.tensor_tensor(c_both[:, :, 2:4], c_in[:], c_both[:, :, 0:2].bitcast(F32), ALU.subtract
                                      ).then_inc(step.sem, 1)
            step.n += 3
            with nc.Block() as block:
                @block.sync
                def _(sp):
                    if layer:
                        load_ahead(sp, n)
                        return
                    for j in range(n):
                        load_one(sp, j // 2, j % 2)
                        if j == 6:
                            sp.dma_start(vec[:], vecs).then_inc(loaded.sem, 16)
                        if j == 7:
                            sp.dma_start(cst[:], consts[:, 0:N_RESIDENT]).then_inc(loaded.sem, 16)
                        if j == 8:
                            sp.dma_start(x[:, :, 0:S], xT).then_inc(stored.sem, 16)
                        if j == 9:
                            sp.dma_start(x[:, :, S:2 * S], ctxT).then_inc(stored.sem, 16)

                @block.tensor
                def _(pe):
                    def chunk(i, s):
                        pe_acc(pe, i, s)
                        pe_stacked(pe, i, s, acc(s, 256), lambda k: c_both[:, k, :], True, True)
                    each_chunk(pe, n, chunk)

                @block.scalar
                def _(act):
                    def chunk(i, s):
                        round_next(act, i, s)
                        act.wait_ge(chunk_done.sem, g0[0] + s + 1 + 2 * i)
                        act.activation(columns(rows, 2 * i + s, 256), acc(s, 256)[0:4, :], ACT.Copy
                                       ).then_inc(acc_free.sem, 1)
                    each_chunk(act, n, chunk)

                @block.vector
                def _(dve):
                    each_chunk(dve, n, lambda i, s: rest_next(dve, i, s))
            if layer == 0:
                loaded.n += 32
                stored.n += 32
            used(n)

        def inverse_root(act, mean_square, rs, eps, done):
            act.activation(rs, mean_square, ACT.Ln, bias=eps).then_inc(rooted.sem, 1)
            act.wait_ge(rooted.sem, done + 1)
            act.activation(rs, rs, ACT.Exp, scale=-0.5).then_inc(rooted.sem, 1)

        class Norm:

            def __init__(self, pe, act, dve, before):
                self.pe, self.act, self.dve, self.before = pe, act, dve, before

        def model_norm(mod, scales, layer, scratch, rs):
            b, q0, s0, u0, l0, r0 = step.n, squared.n, scaled_x.n, upper.n, lower.n, rooted.n
            tok = 2 * S
            x_loaded = stored.n
            parts = [(k, w, slice(w * S, w * S + S)) for k in range(KT) for w in range(2)]

            def pe_steps(pe):
                for k in range(KT):
                    pe.wait_ge(squared.sem, q0 + k + 1)
                    mm = pe.matmul(psum[:, 0:tok], const("ones_model"), scratch(k), start=k == 0, stop=k == KT - 1)
                mm.then_inc(step.sem, 1)

            def act_steps(act):
                act.wait_ge(stored.sem, x_loaded)
                for k in range(KT):
                    act.activation(scratch(k), x[:, k, :], ACT.Square).then_inc(squared.sem, 1)
                round_next(act, 0, 0)
                act.wait_ge(step.sem, b + 2)
                inverse_root(act, psum[:, 0:tok], rs[:, 0:tok], eps_col, r0)
                for n, (k, w, t) in enumerate(parts):
                    act.wait_ge(scaled_x.sem, s0 + n + 1)
                    act.activation(x_hi[:, k, t], scratch(k)[:, t], ACT.Identity, bias=mod[:, k, w:w + 1]
                                   ).then_inc(upper.sem, 1)

            def dve_steps(dve):
                dve.scalar_tensor_tensor(out=scales[:], in0=mod[:, KT:2 * KT, :], scalar=1.0,
                                         in1=par(layer, "norm_g").unsqueeze(2).to_broadcast([P, KT, 2]),
                                         op0=ALU.add, op1=ALU.mult).then_inc(step.sem, 1)
                rest_next(dve, 0, 0)
                dve.wait_ge(stored.sem, x_loaded)
                dve.wait_ge(step.sem, b + 2)
                dve.wait_ge(rooted.sem, r0 + 2)
                for n in range(len(parts) + 3):
                    if n < len(parts):
                        k, w, t = parts[n]
                        dve.scalar_tensor_tensor(out=scratch(k)[:, t], in0=x[:, k, t], scalar=scales[:, k, w:w + 1],
                                                 in1=rs[:, t], op0=ALU.mult, op1=ALU.mult).then_inc(scaled_x.sem, 1)
                    if n >= 3:
                        k, w, t = parts[n - 3]
                        dve.wait_ge(upper.sem, u0 + n - 2)
                        dve.scalar_tensor_tensor(out=x_lo[:, k, t], in0=scratch(k)[:, t], scalar=mod[:, k, w:w + 1],
                                                 in1=x_hi[:, k, t].bitcast(F32), op0=ALU.add, op1=ALU.subtract
                                                 ).then_inc(lower.sem, 1)

            step.n += 2
            squared.n += KT
            rooted.n += 2
            for c in (scaled_x, upper, lower):
                c.n += 2 * KT
            return Norm(pe_steps, act_steps, dve_steps, lambda pe, k: pe.wait_ge(lower.sem, l0 + 2 * k + 2))

        def layer_norm(layer, which):
            gains, biases = par(layer, f"ln{which}_g"), par(layer, f"ln{which}_b")
            b, c0, q0, r0, s0, u0, l0 = step.n, centred.n, squared.n, rooted.n, scaled_x.n, upper.n, lower.n
            ones = const("ones_model")

            def src(k):
                return x[:, k, 0:S]

            def pe_steps(pe):
                for k in range(KT):
                    mm = pe.matmul(psum[:, 0:S], ones, src(k), start=k == 0, stop=k == KT - 1)
                mm.then_inc(step.sem, 1)
                for k in range(KT):
                    pe.wait_ge(squared.sem, q0 + k + 1)
                    mm = pe.matmul(psum[:, 512:512 + S], ones, x[:, k, S:], start=k == 0, stop=k == KT - 1)
                mm.then_inc(step.sem, 1)

            def act_steps(act):
                round_next(act, 0, 0)
                for k in range(KT):
                    act.wait_ge(centred.sem, c0 + k + 1)
                    act.activation(x[:, k, S:], src(k), ACT.Square).then_inc(squared.sem, 1)
                act.wait_ge(step.sem, b + 2)
                inverse_root(act, psum[:, 512:512 + S], rs[:, 0:S], ln_eps_col, r0)
                for k in range(KT):
                    act.wait_ge(scaled_x.sem, s0 + k + 1)
                    act.activation(x_hi[:, k, 0:S], src(k), ACT.Identity, bias=biases[:, k:k + 1]
                                   ).then_inc(upper.sem, 1)

            def dve_steps(dve):
                rest_next(dve, 0, 0)
                dve.wait_ge(step.sem, b + 1)
                for k in range(KT):
                    dve.tensor_tensor(src(k), src(k), psum[:, 0:S], ALU.subtract).then_inc(centred.sem, 1)
                dve.wait_ge(rooted.sem, r0 + 2)
                for n in range(KT + 3):
                    if n < KT:
                        dve.scalar_tensor_tensor(out=src(n), in0=src(n), scalar=gains[:, n:n + 1], in1=rs[:, 0:S],
                                                 op0=ALU.mult, op1=ALU.mult).then_inc(scaled_x.sem, 1)
                    k = n - 2
                    if 0 <= k < KT:
                        dve.wait_ge(upper.sem, u0 + k + 1)
                        dve.scalar_tensor_tensor(out=x_lo[:, k, 0:S], in0=src(k), scalar=biases[:, k:k + 1],
                                                 in1=x_hi[:, k, 0:S].bitcast(F32), op0=ALU.add, op1=ALU.subtract
                                                 ).then_inc(lower.sem, 1)
                    k = n - 3
                    if k >= 0:
                        dve.wait_ge(lower.sem, l0 + k + 1)
                        dve.tensor_scalar(src(k), src(k), biases[:, k:k + 1], None, ALU.add).then_inc(affine.sem, 1)

            step.n += 2
            rooted.n += 2
            for c in (centred, squared, scaled_x, affine, upper, lower):
                c.n += KT
            return Norm(pe_steps, act_steps, dve_steps, lambda pe, k: pe.wait_ge(lower.sem, l0 + k + 1))

        def split_stage(src, hi, lo):
            b = step.n
            with nc.Block() as block:
                @block.scalar
                def _(act):
                    act.activation(hi, src, ACT.Copy).then_inc(step.sem, 1)

                @block.vector
                def _(dve):
                    dve.wait_ge(step.sem, b + 1)
                    dve.tensor_tensor(lo, src, hi.bitcast(F32), ALU.subtract).then_inc(step.sem, 1)
            step.n += 2

        def norm_of(src, nt, tok, ones, eps, gains, biases, func, scratch, rs):
            b, c0, q0, r0, s0 = step.n, centred.n, squared.n, rooted.n, scaled_x.n

            def pe_steps(pe):
                for k in range(nt):
                    mm = pe.matmul(psum[:, 0:tok], ones, src[:, k, 0:tok], start=k == 0, stop=k == nt - 1)
                mm.then_inc(step.sem, 1)
                for k in range(nt):
                    pe.wait_ge(squared.sem, q0 + k + 1)
                    mm = pe.matmul(psum[:, 512:512 + tok], ones, scratch[:, k, 0:tok],
                                   start=k == 0, stop=k == nt - 1)
                mm.then_inc(step.sem, 1)

            def dve_steps(dve):
                dve.wait_ge(step.sem, b + 1)
                for k in range(nt):
                    dve.tensor_tensor(src[:, k, 0:tok], src[:, k, 0:tok], psum[:, 0:tok],
                                      ALU.subtract).then_inc(centred.sem, 1)
                dve.wait_ge(rooted.sem, r0 + 2)
                for k in range(nt):
                    dve.tensor_tensor(src[:, k, 0:tok], src[:, k, 0:tok], rs[:, 0:tok], ALU.mult
                                      ).then_inc(scaled_x.sem, 1)

            def act_steps(act):
                for k in range(nt):
                    act.wait_ge(centred.sem, c0 + k + 1)
                    act.activation(scratch[:, k, 0:tok], src[:, k, 0:tok], ACT.Square).then_inc(squared.sem, 1)
                act.wait_ge(step.sem, b + 2)
                inverse_root(act, psum[:, 512:512 + tok], rs[:, 0:tok], eps, r0)
                for k in range(nt):
                    act.wait_ge(scaled_x.sem, s0 + k + 1)
                    act.activation(src[:, k, 0:tok], src[:, k, 0:tok], func, scale=gains[:, k:k + 1],
                                   bias=biases[:, k:k + 1]).then_inc(affine.sem, 1)

            step.n += 2
            rooted.n += 2
            for c in (centred, squared, scaled_x, affine):
                c.n += nt
            return Norm(pe_steps, act_steps, dve_steps, None)

        scored = count("scored")
        sunk = count("sunk")
        biased = count("biased")
        shift = count("shift")
        exped = count("exped")
        small = count("small")
        scaled = count("scaled")
        turned = count("turned")
        turned_sb = count("turned_sb")
        summed = count("summed")
        taken = count("taken")

        def attention_stage(units, dst, T, bring_back=None):
            U = len(units)
            base = {c: c.n for c in (scored, biased, sunk, shift, exped, small, scaled, turned, turned_sb,
                                     summed, taken)}
            nsunk = np.cumsum([1 if "sink" in u else 0 for u in units]).tolist()
            nsmall = np.cumsum([1 + ("floor" in u) for u in units]).tolist()
            pairs = [u["pair"] for u in units]
            ends = [n for n in range(U) if n == U - 1 or pairs[n + 1] != pairs[n]]

            def after(c, counts, u):
                return base[c] + (counts[u] if u >= 0 else 0)

            def s_ps(u, a, n):
                return psum[:, (u % 3) * 512 + a:(u % 3) * 512 + a + n]

            def o_ps(pair):
                return psum[:, 2560 + (pair % 2) * 512:2560 + (pair % 2) * 512 + 2 * P]

            def blocks(u):
                n = u["n"]
                return [(a, min(P, n - a)) for a in range(0, n, P)]

            with nc.Block() as block:
                prob, probT, mx, den, fac, neg = T

                @block.sync
                def _(sp):
                    if bring_back:
                        sp.dma_start(x_hi[:, :, 0:bring_back].bitcast(F32), kept_hi[:, :, 0:bring_back]
                                     ).then_inc(stored.sem, 16)
                        sp.dma_start(x_lo[:, :, 0:bring_back].bitcast(F32), kept_lo[:, :, 0:bring_back]
                                     ).then_inc(stored.sem, 16)
                        sp.wait_ge(stored.sem, stored.n + 32)

                @block.tensor
                def _(pe):
                    for t in range(U + 5):
                        if t < U:
                            u = units[t]
                            if t >= 3:
                                pe.wait_ge(biased.sem, base[biased] + t - 2)
                            o = s_ps(t, 0, u["keys"][0].shape[1])
                            pe.matmul(o, u["q"], u["keys"][0], start=True, stop=False)
                            mm = pe.matmul(o, u["q"], u["keys"][1], start=False, stop=True)
                            mm.then_inc(scored.sem, 1)
                        v = t - 3
                        if 0 <= v < U:
                            pe.wait_ge(scaled.sem, base[scaled] + v + 1)
                            if v >= 2:
                                pe.wait_ge(turned_sb.sem, base[turned_sb] + v - 1)
                            for a, w in blocks(units[v]):
                                mm = pe.transpose(psum[0:w, 1536 + (v % 2) * 512 + a:1536 + (v % 2) * 512 + a + P],
                                                  prob[:, v % 4, a:a + w], const("ident"))
                            mm.then_inc(turned.sem, 1)
                        v = t - 5
                        if 0 <= v < U:
                            u = units[v]
                            pe.wait_ge(turned_sb.sem, base[turned_sb] + v + 1)
                            if u["pair"] >= 2:
                                pe.wait_ge(taken.sem, base[taken] + u["pair"] - 1)
                            part, qt = u["part"], u["qt"]
                            o = o_ps(u["pair"])[part:part + DH, qt * P:qt * P + P]
                            bl = blocks(u)
                            for n, (a, w) in enumerate(bl):
                                mm = pe.matmul(o, u["vals"][n], probT[0:w, v % 2, a:a + P],
                                               start=u["first"] and n == 0, stop=u["last"] and n == len(bl) - 1)
                            mm.then_inc(summed.sem, 1)

                @block.vector
                def _(dve):
                    for t in range(U + 5):
                        v = t - 1
                        if t < U:
                            u = units[t]
                            n = u["n"]
                            if t >= 4:
                                dve.wait_ge(turned.sem, base[turned] + t - 3)
                            if "sink" in u:
                                dve.tensor_copy(prob[:, t % 4, n:n + 1], u["sink"]).then_inc(sunk.sem, 1)
                            o, s_in = prob[:, t % 4, 0:n], s_ps(t, 0, n)
                            if n > 256:
                                o = o.rearrange("p (a k) -> p a k", k=256)
                                s_in = s_in.rearrange("p (a k) -> p a k", k=256)
                            dve.wait_ge(scored.sem, base[scored] + t + 1)
                            dve.tensor_tensor_reduce(o, s_in, u["bias"], 1.0, -3e38, ALU.add, ALU.max,
                                                     mx[:, t % 4, 0:1]).then_inc(biased.sem, 1)
                        if 0 <= v < U:
                            k = after(small, nsmall, v - 1)
                            dve.wait_ge(exped.sem, base[exped] + v + 1)
                            src = den[:, v % 3, 0:1]
                            if "floor" in units[v]:
                                dve.tensor_scalar(den[:, v % 3, 1:2], src, 1e-30, None, ALU.max).then_inc(small.sem, 1)
                                k += 1
                                dve.wait_ge(small.sem, k)
                                src = den[:, v % 3, 1:2]
                            dve.reciprocal(fac[:, v % 3, 0:1], src).then_inc(small.sem, 1)
                        if t < U:
                            dve.wait_ge(biased.sem, base[biased] + t + 1)
                            dve.tensor_scalar(neg[:, t % 4, 0:1], mx[:, t % 4, 0:1],
                                              u["sink"] if "sink" in u else u.get("floor", -3e38), -1.0,
                                              ALU.max, ALU.mult).then_inc(shift.sem, 1)
                        if 0 <= v < U:
                            u = units[v]
                            n = u["n"]
                            dve.wait_ge(small.sem, k + 1)
                            dve.tensor_scalar(prob[:, v % 4, 0:n], prob[:, v % 4, 0:n], fac[:, v % 3, 0:1],
                                              u.get("gate"), ALU.mult, ALU.mult if "gate" in u else ALU.bypass
                                              ).then_inc(scaled.sem, 1)
                        v = t - 5
                        if v in ends:
                            pair = units[v]["pair"]
                            dve.wait_ge(summed.sem, base[summed] + v + 1)
                            dve.tensor_copy(dst(pair), o_ps(pair)[:, 0:dst(pair).shape[1]]).then_inc(taken.sem, 1)

                @block.scalar
                def _(act):
                    for t in range(U + 5):
                        v = t - 4
                        if 0 <= v < U:
                            act.wait_ge(turned.sem, base[turned] + v + 1)
                            if v >= 2:
                                act.wait_ge(summed.sem, base[summed] + v - 1)
                            bl = blocks(units[v])
                            w = bl[-1][1]
                            n = len(bl) * P
                            act.activation(probT[0:w, v % 2, 0:n], psum[0:w, 1536 + (v % 2) * 512:
                                                                        1536 + (v % 2) * 512 + n],
                                           ACT.Copy).then_inc(turned_sb.sem, 1)
                        if t < U:
                            u = units[t]
                            n = u["n"] + ("sink" in u)
                            act.wait_ge(shift.sem, base[shift] + t + 1)
                            if "sink" in u:
                                act.wait_ge(sunk.sem, after(sunk, nsunk, t))
                            if t >= 3:
                                act.wait_ge(small.sem, after(small, nsmall, t - 3))
                            act.activation(prob[:, t % 4, 0:n], prob[:, t % 4, 0:n], ACT.Exp,
                                           bias=neg[:, t % 4, 0:1], accum_out=den[:, t % 3, 0:1]
                                           ).then_inc(exped.sem, 1)

            for c in (scored, biased, shift, exped, scaled, turned, turned_sb, summed):
                c.n += U
            stored.n += 32 if bring_back else 0
            sunk.n += nsunk[-1]
            small.n += nsmall[-1]
            taken.n += len(ends)

        def attention_buffers(st, keys):
            return (sb("prob", [P, 4, keys + 1], stack=st), sb("probT", [P, 2, keys], stack=st),
                    sb("mx", [P, 4, 1], stack=st), sb("den", [P, 3, 2], stack=st), sb("fac", [P, 3, 1], stack=st),
                    sb("neg", [P, 4, 1], stack=st))

        def merge_stage(branches, y, sg, prod, op_hi, op_lo, tok, gated, bias, take_out):
            seq = []
            for b in range(3):
                if gated:
                    seq += [("gate", b, 0), ("gate", b, 1)]
                for h in range(2):
                    seq += [("merge", b, 2 * h), ("merge", b, 2 * h + 1), ("proj", b, h)]
            seq += [("out", 0, i) for i in range(OUT_CHUNKS)]
            n = len(seq)
            u0, l0, m0, a0, w0 = upper.n, lower.n, mixed.n, added.n, gpart.n
            per_branch = 2

            def chunk(kind, b, i):
                return g0[0] + seq.index((kind, b, i))

            def adds(b, h, piece):
                return a0 + 4 * (b - 1) + 2 * h + piece + 1

            with nc.Block() as block:
                @block.sync
                def _(sp):
                    load_ahead(sp, n)

                @block.tensor
                def _(pe):
                    for j, (kind, b, i) in enumerate(seq):
                        if kind == "proj":
                            def parts_made(k):
                                if k % 2 == 0:
                                    pe.wait_ge(lower.sem, l0 + per_branch * b + k // 2 + 1)
                            pe_columns(pe, j // 2, j % 2, lambda k: op_hi[:, k, 0:tok],
                                       lambda k: op_lo[:, k, 0:tok], tok, kt=4, before=parts_made)
                        elif kind == "out":
                            def y_made(k):
                                if k in (0, 4, 6):
                                    pe.wait_ge(lower.sem, l0 + 3 * per_branch + (0, 4, 6).index(k) + 1)
                            pe_columns(pe, j // 2, j % 2, *model_operand(tok), tok, before=None if i else y_made)
                        else:
                            pe_columns(pe, j // 2, j % 2, *model_operand(tok), tok)

                @block.scalar
                def _(act):
                    for j, (kind, b, i) in enumerate(seq):
                        round_next(act, j // 2, j % 2)
                        if (kind, i) == ("merge", 0):
                            if b:
                                act.wait_ge(chunk_done.sem, chunk("proj", b - 1, 1) + 1)
                            for h in range(2):
                                m = slice(2 * h, 2 * h + 2)
                                if gated:
                                    act.wait_ge(mixed.sem, m0 + 2 * b + h + 1)
                                act.activation(op_hi[:, m, 0:tok], branches[b][:, m, 0:tok], ACT.Copy
                                               ).then_inc(upper.sem, 1)
                        if kind in ("gate", "merge"):
                            act.wait_ge(chunk_done.sem, g0[0] + j + 1)
                            if j:
                                act.wait_ge(acc_free.sem, g0[0] + j)
                        if kind == "gate":
                            if b >= 2:
                                act.wait_ge(added.sem, adds(b - 1, 1, 1))
                            act.activation(prod[:, 2 * i:2 * i + 2, 0:tok],
                                           acc(j % 2, 2 * tok).rearrange("p (m t) -> p m t", m=2), ACT.Silu
                                           ).then_inc(acc_free.sem, 1)
                        elif kind == "merge" and bias is None:
                            act.activation(sg[:, 2 * (i % 2):2 * (i % 2) + 2, 0:tok],
                                           acc(j % 2, 2 * tok).rearrange("p (m t) -> p m t", m=2),
                                           ACT.Sigmoid).then_inc(acc_free.sem, 1)
                        elif kind == "merge":
                            for m in range(2):
                                act.activation(sg[:, 2 * (i % 2) + m, 0:tok], acc(j % 2, tok, m * tok),
                                               ACT.Sigmoid, bias=bias[:, 8 * b + 2 * i + m:8 * b + 2 * i + m + 1]
                                               ).then_inc((gpart, acc_free)[m].sem, 1)
                        elif (kind, b, i) == ("proj", 2, 1):
                            act.wait_ge(chunk_done.sem, g0[0] + j)
                            for part, m in enumerate((slice(0, 4), slice(4, 6), slice(6, 8))):
                                act.wait_ge(added.sem, adds(2, 1 if part else 0, max(part - 1, 0) if part else 1))
                                act.activation(x_hi[:, m, 0:tok], y[:, m, 0:tok], ACT.Copy).then_inc(upper.sem, 1)

                @block.vector
                def _(dve):
                    def y_lower(part, m):
                        dve.wait_ge(upper.sem, u0 + 3 * per_branch + part + 1)
                        dve.tensor_tensor(x_lo[:, m, 0:tok], y[:, m, 0:tok], x_hi[:, m, 0:tok].bitcast(F32),
                                          ALU.subtract).then_inc(lower.sem, 1)

                    inner = 0
                    for j, (kind, b, i) in enumerate(seq):
                        rest_next(dve, j // 2, j % 2)
                        if kind == "gate":
                            m = slice(2 * i, 2 * i + 2)
                            dve.wait_ge(acc_free.sem, g0[0] + j + 1)
                            dve.tensor_tensor(branches[b][:, m, 0:tok], branches[b][:, m, 0:tok], prod[:, m, 0:tok],
                                              ALU.mult).then_inc(mixed.sem, 1)
                        if (kind, i) == ("merge", 0):
                            for h in range(2):
                                m = slice(2 * h, 2 * h + 2)
                                dve.wait_ge(upper.sem, u0 + per_branch * b + h + 1)
                                dve.tensor_tensor(op_lo[:, m, 0:tok], branches[b][:, m, 0:tok],
                                                  op_hi[:, m, 0:tok].bitcast(F32), ALU.subtract
                                                  ).then_inc(lower.sem, 1)
                        if kind == "proj":
                            if (b, i) == (2, 1):
                                y_lower(0, slice(0, 4))
                            dve.wait_ge(acc_free.sem, g0[0] + j)
                            dve.wait_ge(chunk_done.sem, g0[0] + j + 1)
                            if gated and b:
                                dve.wait_ge(mixed.sem, m0 + 2 * b + 2)
                            for piece in range(2):
                                m = slice(2 * piece, 2 * piece + 2)
                                a = acc(j % 2, 2 * tok, 2 * tok * piece).rearrange("p (m t) -> p m t", m=2)
                                dest = y[:, 4 * i + 2 * piece:4 * i + 2 * piece + 2, 0:tok]
                                if b and (b, i) != (1, 0):
                                    dve.wait_ge(added.sem, adds(b, i, piece) - 2)
                                dve.tensor_tensor(prod[:, m, 0:tok] if b else dest, a, sg[:, m, 0:tok], ALU.mult
                                                  ).then_inc((parted, acc_free)[piece].sem, 1)
                                inner += 1 - piece
                            for piece in range(2 if b else 0):
                                m = slice(2 * piece, 2 * piece + 2)
                                dest = y[:, 4 * i + 2 * piece:4 * i + 2 * piece + 2, 0:tok]
                                if piece:
                                    dve.wait_ge(acc_free.sem, g0[0] + j + 1)
                                else:
                                    dve.wait_ge(parted.sem, parted.n + inner)
                                dve.tensor_tensor(dest, dest, prod[:, m, 0:tok], ALU.add).then_inc(added.sem, 1)
                            if (b, i) == (2, 1):
                                y_lower(1, slice(4, 6))
                                y_lower(2, slice(6, 8))
                        if kind == "out":
                            take_out(dve, j, i)
            parted.n += 6
            added.n += 8
            mixed.n += 6 if gated else 0
            upper.n += 9
            lower.n += 9
            gpart.n += 0 if bias is None else 12
            used(n)

        kept_hi = nc.dram_tensor("kept_hi", [P, KT, 2 * S], F32).ap()
        kept_lo = nc.dram_tensor("kept_lo", [P, KT, 2 * S], F32).ap()
        consts_small = sb("consts_small", [P, 2])
        eps_col, ln_eps_col = consts_small[:, 0:1], consts_small[:, 1:2]
        c_in = sb("c_in", [P, KT, 2])
        mod = sb("mod", [P, 3 * KT, 2])
        scales = sb("scales", [P, KT, 2])
        rs = sb("rs", [P, 2 * S])
        with nc.Block() as block:
            @block.vector
            def _(dve):
                dve.memset(eps_col, EPS)
                dve.memset(ln_eps_col, LN_EPS)
        start_stage(c_in)

        def block1(layer):
            tok = 2 * S if layer == 0 else S
            sets = tok // S
            with ExitStack() as st:
                rows = sb("rows", [4, 3 * D], stack=st)
                c_both = sb("c_both", [P, KT, P], F32R, stack=st)
                ada_stage(c_both, rows, layer)
                mod_stage(mod, rows, layer)
            with ExitStack() as st:
                conv_out = sb("conv_out", [P, 4, 2 * S], stack=st)
                nq = sb("nq", [P, 4, 2 * S], stack=st)
                wq = sb("wq", [P, 4, 2 * S], stack=st)
                with ExitStack() as st2:
                    nv = sb("nv", [P, 4, 512], stack=st2)
                    wk = sb("wk", [P, 2, 2 * S], stack=st2)
                    wv = sb("wv", [P, 4, 128], stack=st2)
                    with ExitStack() as st4:
                        nk = sb("nk", [P, 4, 2 * S], stack=st4)
                        with ExitStack() as st3:
                            cpad = sb("cpad", [P, 4, 2, S + 2 * PAD], stack=st3)
                            glu_gate = sb("glu_gate", [P, 4, 2 * S], stack=st3)
                            norm = model_norm(mod, scales, layer, lambda k: (nq, wq)[k // 4][:, k % 4, :], rs)
                            glu_stage(cpad, glu_gate, tok, norm)
                            qkv_stage(layer, tok, cpad, conv_out, nq, nk, nv, wq, wk, wv, glu_gate, st3)
                        with ExitStack() as st3:
                            scratch = sb("scratch", [P, 4, 2 * S], stack=st3)
                            parts = [sb("kpart", [P, 4, 2 * S], F32R, stack=st3)[:] for _ in range(2)]
                            norm = norm_of(conv_out, 4, tok, const("ones_conv"), eps_col, par(layer, "cln_g"),
                                           par(layer, "cln_b"), ACT.Silu, scratch, rs)
                            stack_stage([(nk[:], "k", (x_hi[:], x_lo[:]), parts)], norm=norm)
                    attend1(layer, tok, nq, nv, wq, wk, wv)
                with ExitStack() as st2:
                    y = sb("y", [P, KT, 2 * S], stack=st2)
                    sg = sb("sg", [P, 4, 2 * S], stack=st2)
                    prod = sb("prod", [P, 4, 2 * S], stack=st2)
                    op_hi = sb("op_hi", [P, 4, 2 * S], F32R, stack=st2)
                    op_lo = sb("op_lo", [P, 4, 2 * S], F32R, stack=st2)

                    def take_out(dve, j, i):
                        dve.wait_ge(chunk_done.sem, g0[0] + j + 1)
                        for m in range(2):
                            for w in range(sets):
                                xs = x[:, 2 * i + m, w * S:w * S + S]
                                dve.scalar_tensor_tensor(
                                    out=xs, in0=acc(j % 2, S, m * tok + w * S),
                                    scalar=mod[:, 2 * KT + 2 * i + m, w:w + 1], in1=xs, op0=ALU.mult, op1=ALU.add
                                ).then_inc((acc_free if (m, w) == (1, sets - 1) else parted).sem, 1)
                    merge_stage((conv_out, nq, wq), y, sg, prod, op_hi, op_lo, tok, True, None, take_out)
                    parted.n += OUT_CHUNKS * (2 * sets - 1)

        def glu_stage(cpad, glu_gate, tok, norm):
            sets = tok // S
            n = GLU_CHUNKS
            rb = read.n
            with nc.Block() as block:
                @block.sync
                def _(sp):
                    load_ahead(sp, n)

                @block.tensor
                def _(pe):
                    norm.pe(pe)
                    hi, lo = model_operand(tok)
                    for j in range(n):
                        pe_columns(pe, j // 2, j % 2, hi, lo, tok,
                                   before=None if j else lambda k: norm.before(pe, k))

                @block.scalar
                def _(act):
                    norm.act(act)
                    for j in range(n):
                        if j:
                            round_next(act, j // 2, j % 2)
                        act.wait_ge(chunk_done.sem, g0[0] + j + 1)
                        a = acc(j % 2, 2 * tok)
                        if j < 2:
                            for w in range(sets):
                                o = act.activation(
                                    cpad[:, 2 * j:2 * j + 2, w, PAD:PAD + S],
                                    a.rearrange("p (m t) -> p m t", m=2)[:, :, w * S:w * S + S], ACT.Copy)
                                o.then_inc(acc_free.sem if w == sets - 1 else gpart.sem, 1)
                        else:
                            act.activation(glu_gate[:, 2 * j - 4:2 * j - 2, 0:tok],
                                           a.rearrange("p (m t) -> p m t", m=2), ACT.Sigmoid
                                           ).then_inc(acc_free.sem, 1)

                @block.gpsimd
                def _(pool):
                    pool.memset(cpad[:, :, :, 0:PAD], 0.0)
                    pool.memset(cpad[:, :, :, PAD + S:], 0.0)

                @block.vector
                def _(dve):
                    norm.dve(dve)
                    for j in range(n):
                        if j:
                            rest_next(dve, j // 2, j % 2)
                        if j >= 2:
                            m = slice(2 * j - 4, 2 * j - 2)
                            dve.wait_ge(acc_free.sem, g0[0] + j + 1)
                            for w in range(sets):
                                v = cpad[:, m, w, PAD:PAD + S]
                                dve.tensor_tensor(v, v, glu_gate[:, m, w * S:w * S + S], ALU.mult
                                                  ).then_inc(read.sem, 1)
            read.n += 2 * sets
            if sets == 2:
                gpart.n += 2
            used(n)

        def qkv_stage(layer, tok, cpad, conv_out, nq, nk, nv, wq, wk, wv, tmp, st):
            sets = tok // S
            gains = sb("gains", [P, 4], stack=st)
            sines = sb("sines", [P, 2, S], stack=st)
            plan = [(1, 2 * S, nk[:, 0:2, :]), (1, 2 * S, nk[:, 2:4, :]), (3, 2 * S, wk[:, :, :]),
                    (0, tok, nq[:, 0:2, 0:tok]), (0, tok, nq[:, 2:4, 0:tok]),
                    (2, tok, wq[:, 0:2, 0:tok]), (2, tok, wq[:, 2:4, 0:tok]),
                    (None, 2 * S, nv[:, :, 0:256]), (None, 2 * S, nv[:, :, 256:512]), (None, 2 * S, wv[:, :, :])]
            n = QKV_CHUNKS
            normal = 7
            turns = (2, 5, 6)
            taps = [(ct, k) for k in range(CONV_K) for ct in range(4)]
            cuts = [round(len(taps) * j / n) for j in range(n + 1)]
            cb, b, r0, w0, n0, t0, s0, f0, c0, d0 = (c.n for c in (
                conv_step, step, rooted, gpart, normed, rotated, sined, cosined, finished, read))
            w_conv = par(layer, "conv_w")
            b_conv = par(layer, "conv_b")

            def spare(e, k):
                a = 2048 * ((g0[0] + e) % 2) + 1024
                return psum[:, a:a + k]

            def squares_of(e):
                return tmp[:, 2 * (e % 2):2 * (e % 2) + 2, 0:plan[e][1]]

            with nc.Block() as block:
                @block.sync
                def _(sp):
                    sp.dma_start(kept_hi[:, :, 0:tok], x_hi[:, :, 0:tok].bitcast(F32)).then_inc(stored.sem, 16)
                    sp.dma_start(kept_lo[:, :, 0:tok], x_lo[:, :, 0:tok].bitcast(F32)).then_inc(stored.sem, 16)
                    load_ahead(sp, n)
                    sp.wait_ge(stored.sem, stored.n + 32)

                @block.tensor
                def _(pe):
                    def mean_squares(e):
                        t = plan[e][1]
                        pe.wait_ge(acc_free.sem, g0[0] + e + 1)
                        if e >= 2:
                            pe.wait_ge(rooted.sem, r0 + 2 * (e - 2) + 1)
                            if e - 2 in turns:
                                pe.wait_ge(sined.sem, s0 + turns.index(e - 2) + 1)
                        for m in range(2):
                            mm = pe.matmul(spare(e, 1024)[:, m * t:m * t + t], const("head_mean"),
                                           squares_of(e)[:, m, :], start=True, stop=True)
                        mm.then_inc(step.sem, 1)

                    def turn(e):
                        pe.wait_ge(normed.sem, n0 + e + 1)
                        for m in range(2):
                            mm = pe.matmul(spare(e, 512)[:, m * S:m * S + S], const("rotate"),
                                           plan[e][2][:, m, 0:S], start=True, stop=True)
                        mm.then_inc(rotated.sem, 1)

                    for j, (gain, t, o) in enumerate(plan):
                        if gain is None:
                            pe_rows(pe, j // 2, j % 2, t, min(256, o.shape[2]))
                        else:
                            pe_columns(pe, j // 2, j % 2, *model_operand(t), t)
                        if 0 <= j - 1 < normal:
                            mean_squares(j - 1)
                        if j - 2 in turns:
                            turn(j - 2)

                @block.scalar
                def _(act):
                    for j, (gain, t, o) in enumerate(plan):
                        round_next(act, j // 2, j % 2)
                        act.wait_ge(chunk_done.sem, g0[0] + j + 1)
                        if gain is None:
                            a = acc(j % 2, 1024).rearrange("p (t c) -> p t c", t=4)[:, :, 0:o.shape[2]]
                            act.activation(o, a, ACT.Copy).then_inc(acc_free.sem, 1)
                        else:
                            a = acc(j % 2, 2 * t).rearrange("p (m t) -> p m t", m=2)
                            act.wait_ge(read.sem, d0 + 4)
                            act.activation(o, a, ACT.Identity, scale=gains[:, gain:gain + 1]
                                           ).then_inc(gpart.sem, 1)
                            if j >= 2:
                                act.wait_ge(normed.sem, n0 + j - 1)
                            act.activation(squares_of(j), a, ACT.Square).then_inc(acc_free.sem, 1)
                        e = j - 1
                        if 0 <= e < normal:
                            act.wait_ge(step.sem, b + e + 1)
                            t = plan[e][1]
                            inverse_root(act, spare(e, 2 * t).rearrange("p (m t) -> p m t", m=2), squares_of(e),
                                         eps_col, r0 + 2 * e)

                @block.vector
                def _(dve):
                    first = VECS["na_q"][0]
                    for a in (0, 2):
                        dve.tensor_scalar(gains[:, a:a + 1], vec[:, layer, first + a:first + a + 1], DH ** -0.5,
                                          None, ALU.mult).then_inc(read.sem, 1)
                        dve.tensor_copy(gains[:, a + 1:a + 2], vec[:, layer, first + a + 1:first + a + 2]
                                        ).then_inc(read.sem, 1)
                    for j in range(n):
                        rest_next(dve, j // 2, j % 2)
                        if j - 3 in turns:
                            m = turns.index(j - 3)
                            dve.wait_ge(rotated.sem, t0 + m + 1)
                            if m:
                                dve.wait_ge(finished.sem, c0 + m)
                            dve.tensor_tensor(sines[:], spare(j - 3, 2 * S).rearrange("p (m t) -> p m t", m=2),
                                              const("sin").unsqueeze(1).to_broadcast([P, 2, S]), ALU.mult
                                              ).then_inc(sined.sem, 1)
                        for c in range(cuts[j], cuts[j + 1]):
                            ct, k = taps[c]
                            src = cpad[:, ct, 0:sets, k:k + S]
                            o = conv_out[:, ct, 0:tok].rearrange("p (w t) -> p w t", w=sets)
                            wc = w_conv[:, ct * CONV_K + k:ct * CONV_K + k + 1]
                            if k == 0:
                                dve.tensor_scalar(o, src, wc, b_conv[:, ct:ct + 1], ALU.mult, ALU.add
                                                  ).then_inc(conv_step.sem, 1)
                            else:
                                dve.wait_ge(conv_step.sem, cb + c - 3)
                                dve.scalar_tensor_tensor(out=o, in0=src, scalar=wc, in1=o, op0=ALU.mult,
                                                         op1=ALU.add).then_inc(conv_step.sem, 1)

                @block.gpsimd
                def _(pool):
                    def norm(e):
                        pool.wait_ge(gpart.sem, w0 + e + 1)
                        pool.wait_ge(rooted.sem, r0 + 2 * e + 2)
                        o = plan[e][2]
                        pool.tensor_tensor(o, o, squares_of(e), ALU.mult).then_inc(normed.sem, 1)

                    def cosine(e):
                        pool.wait_ge(rotated.sem, t0 + turns.index(e) + 1)
                        q = plan[e][2][:, :, 0:S]
                        pool.tensor_tensor(q, q, const("cos").unsqueeze(1).to_broadcast([P, 2, S]), ALU.mult
                                           ).then_inc(cosined.sem, 1)

                    def finish(e):
                        m = turns.index(e) + 1
                        pool.wait_ge(cosined.sem, f0 + m)
                        pool.wait_ge(sined.sem, s0 + m)
                        q = plan[e][2][:, :, 0:S]
                        pool.tensor_tensor(q, q, sines[:], ALU.add).then_inc(finished.sem, 1)

                    norm(0)
                    norm(1)
                    norm(2)
                    cosine(2)
                    norm(3)
                    finish(2)
                    norm(4)
                    norm(5)
                    cosine(5)
                    norm(6)
                    finish(5)
                    cosine(6)
                    finish(6)
            conv_step.n += len(taps)
            step.n += normal
            rooted.n += 2 * normal
            gpart.n += normal
            normed.n += normal
            for c in (rotated, sined, cosined, finished):
                c.n += len(turns)
            read.n += 4
            stored.n += 32
            used(n)

        def stack_stage(jobs, bias_of=None, norm=None):
            lb, b, u0, l0 = loaded.n, step.n, upper.n, lower.n
            bias_loads = 16 * 2 if bias_of else 0
            with nc.Block() as block:
                @block.sync
                def _(sp):
                    if bias_of:
                        layer, na_bias = bias_of
                        for a in range(2):
                            off = (layer * HEADS * 15 + 5 - a) * 31 + 15 - (GRID_W - 1)
                            sp.dma_start(na_bias[a * GRID_W:(a + 1) * GRID_W, 0:HEADS * RUN].rearrange(
                                "p (h r) -> p h r", h=HEADS),
                                bass.AP(rpb.tensor, off, [[1, GRID_W], [15 * 31, HEADS], [1, RUN]])
                            ).then_inc(loaded.sem, 16)
                    n = 0
                    for e, (src, kind, outs, bufs) in enumerate(jobs):
                        if kind == "kk":
                            continue
                        for part, sem, done in ((0, upper, u0), (1, lower, l0)):
                            sp.wait_ge(sem.sem, done + e + 1)
                            for half in ((part,) if kind == "q" else (0, 1)):
                                o = (outs[0] if kind == "q" else outs[part]).rearrange(
                                    "p (t two) n -> p t two n", two=2)
                                for two in range(2):
                                    sp.dma_start(o[DH * half:DH * half + DH, :, two, :].bitcast(F32),
                                                 bufs[part][DH * two:DH * two + DH].bitcast(F32)
                                                 ).then_inc(moved.sem, 16)
                                    n += 16
                    if n:
                        sp.wait_ge(moved.sem, moved.n + n)
                    moved.n += n

                @block.scalar
                def _(act):
                    for src, kind, outs, bufs in jobs:
                        act.activation(outs[0] if kind == "kk" else bufs[0], src, ACT.Copy).then_inc(upper.sem, 1)
                    if norm:
                        norm.act(act)

                @block.tensor
                def _(pe):
                    if norm:
                        norm.pe(pe)
                    if bias_of:
                        pe.wait_ge(loaded.sem, lb + bias_loads)
                        for h in range(HEADS):
                            t = bias_of[1][:]
                            mm = pe.matmul(psum[:, 512 * h:512 * h + 6 * GRID_W], const("flip_rows"),
                                           bass.AP(t.tensor, t.offset + h * RUN,
                                                   [list(t.ap[0]), [31, 6], [1, GRID_W]]),
                                           start=True, stop=True)
                        mm.then_inc(step.sem, 1)

                @block.vector
                def _(dve):
                    for e, (src, kind, outs, bufs) in enumerate(jobs):
                        hi, lo = outs if kind == "kk" else bufs
                        dve.wait_ge(upper.sem, u0 + e + 1)
                        dve.tensor_tensor(lo, src, hi.bitcast(F32), ALU.subtract).then_inc(lower.sem, 1)
                    if norm:
                        norm.dve(dve)
                    if bias_of:
                        dve.memset(bias_of[1][:, NA_COLS:], 0.0)
                        dve.wait_ge(step.sem, b + 1)
                        for h in range(HEADS):
                            dve.tensor_tensor(
                                bias_of[1][:, 6 * GRID_W * h:6 * GRID_W * (h + 1)].rearrange(
                                    "p (e c) -> p e c", c=GRID_W),
                                psum[:, 512 * h:512 * h + 6 * GRID_W].rearrange("p (e c) -> p e c", c=GRID_W),
                                const("na_mask").unsqueeze(1).to_broadcast([P, 6, GRID_W]), ALU.add
                            ).then_inc(step.sem, 1)
            loaded.n += bias_loads
            step.n += 1 + HEADS if bias_of else 0
            upper.n += len(jobs)
            lower.n += len(jobs)

        def attend1(layer, tok, nq, nv, wq, wk, wv):
            def before_zeros(t, at, zeros):
                return bass.AP(t.tensor, t.offset + at, [list(t.ap[0]), [zeros - at, 2], [1, 256]])

            def units_of(qs, kk, vals, span, group, bias, sink):
                units = []
                for h in range(HEADS):
                    for qt in range(2):
                        u = dict(q=qs[:, h, qt * P:qt * P + P], keys=[k[:, h // group, span] for k in kk],
                                 n=span.stop - span.start, bias=bias(h, qt),
                                 vals=vals(h), part=DH * (h % 2), qt=qt, pair=h // 2, first=True, last=True)
                        if sink is not None:
                            u["sink"] = sink[:, h:h + 1]
                        units.append(u)
                return units

            def val(h, t):
                return wv[:, t, (h // 4) * DH:(h // 4) * DH + DH]

            def branch(jobs, src, qs, dst, make_units, bias_of=None, bring_back=None):
                with ExitStack() as st:
                    stack_stage(jobs + [(src, "q", (qs[:],), query_parts(st))], bias_of)
                with ExitStack() as st:
                    attention_stage(make_units(), dst, attention_buffers(st, 2 * S), bring_back)

            with ExitStack() as st:
                qs = sb("qs", [P, HEADS, S], F32R, stack=st)
                if layer == 0:
                    branch([], nq[:, :, S:2 * S], qs, lambda pair: nq[:, pair, S:2 * S], lambda: units_of(
                        qs, (x_hi, x_lo), lambda h: [nv[:, 2 + t, h * DH:h * DH + DH] for t in range(2)],
                        slice(S, 2 * S), 1, lambda h, qt: const("zeros"), None))
                na_bias = sb("na_bias", [P, NA_COLS + 256], stack=st)
                branch([], nq[:, :, 0:S], qs, lambda pair: nq[:, pair, 0:S], lambda: units_of(
                    qs, (x_hi, x_lo), lambda h: [nv[:, t, h * DH:h * DH + DH] for t in range(4)],
                    slice(0, 2 * S), 1,
                    lambda h, qt: before_zeros(na_bias[:], (6 * h + 2 - 2 * qt) * GRID_W, NA_COLS), None),
                    bias_of=(layer, na_bias))
            with ExitStack() as st:
                qs = sb("qs", [P, HEADS, S], F32R, stack=st)
                kk = [sb("kk", [P, 2, 2 * S], F32R, stack=st) for _ in range(2)]
                sink = par(layer, "wa_sink")
                jobs = [(wk[:], "kk", (kk[0][:], kk[1][:]), None)]
                if layer == 0:
                    branch(jobs, wq[:, :, S:2 * S], qs, lambda pair: wq[:, pair, S:2 * S], lambda: units_of(
                        qs, kk, lambda h: [val(h, 2), val(h, 3)], slice(S, 2 * S), 4,
                        lambda h, qt: const("zeros"), sink))
                    jobs = []
                branch(jobs, wq[:, :, 0:S], qs, lambda pair: wq[:, pair, 0:S], lambda: units_of(
                    qs, kk, lambda h: [val(h, t) for t in range(4)], slice(0, 2 * S), 4,
                    lambda h, qt: before_zeros(cst[:], CONSTS["band"][0] + 256 * qt, CONSTS["zeros"][0]), sink),
                    bring_back=tok)

        def query_parts(st):
            return [sb("part", [P, 4, S], F32R, stack=st)[:] for _ in range(2)]

        for layer in range(DEPTH):
            block1(layer)

        rel_bias = sb("rel_bias", [P, 2 * HEADS, 256])
        cmp_bias = sb("cmp_bias", [P, HEADS, 2, NC_CMP])
        table = nc.dram_tensor("bias_by_distance", [2 * HEADS, 511], F32).ap()

        def rel_bias_stage():
            b, lb, rb = step.n, loaded.n, read.n
            with ExitStack() as st:
                rel_sb = sb("rel_sb", [32, 2 * HEADS], stack=st)
                bucket = sb("bucket", [32, 511], stack=st)
                tab_sb = sb("tab_sb", [2 * HEADS, 511], stack=st)
                near = sb("near", [P, 2 * HEADS, 256], stack=st)
                ends = sb("ends", [P, HEADS, 353], stack=st)
                with nc.Block() as block:
                    @block.sync
                    def _(sp):
                        sp.dma_start(rel_sb[:], rel).then_inc(loaded.sem, 16)
                        sp.dma_start(bucket[:], consts[0:32, N_RESIDENT:N_CONST]).then_inc(loaded.sem, 16)
                        sp.wait_ge(step.sem, b + 2)
                        sp.dma_start(table, tab_sb[:]).then_inc(loaded.sem, 16)
                        sp.wait_ge(loaded.sem, lb + 48)
                        for h in (0, HEADS):
                            sp.dma_start(near[:, h:h + HEADS, :], bass.AP(
                                table.tensor, h * 511, [[1, P], [511, HEADS], [1, 256]])).then_inc(loaded.sem, 16)
                        sp.dma_start(ends[:], bass.AP(table.tensor, 31, [[1, P], [511, HEADS], [1, 353]])
                                     ).then_inc(loaded.sem, 16)

                    @block.tensor
                    def _(pe):
                        pe.wait_ge(loaded.sem, lb + 32)
                        pe.matmul(psum[0:2 * HEADS, 0:511], rel_sb[:], bucket[:], start=True, stop=True
                                  ).then_inc(step.sem, 1)
                        pe.wait_ge(loaded.sem, lb + 16 * 6)
                        for half in range(2):
                            if half:
                                pe.wait_ge(read.sem, rb + 1)
                            for k in range(4):
                                h = HEADS * half + 2 * k
                                mm = pe.matmul(psum[:, 512 * k:512 * k + 512], const("flip"), near[:, h:h + 2, :],
                                               start=True, stop=True)
                            mm.then_inc(step.sem, 1)
                        for qt in range(2):
                            at = P * (1 - qt)
                            mm = pe.matmul(psum[:, 2048 + 512 * qt:2048 + 512 * qt + HEADS * NC_CMP], const("flip"),
                                           ends[:, :, at:at + 225:16], start=True, stop=True)
                        mm.then_inc(step.sem, 1)

                    @block.scalar
                    def _(act):
                        act.wait_ge(step.sem, b + 1)
                        act.activation(tab_sb[:], psum[0:2 * HEADS, 0:511], ACT.Copy).then_inc(step.sem, 1)

                    @block.vector
                    def _(dve):
                        for half, mask in enumerate(("causal", "causal_band")):
                            dve.wait_ge(step.sem, b + 3 + half)
                            dve.tensor_tensor(rel_bias[:, HEADS * half:HEADS * (half + 1), :],
                                              psum[:, 0:2048].rearrange("p (h k) -> p h k", h=HEADS),
                                              const(mask).unsqueeze(1).to_broadcast([P, HEADS, 256]), ALU.add
                                              ).then_inc(read.sem, 1)
                        m = const("cmp_mask").rearrange("p (t c) -> p t c", t=2)
                        dve.wait_ge(step.sem, b + 5)
                        for qt in range(2):
                            dve.tensor_tensor(cmp_bias[:, :, qt, :], psum[:, 2048 + 512 * qt:2048 + 512 * qt +
                                                                          HEADS * NC_CMP].rearrange(
                                                  "p (h c) -> p h c", h=HEADS),
                                              m[:, qt, :].unsqueeze(1).to_broadcast([P, HEADS, NC_CMP]), ALU.add
                                              ).then_inc(read.sem, 1)
            step.n += 5
            loaded.n += 16 * 6
            read.n += 4

        def ffn_stage(layer, norm):
            up, down = FFN_UP_CHUNKS, FFN_DOWN_CHUNKS
            r0, h0, l0, x0, p0 = read.n, upper.n, lower.n, affine.n, parted.n
            with ExitStack() as st:
                h_hi = sb("h_hi", [P, FT, S], F32R, stack=st)
                h_lo = sb("h_lo", [P, FT, S], F32R, stack=st)
                gate = sb("gate", [P, 2, S], stack=st)
                hid = sb("hid", [P, 2, S], stack=st)

                def first(i, s):
                    return isinstance(i, int) and (i, s) == (0, 0)

                def pairs_of(eng, chunk):
                    chunk(0, 0)
                    chunk(0, 1)
                    with eng.Fori(1, up // 2) as i:
                        chunk(i, 0)
                        chunk(i, 1)

                with nc.Block() as block:
                    @block.sync
                    def _(sp):
                        each_chunk(sp, min(up + down, CHUNKS + 1 - RING - g0[0]), lambda i, s: load_one(sp, i, s))

                    @block.tensor
                    def _(pe):
                        if norm:
                            norm.pe(pe)
                        hi, lo = model_operand(S)
                        pairs_of(pe, lambda i, s: pe_columns(
                            pe, i, s, hi, lo, S,
                            before=(lambda k: norm.before(pe, k)) if norm and first(i, s) else None))

                        def chunk(i, s, start, stop):
                            c = (g0[0] + s) % 2
                            if (g0[0] + up - 1) % 2:
                                order = [(m + 5) % KT for m in range(KT)]
                            else:
                                order = [(m + 1) % KT for m in range(KT)]
                            for k in range(2):
                                pe_half(pe, up // 2 + i, s, k)
                                kt = 4 * i + 2 * s + k
                                pe.wait_ge(lower.sem, l0 + 2 * s + k + 1 + 4 * i)
                                for m in order:
                                    if start and k == 0 and m == order[-2]:
                                        pe.wait_ge(acc_free.sem, g0[0] + up)
                                    b = (k * KT + m) * P
                                    o = psum[:, 512 * m:512 * m + S]
                                    pe.matmul(o, w_hi[:, c, b:b + P], h_hi[:, kt, :], start=start and k == 0,
                                              stop=False)
                                    pe.matmul(o, w_hi[:, c, b:b + P], h_lo[:, kt, :], start=False, stop=False)
                                    mm = pe.matmul(o, w_lo[:, c, b:b + P], h_hi[:, kt, :], start=False,
                                                   stop=stop and k == 1)
                            mm.then_inc(chunk_done.sem, 1)
                        pe.wait_ge(acc_free.sem, g0[0] + up - 1)
                        chunk(0, 0, True, False)
                        chunk(0, 1, False, False)
                        with pe.Fori(1, down // 2) as i:
                            chunk(i, 0, False, False)
                            chunk(i, 1, False, False)
                        chunk(down // 2, 0, False, True)

                    @block.scalar
                    def _(act):
                        if norm:
                            norm.act(act)

                        def chunk(i, s):
                            if not (norm and first(i, s)):
                                round_next(act, i, s)
                            act.wait_ge(chunk_done.sem, g0[0] + s + 1 + 2 * i)
                            act.wait_ge(acc_free.sem, g0[0] + s - 1 + 2 * i)
                            act.activation(gate[:, s, :], acc(s, S), ACT.Silu).then_inc(read.sem, 1)
                        pairs_of(act, chunk)
                        with act.Fori(up // 2, (up + down) // 2) as i:
                            round_next(act, i, 0)
                            round_next(act, i, 1)
                        round_next(act, (up + down) // 2, 0)

                    @block.vector
                    def _(dve):
                        if norm:
                            norm.dve(dve)

                        def chunk(i, s):
                            if not (norm and first(i, s)):
                                rest_next(dve, i, s)
                            dve.wait_ge(read.sem, r0 + s + 1 + 2 * i)
                            dve.wait_ge(lower.sem, l0 + s - 1 + 2 * i)
                            dve.scalar_tensor_tensor(out=hid[:, s, :], in0=acc(s, S, S), scalar=0.5,
                                                     in1=gate[:, s, :], op0=ALU.mult, op1=ALU.mult
                                                     ).then_inc(acc_free.sem, 1)
                        pairs_of(dve, chunk)
                        with dve.Fori(up // 2, (up + down) // 2) as i:
                            rest_next(dve, i, 0)
                            rest_next(dve, i, 1)
                        rest_next(dve, (up + down) // 2, 0)
                        dve.wait_ge(chunk_done.sem, g0[0] + up + down)
                        dve.wait_ge(affine.sem, x0)
                        for m in range(4):
                            xs = x[:, 2 * m:2 * m + 2, 0:S]
                            o = dve.scalar_tensor_tensor(
                                out=xs, in0=xs, scalar=DN_ALPHA,
                                in1=psum[:, 1024 * m:1024 * m + 1024].rearrange("p (m t) -> p m t", m=2)[:, :, 0:S],
                                op0=ALU.mult, op1=ALU.add)
                            if m < 3:
                                o.then_inc(parted.sem, 1)
                            else:
                                o.then_inc(acc_free.sem, down)

                    @block.gpsimd
                    def _(pool):
                        def chunk(i, s):
                            j = 2 * i + s
                            pool.wait_ge(acc_free.sem, g0[0] + s + 1 + 2 * i)
                            pool.tensor_copy(h_hi[:, j, :], hid[:, s, :]).then_inc(upper.sem, 1)
                            pool.wait_ge(upper.sem, h0 + s + 1 + 2 * i)
                            pool.tensor_tensor(h_lo[:, j, :], hid[:, s, :], h_hi[:, j, :].bitcast(F32),
                                               ALU.subtract).then_inc(lower.sem, 1)
                        pairs_of(pool, chunk)
            read.n += up
            upper.n += up
            lower.n += up
            parted.n += 3
            used(up + down)

        def mix_stage(layer):
            with ExitStack() as st:
                kv_cmp = x[:, 0:4, S:]
                oa = x[:, 0:4, S:]
                v_c = x[:, 4:8, S:]
                kkf = (x_hi[:, :, S:], x_lo[:, :, S:])
                ob = sb("ob", [P, 4, S], stack=st)
                oc = sb("oc", [P, 4, S], stack=st)
                eighth = DH ** -0.5
                with ExitStack() as st2:
                    v_b = sb("v_b", [P, 2, 160], stack=st2)
                    gates = sb("gates", [P, 2, 24], stack=st2)
                    with ExitStack() as st3:
                        qs = sb("qs", [P, HEADS, S], F32R, stack=st3)
                        kks = [sb("kks", [P, 2, S], F32R, stack=st3) for _ in range(2)]
                        kkw = [sb("kkw", [P, 2, S], F32R, stack=st3) for _ in range(2)]
                        v_sw = sb("v_sw", [P, 2, 256], stack=st3)
                        kkc = [sb("kkc", [P, 2, NC_CMP + 1], F32R, stack=st3) for _ in range(2)]
                        vc = sb("vc", [NC_CMP, 2, DH], stack=st3)
                        project_stage([("q", qs[:, 0:4, :], eighth), ("q", qs[:, 4:8, :], eighth),
                                       ("c", kv_cmp[:, 0:2, :], 1.0), ("c", kv_cmp[:, 2:4, :], 1.0),
                                       ("kk", (kks[0][:], kks[1][:]), 1.0), ("kk", (kkw[0][:], kkw[1][:]), 1.0),
                                       ("r", v_sw[:], 1.0), ("r", v_b[:], 1.0)], layer_norm(layer, 1))
                        with ExitStack() as st4:
                            compress_stage(layer, kv_cmp, kkc, vc, v_b, gates, st4)
                        with ExitStack() as st4:
                            bufs = attention_buffers(st4, S)
                            attend_nsa(layer, oa, qs, kkc, kks, kkw, v_sw, vc, gates, bufs)
                    qs = [sb("qs", [P, HEADS, S], F32R, stack=st2) for _ in range(2)]
                    kkb = [sb("kkb", [P, 2, S], F32R, stack=st2) for _ in range(2)]
                    fox_bias = [sb("fox_bias", [P, HEADS, P * (qt + 1)], stack=st2) for qt in range(2)]
                    project_stage([("q", qs[0][:, 0:4, :], eighth), ("q", qs[0][:, 4:8, :], eighth),
                                   ("kk", (kkb[0][:], kkb[1][:]), 1.0),
                                   ("q", qs[1][:, 0:4, :], eighth), ("q", qs[1][:, 4:8, :], eighth),
                                   ("k", (kkf[0][:, 0:4, :], kkf[1][:, 0:4, :]), 1.0),
                                   ("k", (kkf[0][:, 4:8, :], kkf[1][:, 4:8, :]), 1.0),
                                   ("r", v_c[:, 0:4:2, :], 1.0), ("r", v_c[:, 1:4:2, :], 1.0)],
                                  beside=Forget(layer, v_b, fox_bias, st2))
                    bufs = attention_buffers(st2, S)
                    attend_others(layer, ob, oc, qs, kkb, kkf, v_b, v_c, fox_bias, bufs)
                with ExitStack() as st2:
                    y = sb("y", [P, KT, S], stack=st2)
                    sg = sb("sg", [P, 4, S], stack=st2)
                    prod = sb("prod", [P, 4, S], stack=st2)
                    op_hi = sb("op_hi", [P, 4, S], F32R, stack=st2)
                    op_lo = sb("op_lo", [P, 4, S], F32R, stack=st2)

                    def take_out(dve, j, i):
                        xs = x[:, 2 * i:2 * i + 2, 0:S]
                        dve.wait_ge(chunk_done.sem, g0[0] + j + 1)
                        dve.scalar_tensor_tensor(out=xs, in0=xs, scalar=DN_ALPHA,
                                                 in1=acc(j % 2, 2 * S).rearrange("p (m t) -> p m t", m=2),
                                                 op0=ALU.mult, op1=ALU.add).then_inc(acc_free.sem, 1)
                    merge_stage((oa, ob, oc), y, sg, prod, op_hi, op_lo, S, False, par(layer, "b_gate"), take_out)

        def project_stage(plan, norm=None, beside=None):
            n = len(plan)
            u0, p0 = upper.n, [p.n for p in placed]
            halves = [j for j, (kind, _, _) in enumerate(plan) if kind not in "cr"]
            moves = [j for j in halves if plan[j][0] != "kk"]
            copies = {"q": 4, "k": 8}

            def moved_by(m):
                return p0[m % 2] + 16 * sum(copies[plan[j][0]] for j in moves[m % 2:m + 1:2])

            with ExitStack() as st, nc.Block() as block:
                part = [[sb("part", [P, 2, S], F32R, stack=st) for _ in range(2)] for _ in range(2)]

                @block.sync
                def _(sp):
                    def move(j):
                        if j not in moves:
                            return
                        kind, outs, _ = plan[j]
                        m, e = moves.index(j), halves.index(j)
                        if m >= 2:
                            sp.wait_ge(placed[m % 2].sem, moved_by(m - 2))
                        for p in range(2):
                            if p == 0:
                                sp.wait_ge(upper.sem, u0 + e + 1)
                            else:
                                sp.wait_ge(acc_free.sem, g0[0] + j + 1)
                            for half in ((p,) if kind == "q" else (0, 1)):
                                o = (outs if kind == "q" else outs[p]).rearrange("p (t two) n -> p t two n", two=2)
                                for two in range(2):
                                    sp.dma_start(o[DH * half:DH * half + DH, :, two, :].bitcast(F32),
                                                 part[m % 2][p][DH * two:DH * two + DH].bitcast(F32)
                                                 ).then_inc(placed[m % 2].sem, 16)

                    loads = min(n, CHUNKS + 1 - RING - g0[0])
                    for j in range(n):
                        if j < loads:
                            load_one(sp, j // 2, j % 2)
                        if j:
                            move(j - 1)
                    move(n - 1)
                    for m in range(max(len(moves) - 2, 0), len(moves)):
                        sp.wait_ge(placed[m % 2].sem, moved_by(m))

                @block.tensor
                def _(pe):
                    if norm:
                        norm.pe(pe)
                    for j, (kind, o, _) in enumerate(plan):
                        if beside:
                            beside.pe(pe, j)
                        if kind == "r":
                            pe_rows(pe, j // 2, j % 2, S, o.shape[2])
                        else:
                            pe_columns(pe, j // 2, j % 2, *model_operand(S), S,
                                       before=None if j or not norm else lambda k: norm.before(pe, k))

                @block.scalar
                def _(act):
                    if norm:
                        norm.act(act)
                    for j, (kind, o, scale) in enumerate(plan):
                        if j or not norm:
                            round_next(act, j // 2, j % 2)
                        if beside:
                            beside.act(act, j)
                        act.wait_ge(chunk_done.sem, g0[0] + j + 1)
                        act.wait_ge(acc_free.sem, g0[0] + j)
                        a = acc(j % 2, 512).rearrange("p (m t) -> p m t", m=2)
                        if kind in "cr":
                            act.activation(o, a[:, :, 0:o.shape[2]], ACT.Copy, scale=scale).then_inc(acc_free.sem, 1)
                            continue
                        hi = o[0] if kind == "kk" else part[moves.index(j) % 2][0][:]
                        if kind != "kk" and moves.index(j) >= 2:
                            m = moves.index(j)
                            act.wait_ge(placed[m % 2].sem, moved_by(m - 2))
                        act.activation(hi, a, ACT.Copy, scale=scale).then_inc(upper.sem, 1)

                @block.vector
                def _(dve):
                    if norm:
                        norm.dve(dve)
                    for j, (kind, o, scale) in enumerate(plan):
                        if j or not norm:
                            rest_next(dve, j // 2, j % 2)
                        if beside:
                            beside.dve(dve, j)
                        if kind in "cr":
                            continue
                        a = acc(j % 2, 512).rearrange("p (m t) -> p m t", m=2)
                        hi, lo = o if kind == "kk" else [t[:] for t in part[moves.index(j) % 2]]
                        dve.wait_ge(upper.sem, u0 + halves.index(j) + 1)
                        if kind != "kk" and moves.index(j) >= 2:
                            m = moves.index(j)
                            dve.wait_ge(placed[m % 2].sem, moved_by(m - 2))
                        dve.scalar_tensor_tensor(out=lo, in0=a, scalar=scale, in1=hi.bitcast(F32), op0=ALU.mult,
                                                 op1=ALU.subtract).then_inc(acc_free.sem, 1)
            upper.n += len(halves)
            for m in range(max(len(moves) - 2, 0), len(moves)):
                placed[m % 2].n = moved_by(m)
            used(n)

        def compress_stage(layer, kv_cmp, kkc, vc, v_b, gates, st):
            flat = sb("flat", [P, 4, CMP_T // 2, NC_CMP], stack=st)
            both = sb("both", [P, 2, CMP_T // 2, P], F32R, stack=st)
            rows = sb("rows", [DH, 2, 256], stack=st)
            hidden = sb("hidden", [P, 4, 2 * NC_CMP], stack=st)
            W = 2 * NC_CMP
            n = CMP_CHUNKS
            rb, hb, lb, b, gb = read.n, hpart.n, lpart.n, step.n, gpart.n

            def o_of(w):
                return psum[:, 1024 + 512 * w:1024 + 512 * w + 256]

            with nc.Block() as block:
                @block.sync
                def _(sp):
                    load_ahead(sp, n)

                @block.gpsimd
                def _(pool):
                    pool.memset(both[:].bitcast(F32), 0.0).then_inc(gpart.sem, 1)

                @block.vector
                def _(dve):
                    for part in kkc:
                        dve.memset(part[:, :, NC_CMP:].bitcast(F32), 0.0)
                    for w in range(4):
                        pe_ = par(layer, "pe_k" if w < 2 else "pe_v")
                        for a in range(2):
                            r = slice(a * DH, a * DH + DH)
                            for half in range(2):
                                src = kv_cmp[r, w, :].rearrange("p (b t) -> p t b", t=16)
                                src = src[:, a:16:2, half:half + NC_CMP]
                                tp = slice(8 * half, 8 * half + 8)
                                dve.tensor_tensor(flat[r, w, tp, :], src,
                                                  pe_[r, tp].unsqueeze(2).to_broadcast([DH, 8, NC_CMP]), ALU.add
                                                  ).then_inc(read.sem, 1)
                    for w in range(2):
                        for g in range(2):
                            dve.wait_ge(hpart.sem, hb + 2 * w + g + 1)
                            dve.tensor_tensor(both[:, w, :, 32 + g * NC_CMP:32 + (g + 1) * NC_CMP],
                                              flat[:, 2 * w + g, :, :],
                                              both[:, w, :, g * NC_CMP:(g + 1) * NC_CMP].bitcast(F32), ALU.subtract
                                              ).then_inc(lpart.sem, 1)
                    for j in range(n):
                        rest_next(dve, j // 2, j % 2)
                    dve.wait_ge(step.sem, b + 4)
                    dve.tensor_tensor(kkc[1][:, :, 0:NC_CMP], psum[:, 0:W].rearrange("p (g c) -> p g c", g=2),
                                      kkc[0][:, :, 0:NC_CMP].bitcast(F32), ALU.subtract).then_inc(step.sem, 1)
                    dve.tensor_copy(vc[:], psum[0:NC_CMP, 512:512 + 2 * DH].rearrange("p (g d) -> p g d", g=2)
                                    ).then_inc(step.sem, 1)

                @block.scalar
                def _(act):
                    act.activation(gates[:], v_b[:, :, 128:152], ACT.Sigmoid)
                    act.wait_ge(read.sem, rb + 16)
                    act.wait_ge(gpart.sem, gb + 1)
                    for w in range(2):
                        for g in range(2):
                            act.activation(both[:, w, :, g * NC_CMP:(g + 1) * NC_CMP], flat[:, 2 * w + g, :, :],
                                           ACT.Copy).then_inc(hpart.sem, 1)
                    for j in range(n):
                        round_next(act, j // 2, j % 2)
                        if j % 2:
                            act.wait_ge(chunk_done.sem, g0[0] + j + 1)
                            act.activation(rows[:, j // 2, :], o_of(j // 2)[0:DH, :], ACT.Copy
                                           ).then_inc(acc_free.sem, 2)
                    act.wait_ge(step.sem, b + 1)
                    act.activation(hidden[:], psum[:, 2048:2048 + 4 * W].rearrange("p (j c) -> p j c", j=4),
                                   ACT.Gelu_apprx_tanh).then_inc(step.sem, 1)
                    act.wait_ge(step.sem, b + 3)
                    act.activation(kkc[0][:, :, 0:NC_CMP], psum[:, 0:W].rearrange("p (g c) -> p g c", g=2), ACT.Copy
                                   ).then_inc(step.sem, 1)

                @block.tensor
                def _(pe):
                    pe.wait_ge(lpart.sem, lb + 4)
                    for j in range(n):
                        w = j // 2
                        pe_stacked(pe, w, j % 2, o_of(w), lambda k: both[:, w, KT * (j % 2) + k, :], j % 2 == 0,
                                   j % 2 == 1)
                    pe.wait_ge(acc_free.sem, g0[0] + n)
                    for w in range(2):
                        for t in range(2):
                            at = 2048 + (2 * w + t) * W
                            mm = pe.matmul(psum[:, at:at + W], rows[:, w, t * P:t * P + P], const("fold", DH),
                                           start=True, stop=True)
                    mm.then_inc(step.sem, 1)
                    pe.wait_ge(step.sem, b + 2)
                    for t in range(2):
                        mm = pe.matmul(psum[:, 0:W], par(layer, "k_w2")[:, t * P:t * P + P], hidden[:, t, :],
                                       start=t == 0, stop=t == 1)
                    for g in range(2):
                        for t in range(2):
                            mm = pe.matmul(psum[0:NC_CMP, 512 + g * DH:512 + (g + 1) * DH],
                                           hidden[:, 2 + t, g * NC_CMP:(g + 1) * NC_CMP],
                                           par(layer, "v_w2")[:, t * DH:t * DH + DH], start=t == 0, stop=t == 1)
                    mm.then_inc(step.sem, 1)
            gpart.n += 1
            read.n += 16
            hpart.n += 4
            lpart.n += 4
            step.n += 6
            used(n)

        class Forget:

            def __init__(self, layer, v_b, fox_bias, st):
                self.layer, self.v_b, self.fox_bias = layer, v_b, fox_bias
                self.z = sb("z", [P, 2, 3 * 8], stack=st)
                self.lf = sb("lf", [P, 2, 2 * 8], stack=st)
                self.c_col = sb("c_col", [P, 2, 8], stack=st)
                self.b, self.rb, self.m0 = step.n, read.n, mixed.n
                step.n += 9
                read.n += HEADS
                mixed.n += 2 * HEADS

            def bank(self, h):
                return 512 * (1, 2, 3, 5)[h % 4]

            def dve(self, dve, j):
                b, z, lf = self.b, self.z, self.lf
                zz, neg, ab = z[:, :, 0:8], z[:, :, 8:16], z[:, :, 16:24]
                if j == 0:
                    dve.tensor_tensor(zz, self.v_b[:, :, 152:160], par(self.layer, "b_f").unsqueeze(1).to_broadcast(
                        [P, 2, 8]), ALU.add).then_inc(step.sem, 1)
                    dve.wait_ge(step.sem, b + 1)
                    dve.tensor_scalar(neg, zz, 0.0, None, ALU.min).then_inc(step.sem, 1)
                    dve.wait_ge(step.sem, b + 2)
                    dve.scalar_tensor_tensor(out=ab, in0=neg, scalar=2.0, in1=zz, op0=ALU.mult, op1=ALU.subtract
                                             ).then_inc(step.sem, 1)
                if j == 2:
                    dve.wait_ge(step.sem, b + 5)
                    dve.tensor_tensor(lf[:, :, 0:8], neg, ab, ALU.subtract).then_inc(step.sem, 1)
                    dve.tensor_tensor(lf[:, :, 8:16], ab, neg, ALU.subtract).then_inc(step.sem, 1)
                if j == 4:
                    dve.wait_ge(step.sem, b + 8)
                    dve.tensor_copy(self.c_col[:], psum[:, 3072:3088].rearrange("p (t h) -> p t h", t=2)
                                    ).then_inc(step.sem, 1)
                    dve.wait_ge(step.sem, b + 9)
                if j in (4, 6):
                    for h in range(2 * j - 8, 2 * j - 4):
                        dve.wait_ge(read.sem, self.rb + h + 1)
                        for qt in range(2):
                            nk = P * (qt + 1)
                            dve.scalar_tensor_tensor(
                                out=self.fox_bias[qt][:, h, 0:nk], in0=psum[:, self.bank(h):self.bank(h) + nk],
                                scalar=self.c_col[:, qt, h:h + 1],
                                in1=const("causal") if qt else const("causal")[:, P:2 * P],
                                op0=ALU.add, op1=ALU.add).then_inc(mixed.sem, 1)

            def act(self, act, j):
                ab = self.z[:, :, 16:24]
                if j == 1:
                    act.wait_ge(step.sem, self.b + 3)
                    act.activation(ab, ab, ACT.Exp).then_inc(step.sem, 1)
                    act.wait_ge(step.sem, self.b + 4)
                    act.activation(ab, ab, ACT.Ln, bias=1.0).then_inc(step.sem, 1)

            def pe(self, pe, j):
                upto = const("upto")
                if j == 3:
                    pe.wait_ge(step.sem, self.b + 7)
                    for qt in range(2):
                        for t in range(qt + 1):
                            mm = pe.matmul(psum[:, 3072 + 8 * qt:3080 + 8 * qt],
                                           upto[:, t * S + qt * P:t * S + qt * P + P],
                                           self.lf[:, t, 0:8], start=t == 0, stop=t == qt)
                    mm.then_inc(step.sem, 1)
                if j in (3, 5):
                    for h in range(2 * j - 6, 2 * j - 2):
                        if h >= 4:
                            pe.wait_ge(mixed.sem, self.m0 + 2 * (h - 3))
                        for t in range(2):
                            mm = pe.matmul(psum[:, self.bank(h):self.bank(h) + S],
                                           self.lf[:, t, 8 + h:9 + h].to_broadcast([P, P]),
                                           upto[:, t * S:t * S + S], start=t == 0, stop=t == 1)
                        mm.then_inc(read.sem, 1)

        def causal_bias(tile, qt):
            return tile if qt else tile[:, P:2 * P]

        def attend_nsa(layer, oa, qs, kkc, kks, kkw, v_sw, vc, gates, bufs):
            units = []
            for h in range(HEADS):
                g = h // 4
                for qt in range(2):
                    nk = P * (qt + 1)
                    common = dict(q=qs[:, h, qt * P:qt * P + P], part=DH * (h % 2), qt=qt, pair=h // 2)
                    units.append(dict(common, keys=[k[:, g, :] for k in kkc], n=NC_CMP,
                                      bias=cmp_bias[:, h, qt, :], vals=[vc[:, g, :]], first=True, last=False,
                                      gate=gates[:, qt, 3 * h:3 * h + 1], floor=-BIG / 10))
                    for n, kk in enumerate((kks, kkw)):
                        units.append(dict(common, keys=[k[:, g, :] for k in kk], n=nk,
                                          bias=causal_bias(rel_bias[:, h, :], qt),
                                          vals=[v_sw[:, t, n * P + g * DH:n * P + g * DH + DH] for t in range(qt + 1)],
                                          first=False, last=n == 1, gate=gates[:, qt, 3 * h + n + 1:3 * h + n + 2]))
            attention_stage(units, lambda pair: oa[:, pair, :], bufs)

        def attend_others(layer, ob, oc, qs, kkb, kkf, v_b, v_c, fox_bias, bufs):
            units = []
            for h in range(HEADS):
                g = h // 4
                for qt in range(2):
                    units.append(dict(q=qs[0][:, h, qt * P:qt * P + P], keys=[k[:, g, :] for k in kkb],
                                      n=P * (qt + 1), part=DH * (h % 2), qt=qt, pair=h // 2, first=True,
                                      last=True, bias=causal_bias(rel_bias[:, HEADS + h, :], qt),
                                      vals=[v_b[:, t, g * DH:g * DH + DH] for t in range(qt + 1)],
                                      sink=par(layer, "sinks")[:, h:h + 1]))
            for h in range(HEADS):
                for qt in range(2):
                    units.append(dict(q=qs[1][:, h, qt * P:qt * P + P], keys=[k[:, h, :] for k in kkf],
                                      n=P * (qt + 1), part=DH * (h % 2), qt=qt, pair=4 + h // 2, first=True,
                                      last=True, bias=fox_bias[qt][:, h, 0:P * (qt + 1)],
                                      vals=[v_c[:, 2 * t + h // 4, (h % 4) * DH:(h % 4) * DH + DH]
                                           for t in range(qt + 1)]))
            attention_stage(units, lambda pair: (ob, oc)[pair // 4][:, pair % 4, :], bufs)

        rel_bias_stage()
        split_stage(x[:, :, 0:S], x_hi[:, :, 0:S], x_lo[:, :, 0:S])
        for layer in range(DEPTH):
            ffn_stage(layer, layer_norm(layer - 1, 3) if layer else None)
            mix_stage(layer)
            ffn_stage(layer, layer_norm(layer, 2))
        base = affine.n
        norm = norm_of(x[:, :, 0:S], KT, S, const("ones_model"), ln_eps_col, par(DEPTH - 1, "ln3_g"),
                       par(DEPTH - 1, "ln3_b"), ACT.Identity, x[:, :, S:], rs)
        with nc.Block() as block:
            @block.tensor
            def _(pe):
                norm.pe(pe)

            @block.vector
            def _(dve):
                norm.dve(dve)

            @block.scalar
            def _(act):
                norm.act(act)

            @block.sync
            def _(sp):
                for k in range(0, KT, 2):
                    sp.wait_ge(affine.sem, base + k + 2)
                    sp.dma_start(out[:, k:k + 2, :], x[:, k:k + 2, 0:S]).then_inc(stored.sem, 16)
                sp.wait_ge(stored.sem, stored.n + 16 * (KT // 2))



def _cols(w, cols):
    kt = w.shape[0] // P
    return w[:, cols].reshape(kt, P, -1, P).transpose(1, 2, 0, 3).reshape(P, -1)


def _rows(w, cols):
    a = np.zeros((w.shape[0], 256), w.dtype)
    a[:, :len(cols)] = w[:, cols]
    return a.reshape(-1, P, 256).transpose(1, 0, 2).reshape(P, -1)


def _r(a, n):
    return np.arange(a, a + n)


def _twice(a):
    return np.concatenate([_r(a, DH), _r(a, DH), _r(a + DH, DH), _r(a + DH, DH)])


def weight_stream(v):
    out = np.empty((CHUNKS + 1, P, CB * P), np.float32)
    out[CHUNKS] = 0.0
    n = 0

    def put(a):
        nonlocal n
        out[n] = a
        n += 1

    def span(w, a, m):
        for c in range(a, a + m, 256):
            put(_cols(w, _r(c, 256)))

    def merge(w_gate, at, w_proj):
        for h in range(2):
            span(w_gate, at + 512 * h, 512)
            put(_cols(w_proj, _r(512 * h, 512)))

    for l in range(DEPTH):
        w = v["w_in"][l]
        for c in range(0, 3 * D, 256):
            put(_rows(v["w_ada"][l], _r(c, 256)))
        span(w, A_VAL, 1024)
        span(w, NK, 512)
        put(_cols(w, _twice(WK)))
        span(w, NQ, 512)
        span(w, WQ, 512)
        for c in (0, 256):
            put(_rows(w, _r(NV + c, 256)))
        put(_rows(w, _r(WV, 128)))
        for b, (gate, proj) in enumerate(((A_GATE, "w_proj_a"), (N_GATE, "w_proj_b"), (W_GATE, "w_proj_c"))):
            span(w, gate, 512)
            merge(w, MERGE + D * b, v[proj][l])
        span(v["w_o"][l], 0, D)
    for l in range(DEPTH):
        def ffn(name):
            w1, w2 = v[name + "_w1_2"][l], v[name + "_w2_2"][l]
            for t in range(FT):
                put(_cols(w1, np.concatenate([_r(t * P, P), _r(D_FF + t * P, P)])))
            for c in range(FT // 2):
                put(w2[c * 256:(c + 1) * 256].reshape(2, P, KT, P).transpose(1, 0, 2, 3).reshape(P, -1))
        w = v["w_in_2"][l]
        ffn("ffn1")
        span(w, QA, 512)
        for c in (KCMP, VCMP, KSLC, KWIN):
            put(_cols(w, _twice(c)))
        put(_rows(w, np.concatenate([_r(VSLC, 128), _r(VWIN, 128)])))
        put(_rows(w, np.concatenate([_r(VB, 128), _r(GA, 24), _r(FC, 8)])))
        for name in ("cmp_k_w1_2", "cmp_v_w1_2"):
            for t in range(2):
                put(_rows(v[name][l][t * D:(t + 1) * D], _r(0, 256)))
        span(w, QB, 512)
        put(_cols(w, _twice(KB)))
        span(w, QC, 512)
        span(w, KC, 512)
        for c in (0, 256):
            put(_rows(w, _r(VC + c, 256)))
        for b, proj in enumerate(("w_br_a_2", "w_br_b_2", "w_br_c_2")):
            merge(v["w_gate_2"][l], D * b, v[proj][l])
        span(v["w_out_2"][l], 0, D)
        ffn("ffn2")
    assert n == CHUNKS
    return out


def small_parameters(v):
    out = np.zeros((P, DEPTH, N_VEC), np.float32)

    def put(l, name, a):
        s, e = VECS[name]
        out[:, l, s:e] = a

    def by_tile(a):
        return a.reshape(-1, P).T

    def everywhere(a):
        return np.broadcast_to(a, (P, a.shape[0]))

    for l in range(DEPTH):
        put(l, "norm_g", by_tile(v["norm_g"][l]))
        put(l, "b_ada", by_tile(v["b_ada"][l]))
        put(l, "conv_w", v["conv_w"][l].reshape(CONV_K, 4, P).transpose(2, 1, 0).reshape(P, -1))
        for name in ("conv_b", "cln_g", "cln_b"):
            put(l, name, by_tile(v[name][l]))
        for name, src in (("na_q", "na_q_norm"), ("na_k", "na_k_norm"), ("wa_q", "wa_q_norm"), ("wa_k", "wa_k_norm")):
            put(l, name, np.concatenate([v[src][l]] * 2)[:, None])
        put(l, "wa_sink", everywhere(v["wa_sink"][l]))
        for name in ("ln1_g", "ln1_b", "ln2_g", "ln2_b", "ln3_g", "ln3_b", "b_gate"):
            put(l, name, by_tile(v[name + "_2"][l]))
        for name, src in (("pe_k", "cmp_pe_k_2"), ("pe_v", "cmp_pe_v_2")):
            put(l, name, v[src][l].reshape(CMP_T // 2, P).T)
        put(l, "sinks", everywhere(v["swa_sinks_2"][l]))
        put(l, "b_f", everywhere(v["fox_b_f_2"][l]))
        w = v["cmp_k_w2_2"][l].reshape(2, P, DH).transpose(1, 0, 2)
        put(l, "k_w2", np.concatenate([w, w], axis=2).reshape(P, -1))
        put(l, "v_w2", v["cmp_v_w2_2"][l].reshape(2, P, DH).transpose(1, 0, 2).reshape(P, -1))
    return out


def constants():
    out = np.zeros((P, N_CONST), np.float32)

    def put(name, a):
        s, e = CONSTS[name]
        out[:a.shape[0], s:e] = a

    p = np.arange(P)
    put("ident", np.eye(P))
    put("ones_model", np.full((P, P), 1.0 / D))
    put("ones_conv", np.full((P, P), 1.0 / D_CONV))
    put("head_mean", (p[:, None] // DH == p[None] // DH) / float(DH))
    rot = np.zeros((P, P))
    for m in range(P):
        if m % 32 < 16:
            rot[m + 16, m] = -1.0
        else:
            rot[m - 16, m] = 1.0
    put("rotate", rot)
    t = np.arange(S)
    put("upto", np.concatenate([(128 * s + p[:, None] <= t[None]) for s in range(2)], axis=1))
    inv = (np.float32(10000.0) ** (-np.arange(16, dtype=np.float32) / 16)).astype(np.float32)
    pos = np.stack([t // GRID_W, t % GRID_W]).astype(np.float32)
    ang = pos[(p % DH) // 32] * inv[p % 16][:, None]
    put("cos", np.cos(ang.astype(np.float64)))
    put("sin", np.sin(ang.astype(np.float64)))
    k = np.arange(S)
    put("band", np.concatenate([np.where(abs(128 * q + p[:, None] - k[None]) <= 128, 0.0, -BIG) for q in range(2)],
                               axis=1))
    dist = 128 + p[:, None] - k[None]
    put("causal", np.where(dist >= 0, 0.0, -BIG))
    put("causal_band", np.where((dist >= 0) & (dist < 128), 0.0, -BIG))
    ends = 16 * np.arange(NC_CMP) + CMP_T - 1
    put("cmp_mask", np.concatenate([np.where(ends[None] <= 128 * q + p[:, None], 0.0, -BIG) for q in range(2)],
                                   axis=1))
    j, c = p % GRID_W, np.arange(GRID_W)
    start = np.clip(j - 8, 0, GRID_W - 16)
    put("na_mask", np.where((c[None] >= start[:, None]) & (c[None] < start[:, None] + 16), 0.0, -BIG))
    put("flip", np.eye(P)[::-1])
    put("fold", np.concatenate([np.eye(32), np.eye(32)])[:, :2 * NC_CMP])
    put("flip_rows", np.kron(np.eye(2), np.eye(GRID_W)[::-1]))
    n = np.maximum(255 - np.arange(511), 0)
    ratio = np.log(np.maximum(n, 1).astype(np.float32) / np.float32(16)) / np.float32(np.log(8.0))
    large = 16 + (ratio * np.float32(16)).astype(np.int32)
    bucket = np.where(n < 16, n, np.minimum(large, 31))
    put("bucket", (np.arange(32)[:, None] == bucket[None]))
    return out


def kernel(**inputs):
    import concourse.bacc as bacc
    from concourse.bass_utils import run_bass_kernel_spmd

    v = {k: np.asarray(a) for k, a in inputs.items()}

    def tiles(a):
        return np.ascontiguousarray(a.reshape(-1, KT, P).transpose(2, 1, 0))

    arrays = {
        "wstream": weight_stream(v),
        "xT": tiles(v["x"][0]),
        "ctxT": tiles(v["ctx"][0]),
        "cT": tiles(np.stack([v["c"][0], v["c_ctx"]])),
        "consts": constants(),
        "vecs": small_parameters(v),
        "rpb": np.ascontiguousarray(v["na_rpb"]).reshape(-1),
        "rel": np.ascontiguousarray(v["rel_bias_2"]),
    }
    nc = bacc.Bacc("TRN2", target_bir_lowering=False, num_devices=1)
    args = {k: nc.dram_tensor(k, a.shape, F32, kind="ExternalInput").ap() for k, a in arrays.items()}
    out = nc.dram_tensor("out", (P, KT, S), F32, kind="ExternalOutput").ap()
    build(nc, out=out, **args)
    r = run_bass_kernel_spmd(nc, [arrays], core_ids=[0])
    return np.ascontiguousarray(r.results[0]["out"].transpose(2, 1, 0)).reshape(1, S, D)
```
